# Optimizing a Trainium2 kernel written in Bass

```python
import math
import jax, jax.numpy as jnp
from jax import lax
import numpy as np

D_MODEL = 1024
BATCH = 1
SEQ = 512
DEPTH = 1

SSM_WIDTH = D_MODEL // 2
SSM_GROUP = 16
SSM_GROUPS = SSM_WIDTH // SSM_GROUP
SSM_STATE = 64
DT_MIN = 1e-3
DT_MAX = 1e-1
MLA_HEADS = 8
MLA_NOPE = 64
MLA_ROPE = 32
MLA_V = 64
MLA_Q_LORA = 384
MLA_KV_LORA = 256
ROPE_THETA = 10000.0
Q_BLOCK = 128
N_BRANCHES = 2
IN_SPLITS = [SSM_WIDTH,
             SSM_WIDTH + MLA_Q_LORA,
             SSM_WIDTH + MLA_Q_LORA + MLA_KV_LORA,
             SSM_WIDTH + MLA_Q_LORA + MLA_KV_LORA + MLA_ROPE]
IN_WIDTH = SSM_WIDTH + MLA_Q_LORA + MLA_KV_LORA + MLA_ROPE + N_BRANCHES * D_MODEL
MEM_TOKENS = 256
MEM_HEADS = 4
MEM_HEAD_DIM = D_MODEL // MEM_HEADS
PEER_HEADS = 8
PEER_N_KEYS = 128
PEER_EXPERTS = PEER_N_KEYS * PEER_N_KEYS
PEER_KEY_DIM = 256
PEER_HALF = PEER_KEY_DIM // 2
PEER_TOPK = 16
PEER_TOKEN_BLOCK = 128
NORM_EPS = 1e-6

kernel_name = "hybrid_s5_mla_peer_encoder"

def rms_norm(x, g):
    xf = x.astype(jnp.float32)
    y = xf * lax.rsqrt(jnp.mean(xf * xf, axis=-1, keepdims=True) + NORM_EPS)
    return (y * g.astype(jnp.float32)).astype(x.dtype)

def rope_tables(positions):
    inv_freq = 1.0 / (ROPE_THETA ** (jnp.arange(0, MLA_ROPE, 2, dtype=jnp.float32) / MLA_ROPE))
    ang = positions.astype(jnp.float32)[..., None] * inv_freq
    return jnp.cos(ang), jnp.sin(ang)

def apply_rope(t, cos, sin):
    t1, t2 = jnp.split(t, 2, axis=-1)
    cos = cos.astype(t.dtype)
    sin = sin.astype(t.dtype)
    return jnp.concatenate([t1 * cos - t2 * sin, t2 * cos + t1 * sin], axis=-1)

def _complex_linear_combine(left, right):
    ar1, ai1, br1, bi1 = left
    ar2, ai2, br2, bi2 = right
    ar = ar2 * ar1 - ai2 * ai1
    ai = ar2 * ai1 + ai2 * ar1
    br = ar2 * br1 - ai2 * bi1 + br2
    bi = ar2 * bi1 + ai2 * br1 + bi2
    return (ar, ai, br, bi)

def s5_direction(u, lam_re, lam_im, log_dt, b_re, b_im, c_re, c_im, reverse):
    f32 = jnp.float32
    lam_re = lam_re.astype(f32); lam_im = lam_im.astype(f32)
    dt = jnp.exp(log_dt.astype(f32))[:, None]
    mag = jnp.exp(lam_re * dt)
    ar = mag * jnp.cos(lam_im * dt)
    ai = mag * jnp.sin(lam_im * dt)
    nr = ar - 1.0
    den = lam_re * lam_re + lam_im * lam_im
    fr = (nr * lam_re + ai * lam_im) / den
    fi = (ai * lam_re - nr * lam_im) / den
    b_re = b_re.astype(f32); b_im = b_im.astype(f32)
    bb_re = fr[..., None] * b_re - fi[..., None] * b_im
    bb_im = fr[..., None] * b_im + fi[..., None] * b_re
    bu_re = jnp.einsum('blgc,gpc->blgp', u, bb_re)
    bu_im = jnp.einsum('blgc,gpc->blgp', u, bb_im)
    L = u.shape[1]
    a_re = jnp.broadcast_to(ar[None, None], (1, L) + ar.shape)
    a_im = jnp.broadcast_to(ai[None, None], (1, L) + ai.shape)
    _, _, s_re, s_im = lax.associative_scan(
        _complex_linear_combine, (a_re, a_im, bu_re, bu_im), reverse=reverse, axis=1)
    return (jnp.einsum('blgp,gcp->blgc', s_re, c_re.astype(f32))
            - jnp.einsum('blgp,gcp->blgc', s_im, c_im.astype(f32)))

def mla_attention(q_nope, q_rope, k_nope, k_rope, v):
    Bsz, L, H, _ = q_nope.shape
    nb = L // Q_BLOCK
    scale = (MLA_NOPE + MLA_ROPE) ** -0.5

    def to_blocks(t):
        return jnp.moveaxis(t.reshape((Bsz, nb, Q_BLOCK) + t.shape[2:]), 1, 0)

    def block(qs):
        qn, qr = qs
        s = (jnp.einsum('bqhd,bkhd->bhqk', qn, k_nope, preferred_element_type=jnp.float32)
             + jnp.einsum('bqhr,bkr->bhqk', qr, k_rope, preferred_element_type=jnp.float32)) * scale
        p = jax.nn.softmax(s, axis=-1).astype(v.dtype)
        return jnp.einsum('bhqk,bkhd->bqhd', p, v)

    o = lax.map(block, (to_blocks(q_nope), to_blocks(q_rope)))
    return jnp.moveaxis(o, 0, 1).reshape(Bsz, L, H * MLA_V)

def mixer_block(xn, cos, sin, w_in, b_gate, lam_re, lam_im, log_dt, b_re, b_im, c_re, c_im,
                d_skip, w_ssm_glu, g_q_lora, w_uq, g_kv_lora, w_ukv, w_mla_o, w_out):
    Bsz, L, _ = xn.shape
    proj = xn @ w_in
    u_ssm, c_q, c_kv, k_rope, gate_logits = jnp.split(proj, IN_SPLITS, axis=-1)

    u = u_ssm.reshape(Bsz, L, SSM_GROUPS, SSM_GROUP).astype(jnp.float32)
    y = (s5_direction(u, lam_re[0], lam_im[0], log_dt[0], b_re[0], b_im[0], c_re[0], c_im[0], False)
         + s5_direction(u, lam_re[1], lam_im[1], log_dt[1], b_re[1], b_im[1], c_re[1], c_im[1], True))
    y = y.reshape(Bsz, L, SSM_WIDTH) + d_skip.astype(jnp.float32) * u_ssm.astype(jnp.float32)
    y = jax.nn.gelu(y).astype(xn.dtype)
    glu_val, glu_gate = jnp.split(y @ w_ssm_glu, 2, axis=-1)
    branch_ssm = glu_val * jax.nn.sigmoid(glu_gate)

    c_q = rms_norm(c_q, g_q_lora)
    q = (c_q @ w_uq).reshape(Bsz, L, MLA_HEADS, MLA_NOPE + MLA_ROPE)
    q_nope = q[..., :MLA_NOPE]
    q_rope = apply_rope(q[..., MLA_NOPE:], cos[:, :, None], sin[:, :, None])
    c_kv = rms_norm(c_kv, g_kv_lora)
    kv = (c_kv @ w_ukv).reshape(Bsz, L, MLA_HEADS, MLA_NOPE + MLA_V)
    k_nope = kv[..., :MLA_NOPE]
    v = kv[..., MLA_NOPE:]
    k_rope = apply_rope(k_rope, cos, sin)
    branch_mla = mla_attention(q_nope, q_rope, k_nope, k_rope, v) @ w_mla_o

    gates = jax.nn.sigmoid((gate_logits + b_gate).astype(jnp.float32)).astype(xn.dtype)
    g_ssm, g_mla = jnp.split(gates, N_BRANCHES, axis=-1)
    return (g_ssm * branch_ssm + g_mla * branch_mla) @ w_out

def memory_cross_attention(hn, memn, w_q, w_kv, w_o):
    Bsz, L, _ = hn.shape
    M = memn.shape[1]
    q = (hn @ w_q).reshape(Bsz, L, MEM_HEADS, MEM_HEAD_DIM)
    k, v = jnp.split(memn @ w_kv, 2, axis=-1)
    k = k.reshape(Bsz, M, MEM_HEADS, MEM_HEAD_DIM)
    v = v.reshape(Bsz, M, MEM_HEADS, MEM_HEAD_DIM)
    s = jnp.einsum('blhd,bmhd->bhlm', q, k, preferred_element_type=jnp.float32) * (MEM_HEAD_DIM ** -0.5)
    p = jax.nn.softmax(s, axis=-1).astype(v.dtype)
    o = jnp.einsum('bhlm,bmhd->blhd', p, v).reshape(Bsz, L, D_MODEL)
    return o @ w_o

def peer_ffn(hn, w_q, sub_keys, u_emb, v_emb):
    Bsz, L, D = hn.shape
    tokens = hn.reshape(-1, PEER_TOKEN_BLOCK, D)

    def block(xc):
        T = xc.shape[0]
        q = (xc @ w_q).reshape(T, PEER_HEADS, 2, PEER_HALF)
        s = jnp.einsum('thsd,hsnd->thsn', q, sub_keys, preferred_element_type=jnp.float32)
        s1, i1 = lax.top_k(s[:, :, 0], PEER_TOPK)
        s2, i2 = lax.top_k(s[:, :, 1], PEER_TOPK)
        cand_s = (s1[..., :, None] + s2[..., None, :]).reshape(T, PEER_HEADS, PEER_TOPK * PEER_TOPK)
        cand_i = (i1[..., :, None] * PEER_N_KEYS + i2[..., None, :]).reshape(T, PEER_HEADS, PEER_TOPK * PEER_TOPK)
        top_s, pos = lax.top_k(cand_s, PEER_TOPK)
        idx = jnp.take_along_axis(cand_i, pos, axis=-1)
        gate = jax.nn.softmax(top_s, axis=-1)
        u = jnp.take(u_emb, idx, axis=0)
        act = jax.nn.gelu(jnp.einsum('thkd,td->thk', u, xc).astype(jnp.float32))
        vv = jnp.take(v_emb, idx, axis=0)
        return jnp.einsum('thk,thkd->td', (gate * act).astype(vv.dtype), vv)

    return lax.map(block, tokens).reshape(Bsz, L, D)

def setup_inputs(seed: int = 0) -> dict:
    key = jax.random.key(seed)
    ks = iter(jax.random.split(key, 48))

    def nrm(shape, std):
        return std * jax.random.normal(next(ks), shape, jnp.float32)

    def gain(shape):
        return 1.0 + nrm(shape, 0.02)

    G, P, Cg = SSM_GROUPS, SSM_STATE, SSM_GROUP
    x = nrm((BATCH, SEQ, D_MODEL), 1.0)
    mem = nrm((BATCH, MEM_TOKENS, D_MODEL), 1.0)
    positions = jnp.broadcast_to(jnp.arange(SEQ, dtype=jnp.int32)[None, :], (BATCH, SEQ))
    g_mix = gain((DEPTH, D_MODEL))
    w_in = nrm((DEPTH, D_MODEL, IN_WIDTH), D_MODEL ** -0.5)
    b_gate = nrm((DEPTH, N_BRANCHES * D_MODEL), 0.02)
    ssm_lam_re = -0.5 + nrm((DEPTH, 2, G, P), 0.01)
    ssm_lam_im = math.pi * jnp.arange(P, dtype=jnp.float32) + nrm((DEPTH, 2, G, P), 0.01)
    ssm_log_dt = jax.random.uniform(next(ks), (DEPTH, 2, G), jnp.float32,
                                    math.log(DT_MIN), math.log(DT_MAX))
    ssm_b_re = nrm((DEPTH, 2, G, P, Cg), (2 * Cg) ** -0.5)
    ssm_b_im = nrm((DEPTH, 2, G, P, Cg), (2 * Cg) ** -0.5)
    ssm_c_re = nrm((DEPTH, 2, G, Cg, P), P ** -0.5)
    ssm_c_im = nrm((DEPTH, 2, G, Cg, P), P ** -0.5)
    ssm_d = nrm((DEPTH, SSM_WIDTH), 1.0)
    w_ssm_glu = nrm((DEPTH, SSM_WIDTH, 2 * D_MODEL), SSM_WIDTH ** -0.5)
    g_q_lora = gain((DEPTH, MLA_Q_LORA))
    w_uq = nrm((DEPTH, MLA_Q_LORA, MLA_HEADS * (MLA_NOPE + MLA_ROPE)), MLA_Q_LORA ** -0.5)
    g_kv_lora = gain((DEPTH, MLA_KV_LORA))
    w_ukv = nrm((DEPTH, MLA_KV_LORA, MLA_HEADS * (MLA_NOPE + MLA_V)), MLA_KV_LORA ** -0.5)
    w_mla_o = nrm((DEPTH, MLA_HEADS * MLA_V, D_MODEL), (MLA_HEADS * MLA_V) ** -0.5)
    w_out = nrm((DEPTH, D_MODEL, D_MODEL), D_MODEL ** -0.5)
    g_mem_q = gain((DEPTH, D_MODEL))
    g_mem_kv = gain((DEPTH, D_MODEL))
    w_mem_q = nrm((DEPTH, D_MODEL, D_MODEL), D_MODEL ** -0.5)
    w_mem_kv = nrm((DEPTH, D_MODEL, 2 * D_MODEL), D_MODEL ** -0.5)
    w_mem_o = nrm((DEPTH, D_MODEL, D_MODEL), D_MODEL ** -0.5)
    g_peer = gain((DEPTH, D_MODEL))
    w_peer_q = nrm((DEPTH, D_MODEL, PEER_HEADS * PEER_KEY_DIM), D_MODEL ** -0.5)
    peer_sub_keys = nrm((DEPTH, PEER_HEADS, 2, PEER_N_KEYS, PEER_HALF), PEER_HALF ** -0.5)
    peer_u = nrm((DEPTH, PEER_EXPERTS, D_MODEL), D_MODEL ** -0.5)
    peer_v = nrm((DEPTH, PEER_EXPERTS, D_MODEL), PEER_HEADS ** -0.5)
    g_final = gain((D_MODEL,))
    return {"x": x, "mem": mem, "positions": positions, "g_mix": g_mix, "w_in": w_in,
            "b_gate": b_gate, "ssm_lam_re": ssm_lam_re, "ssm_lam_im": ssm_lam_im,
            "ssm_log_dt": ssm_log_dt, "ssm_b_re": ssm_b_re, "ssm_b_im": ssm_b_im,
            "ssm_c_re": ssm_c_re, "ssm_c_im": ssm_c_im, "ssm_d": ssm_d, "w_ssm_glu": w_ssm_glu,
            "g_q_lora": g_q_lora, "w_uq": w_uq, "g_kv_lora": g_kv_lora, "w_ukv": w_ukv,
            "w_mla_o": w_mla_o, "w_out": w_out, "g_mem_q": g_mem_q, "g_mem_kv": g_mem_kv,
            "w_mem_q": w_mem_q, "w_mem_kv": w_mem_kv, "w_mem_o": w_mem_o, "g_peer": g_peer,
            "w_peer_q": w_peer_q, "peer_sub_keys": peer_sub_keys, "peer_u": peer_u,
            "peer_v": peer_v, "g_final": g_final}

def reference(x, mem, positions, g_mix, w_in, b_gate, ssm_lam_re, ssm_lam_im, ssm_log_dt,
              ssm_b_re, ssm_b_im, ssm_c_re, ssm_c_im, ssm_d, w_ssm_glu, g_q_lora, w_uq,
              g_kv_lora, w_ukv, w_mla_o, w_out, g_mem_q, g_mem_kv, w_mem_q, w_mem_kv, w_mem_o,
              g_peer, w_peer_q, peer_sub_keys, peer_u, peer_v, g_final):
    cos, sin = rope_tables(positions)
    h = x
    for l in range(DEPTH):
        h = h + mixer_block(rms_norm(h, g_mix[l]), cos, sin, w_in[l], b_gate[l],
                            ssm_lam_re[l], ssm_lam_im[l], ssm_log_dt[l], ssm_b_re[l], ssm_b_im[l],
                            ssm_c_re[l], ssm_c_im[l], ssm_d[l], w_ssm_glu[l], g_q_lora[l], w_uq[l],
                            g_kv_lora[l], w_ukv[l], w_mla_o[l], w_out[l])
        h = h + memory_cross_attention(rms_norm(h, g_mem_q[l]), rms_norm(mem, g_mem_kv[l]),
                                       w_mem_q[l], w_mem_kv[l], w_mem_o[l])
        h = h + peer_ffn(rms_norm(h, g_peer[l]), w_peer_q[l], peer_sub_keys[l], peer_u[l], peer_v[l])
    return rms_norm(h, g_final)


_drawn_inputs = setup_inputs


def setup_inputs(seed=0):
    import zlib

    import numpy as np

    out = dict(_drawn_inputs(seed))
    spreads = {}
    factors = {'g_mix': 4.445,
     'b_gate': 8.0,
     'ssm_lam_re': 64.0,
     'g_q_lora': 8.0,
     'g_kv_lora': 7.101,
     'g_mem_q': 6.92,
     'g_mem_kv': 5.505,
     'g_final': 7.659,
     'g_peer': 8.0}
    for name, (base, spread) in spreads.items():
        noise = np.random.default_rng([zlib.crc32(name.encode()), seed]).standard_normal(out[name].shape)
        drawn = base * np.exp(spread * noise) if base else spread * noise
        out[name] = __import__('jax').numpy.asarray(drawn.astype(out[name].dtype))
    for name, factor in factors.items():
        out[name] = (out[name] * factor).astype(out[name].dtype)
    return out
```

```python
import math
from contextlib import ExitStack

import numpy as np

import concourse.bass as bass
import concourse.mybir as mybir

F32 = mybir.dt.float32
I32 = mybir.dt.int32
U32 = mybir.dt.uint32
ALU = mybir.AluOpType
ACT = mybir.ActivationFunctionType
AX = mybir.AxisListType

P = 128
T, D = 512, 1024
NT, KD = T // P, D // P
EPS = 1e-6
SW, G, CG, NS = 512, 32, 16, 64
CH = P // CG
M = T // CH
GB = 8
NB = G // GB
NH, NOPE, ROPE, HV = 8, 64, 32, 64
QL, KVL = 384, 256
QD = NOPE + ROPE
MT, MH, MD = 256, 4, 256
PH, NK, KH, TOPK = 8, 128, 128, 16
NHS = 2 * PH
NG = NT * PH

VEC = {}
_at = 0
for _n, _w in (("g_mix", 8), ("g_mem_q", 8), ("g_mem_kv", 8), ("g_peer", 8), ("b_gate", 16),
               ("g_q_lora", 3), ("g_kv_lora", 2)):
    VEC[_n] = (_at, _w)
    _at += _w
NVEC = _at

C_ID, C_IOTA, C_ROPE = 0, P, P + 16
NCONST = C_ROPE + 4

NEG = -3.0e38
TWO_PI = 2 * math.pi
PI_HI = 6.28125
PI_MID = round((TWO_PI - PI_HI) * 2 ** 20) / 2 ** 20
PI_LO = TWO_PI - PI_HI - PI_MID
ROUND = 1.5 * 2 ** 23
PI_CLAMP = 3.1415925
SLOTS = 5
TOPK_STEPS = 26
SLAB = 2048
RING = 8


def host_constants():
    c = np.zeros((P, NCONST), np.float32)
    c[:, C_ID:C_ID + P] = np.eye(P, dtype=np.float32)
    c[:, C_IOTA:C_IOTA + 16] = np.arange(16, dtype=np.float32)
    freq = 1.0 / (np.float32(10000.0) ** (np.arange(0, ROPE, 2, dtype=np.float32) / np.float32(ROPE)))
    c[:, C_ROPE] = freq.astype(np.float32)[np.arange(P) % 16]
    cos_rows = slice(64, 96)
    c[cos_rows, C_ROPE + 1] = 0.25
    c[cos_rows, C_ROPE + 2] = math.pi / 2
    c[:, C_ROPE + 3] = 1.0
    c[96:112, C_ROPE + 3] = -1.0
    return c


def psum_jobs():
    j = [("vec",), ("par",), ("C", 0), ("C", 1)]
    j += [("xT", k) for k in range(KD)]
    j += [("u", q) for q in range(4)]
    j += [("uT", q) for q in range(G // 4)]
    j += [("cq", m) for m in range(3)] + [("ckv", m) for m in range(2)] + [("kr",)]

    def prep(b):
        return [("bT", b, r, s) for r in range(2) for s in range(2)] + [("D", b, s) for s in range(2)]

    j += prep(0) + [("X", 0, 0), ("X", 0, 1)]
    for b in range(NB):
        if b + 1 < NB:
            j += prep(b + 1)
        j += [("Y", b)]
        if b + 1 < NB:
            j += [("X", b + 1, 0), ("X", b + 1, 1)]
    j += [("yt", q) for q in range(G // 4)] + [("yT", f) for f in range(4)] + [("qn",), ("kvn",)]
    j += [("V", kt) for kt in range(NT)] + [("Q", 0), ("K", 0)]
    for i in range(NH * NT + 2):
        h, qt = divmod(i, NT)
        if i < NH * NT:
            j.append(("S", i))
            if qt == 1 and h + 1 < NH:
                j += [("Q", h + 1), ("K", h + 1)]
        if i >= 2:
            j.append(("PT", i - 2))
            if (i - 2) % NT == NT - 1:
                j.append(("O", (i - 2) // NT))
    for i in range(KD):
        j += [("val", i), ("gate", i), ("gs", i), ("gm", i), ("mla", i)]
    j += [("out", n, p) for n in range(4) for p in range(2)]
    j += [("mT", k) for k in range(KD)]
    j += [("Km", m) for m in range(4)] + [("Vm", n) for n in range(4)]
    j += [("keyT", q) for q in range(4)]
    j += [("hT", k) for k in range(KD)] + [("Qm", m) for m in range(KD)]
    for i in range(MH * NT + 2):
        if i < MH * NT:
            j.append(("Sm", i))
        if i >= 2:
            j.append(("PTm", i - 2))
            if (i - 2) % NT == NT - 1:
                j += [("Om", (i - 2) // NT, d) for d in range(2)]
    j += [("mo", n, p) for n in range(4) for p in range(2)]
    j += [("pT", k) for k in range(KD)]
    j.append(("pq", 0))
    for s in range(NHS):
        if s + 1 < NHS:
            j.append(("pq", s + 1))
        j.append(("ps", s))
    return j


def slab_plan():
    s = [(("u", 0), ("u", 3)), (("u", 1), ("u", 3)),
         (("c", 0), ("cq", 1)), (("c", 1), ("ckv", 0)), (("c", 2), ("kr",)),
         (("ukv",), ("K", NH - 1))]
    for i in range(KD):
        s.append((("mix", i), ("mla", i)))
        s.append((("gates", i), ("gm", i)))
    s += [(("out", n), ("out", n, 1)) for n in range(4)]
    s += [(("mk", n), ("Km", n)) for n in range(4)]
    s += [(("mv", n), ("Vm", n)) for n in range(4)]
    s += [(("mq", n), ("Qm", 2 * n + 1)) for n in range(4)]
    s += [(("mo", n), ("mo", n, 1)) for n in range(4)]
    s += [(("pq", n), ("pq", 2 * n + 1)) for n in range(8)]
    return s


def rows(w, lo, hi):
    return w[:, lo:hi].rearrange("(k p) n -> p k n", p=P)


def encoder_layer(nc, x, mem, positions, g_mix, w_in, b_gate, ssm_lam_re, ssm_lam_im, ssm_log_dt,
                  ssm_b_re, ssm_b_im, ssm_c_re, ssm_c_im, ssm_d, w_ssm_glu, g_q_lora, w_uq,
                  g_kv_lora, w_ukv, w_mla_o, w_out, g_mem_q, g_mem_kv, w_mem_q, w_mem_kv, w_mem_o,
                  g_peer, w_peer_q, peer_sub_keys, peer_u, peer_v, g_final, consts, out):
    ctx = ExitStack()
    with ctx:
        def sb(name, *shape, dt=F32):
            return ctx.enter_context(nc.sbuf_tensor(name, list(shape), dt))

        def sem(name):
            return ctx.enter_context(nc.semaphore(name))

        cst = sb("cst", P, NCONST)
        ident = cst[:, C_ID:C_ID + P]
        iota16 = cst[:, C_IOTA:C_IOTA + 16]
        ones = sb("ones", P, P)
        vecrow = sb("vecrow", NVEC, P)
        vec = sb("vec", P, NVEC)
        stat = sb("stat", P, 104)
        H = sb("H", P, NT, D)
        XN = sb("XN", P, NT * D)
        FT = sb("FT", P, KD, T)
        slabs = sb("slabs", P, SLOTS * SLAB)
        R = sb("R", P, 28416)
        xn = XN[:, :].rearrange("p (t d) -> p t d", t=NT)

        def reg(lo, *shape, base=R, parts=P):
            n = int(np.prod(shape))
            v = base[0:parts, lo:lo + n]
            names = "abcd"[:len(shape)]
            if len(shape) > 1:
                v = v.rearrange(f"p ({' '.join(names)}) -> p {' '.join(names)}",
                                **dict(zip(names, shape)))
            return v

        Hf = H[:, :, :].rearrange("p t d -> p (t d)")
        U = reg(0, G, M)
        cqT, ckvT = reg(2048, 3, T), reg(3584, 2, T)
        VB = [reg(4608, GB, CH, CG), reg(5632, GB, CH, CG)]
        bb = [reg(6656, G, CG), reg(7168, G, CG)]
        Cc = [reg(7680, G, CG), reg(8192, G, CG)]
        EXT = [reg(8704, GB, 2 * CH - 1, CG), reg(10624, GB, 2 * CH - 1, CG)]
        BT = [reg(12544, GB, P), reg(13568, GB, P)]
        DTm = reg(14592, GB, P)
        t4 = [reg(16640 + 512 * i, GB * M) for i in range(4)]
        ta, tb = reg(16640, GB, CH, CG), reg(17664, GB, CH, CG)
        Z = [reg(18688, GB * M), reg(19200, GB * M)]
        Zs = [reg(15616, GB * M), reg(16128, GB * M)]
        Sst = [reg(19712, GB, M), reg(20224, GB, M)]
        M8 = reg(20736, GB, M)
        Tim = reg(21248, G, M)
        Craw = [reg(18688, NB, P), reg(19200, NB, P)]
        sm = reg(23296, 96, G)
        krT = reg(26368, T)
        mask = reg(26880, M)
        negC = reg(26944, G, CG)
        parrow = [reg(27456 + 128 * i, P, parts=G) for i in range(4)]
        drow = reg(27968, P, parts=G)
        dtrow = reg(28096, 2, parts=G)
        Wst = [[Hf[:, 2048 * q + 1024 * r:2048 * q + 1024 * (r + 1)].rearrange(
            "p (g j c) -> p g j c", g=GB, j=CH) for r in range(2)] for q in range(2)]
        ustage = XN[:, 0:2048].rearrange("p (g q c) -> p g q c", g=G, q=4)
        ytok = XN[0:M, :].rearrange("p (j n) -> p j n", j=CH)
        Tre = XN[:, 2048:4096].rearrange("p (g m) -> p g m", g=G)
        yT = reg(0, 4, T)
        wuq = reg(4608, 3, NH, P)
        V = reg(7680, NT, NH * HV)
        OT = reg(9728, 4, T)
        posb = reg(11776, T).bitcast(I32)
        TAB = reg(12288, T)
        tA, tB, tC = reg(12800, T), reg(13312, T), reg(13824, T)
        QT = [reg(14336, T), reg(14848, T)]
        KT = [reg(15360, T), reg(15872, T)]
        Pm = [reg(16384, T), reg(16896, T)]
        PT = [reg(17408, NT, T), reg(19456, NT, T)]
        lat = [reg(21504, T), reg(22016, T)]
        latsq = reg(17408, 5, T)
        mixtmp = [[reg(21504 + 512 * (5 * q + i), T) for i in range(5)] for q in range(2)]
        mixT = XN[:, :].rearrange("p (k t) -> p k t", k=KD)
        memx = reg(26624 - 2048, 2, D)
        memT = reg(2048, KD, MT)
        KmT = reg(4096, KD, MT)
        Vm = reg(6144, 2, D)
        QmT = reg(8192, KD, T)
        OmT = reg(12288, KD, T)
        Pmm = [reg(16384, MT), reg(16640, MT)]
        PTm = [reg(16896, 2, T), reg(17920, 2, T)]
        keyraw = reg(18944, NHS, KH)
        keysT = reg(20992, NHS, NK)
        qhs = [reg(0, T), reg(512, T)]
        SC = reg(1024, NG, 2 * NK)
        ringmem = [slabs[:, D * i:D * (i + 1)] for i in range(10)] + [reg(9216 + D * i, D) for i in range(6)]
        Ub, Vb = ringmem[:RING], ringmem[RING:]
        XC = reg(15360, D)
        junk = reg(17408, D)
        sc0, sc1 = reg(18432, 2, NK), reg(18688, 2, NK)
        cand, cand1 = reg(18944, TOPK * TOPK), reg(19200, TOPK * TOPK)
        eq = reg(19456, 2 * TOPK, TOPK)
        tv = reg(19968, 2, TOPK)
        ti = reg(20000, 2, TOPK).bitcast(U32)
        tif = reg(20032, 2, TOPK)
        cv = reg(20064, TOPK)
        cpos = reg(20080, TOPK).bitcast(U32)
        cpp = reg(20096, 2 * TOPK).bitcast(U32)
        cpf = reg(20128, 2 * TOPK)
        isel = reg(20160, 2 * TOPK)
        nmx, esum = reg(20192, 1), reg(20193, 1)
        idxf = reg(20194, TOPK)
        idxu = [reg(20224 + 16 * i, TOPK).bitcast(U32) for i in range(2)]
        idxv = [reg(20256 + 16 * i, TOPK).bitcast(U32) for i in range(2)]
        ex = reg(20288, TOPK)
        rinv = reg(20304, 1)
        gate = [reg(20320 + 16 * i, TOPK) for i in range(2)]
        act_row = reg(20352, TOPK)
        gel = reg(20368, TOPK)
        wgt = [reg(20384 + 16 * i, TOPK) for i in range(2)]
        diag = [reg(20480 + 128 * i, P) for i in range(4)]
        gprow = reg(23040, D)
        gfrow = reg(24064, D)

        ps = [ctx.enter_context(nc.psum_tensor(f"bank{i}", [P, 512], F32)) for i in range(8)]

        filled = [sem(f"filled{i}") for i in range(8)]
        drained = [sem(f"drained{i}") for i in range(8)]
        slab_in = [sem(f"slab_in{i}") for i in range(SLOTS)]
        ld_u = [sem(f"ld_u{i}") for i in range(RING)]
        ld_v = [sem(f"ld_v{i}") for i in range(RING)]
        d_cst, d_vec, d_par, d_x, d_ssm = [sem(n) for n in ("d_cst", "d_vec", "d_par", "d_x", "d_ssm")]
        d_res, d_wuq, d_pos, d_mem, d_key = [sem(n) for n in ("d_res", "d_wuq", "d_pos", "d_mem", "d_key")]
        d_grow, d_out = sem("d_grow"), sem("d_out")
        c_dve, c_act, c_pool, c_loop = [sem(n) for n in ("c_dve", "c_act", "c_pool", "c_loop")]
        sq_done, var_done, std_done, xn_done = [sem(n) for n in ("sq_done", "var_done", "std_done", "xn_done")]
        ones_set, zeros_set, par_rows = [sem(n) for n in ("ones_set", "zeros_set", "par_rows")]
        args_done, trig_done, bb_done, table_done = [sem(n) for n in ("args_done", "trig_done", "bb_done", "table_done")]
        vb_done, ext_done, w_done, s_done, yg_done, pow_done = [
            sem(n) for n in ("vb_done", "ext_done", "w_done", "s_done", "yg_done", "pow_done")]
        lat_sq, lat_var, lat_std, lat_done = [sem(n) for n in ("lat_sq", "lat_var", "lat_std", "lat_done")]
        rope_arg, rope_sin, kr_done, qk_done = [sem(n) for n in ("rope_arg", "rope_sin", "kr_done", "qk_done")]
        negmax, p_done = sem("negmax"), sem("p_done")
        sig_done, mix_done = sem("sig_done"), sem("mix_done")
        mnegmax, mp_done = sem("mnegmax"), sem("mp_done")
        idxu_ready, idxv_ready, gates_neg, gates_exp = [
            sem(n) for n in ("idxu_ready", "idxv_ready", "gates_neg", "gates_exp")]
        dots, gelu_done, w_ready, diag_done, v_summed = [
            sem(n) for n in ("dots", "gelu_done", "w_ready", "diag_done", "v_summed")]
        acc_taken, final_done = sem("acc_taken"), sem("final_done")
        apart_dve, apart_pool = sem("apart_dve"), sem("apart_pool")

        jobs = psum_jobs()
        place = {k: (i % 8, i // 8) for i, k in enumerate(jobs)}
        assert len(place) == len(jobs)
        uses = [sum(1 for i in range(len(jobs)) if i % 8 == b) for b in range(8)]

        def take(pe, key):
            b, n = place[key]
            if n:
                pe.wait_ge(drained[b], n)
            return ps[b]

        def full(key):
            return filled[place[key][0]]

        def await_full(eng, key):
            b, n = place[key]
            eng.wait_ge(filled[b], n + 1)
            return ps[b]

        def empty(key):
            return drained[place[key][0]]

        def await_drained(eng, key):
            b, n = place[key]
            eng.wait_ge(drained[b], n + 1)

        plan = slab_plan()
        slab_no = {k: i for i, (k, _) in enumerate(plan)}

        def slab(key, *shape):
            s = (slab_no[key] % SLOTS) * SLAB
            n = int(np.prod(shape))
            return slabs[:, s:s + n].rearrange("p (k n) -> p k n", k=shape[0])

        def slab_parts(key):
            kind = key[0]
            if kind == "u":
                return [(slab(key, 8, 256), rows(w_in, 256 * key[1], 256 * key[1] + 256))]
            if kind == "c" and key[1] < 2:
                lo = SW + 256 * key[1]
                return [(slab(key, 8, 256), rows(w_in, lo, lo + 256))]
            if kind == "c":
                lo = SW + 512
                kr = lo + 128
                s = slab(key, 8, 256)
                parts = [(s[:, :, 0:128], rows(w_in, lo, lo + 128))]
                for i in range(2):
                    at = 128 + 64 * i
                    parts += [(s[:, :, at:at + 32], rows(w_in, kr, kr + 32)),
                              (s[:, :, at + 32:at + 48], rows(w_in, kr + 16, kr + 32)),
                              (s[:, :, at + 48:at + 64], rows(w_in, kr, kr + 16))]
                return parts
            if kind == "ukv":
                return [(slab(key, 2, 1024), rows(w_ukv, 0, 1024))]
            if kind == "mix":
                lo = P * key[1]
                s = slab(key, 4, 3 * P)
                return [(s[:, :, 0:P], rows(w_ssm_glu, lo, lo + P)),
                        (s[:, :, P:2 * P], rows(w_ssm_glu, D + lo, D + lo + P)),
                        (s[:, :, 2 * P:3 * P], rows(w_mla_o, lo, lo + P))]
            if kind == "gates":
                lo = SW + QL + KVL + ROPE + 128 * key[1]
                s = slab(key, 8, 256)
                return [(s[:, :, 0:128], rows(w_in, lo, lo + 128)),
                        (s[:, :, 128:256], rows(w_in, lo + D, lo + D + 128))]
            w, lo = {"out": (w_out, 0), "mk": (w_mem_kv, 0), "mv": (w_mem_kv, D), "mq": (w_mem_q, 0),
                     "mo": (w_mem_o, 0), "pq": (w_peer_q, 0)}[kind]
            lo += 256 * key[1]
            return [(slab(key, 8, 256), rows(w, lo, lo + 256))]

        slab_need, had = [], [0] * SLOTS
        for n, (key, _) in enumerate(plan):
            had[n % SLOTS] += 16 * len(slab_parts(key))
            slab_need.append(had[n % SLOTS])

        def await_slab(pe, key):
            n = slab_no[key]
            pe.wait_ge(slab_in[n % SLOTS], slab_need[n])

        block = ctx.enter_context(nc.Block())

        @block.sync
        def _(sp):
            sp.dma_start(cst[:, :], consts).then_inc(d_cst, 16)
            sp.dma_start(xn, x[0].rearrange("(t p) d -> p t d", p=P)).then_inc(d_x, 16)
            for name, w in (("g_mix", g_mix), ("g_mem_q", g_mem_q), ("g_mem_kv", g_mem_kv),
                            ("g_peer", g_peer), ("b_gate", b_gate), ("g_q_lora", g_q_lora),
                            ("g_kv_lora", g_kv_lora)):
                lo, n = VEC[name]
                sp.dma_start(vecrow[lo:lo + n, :], w[0].rearrange("(k p) -> k p", p=P)).then_inc(d_vec, 16)
            for i, w in enumerate((ssm_lam_re, ssm_lam_im)):
                sp.dma_start(parrow[i].rearrange("g (d p) -> g d p", d=2),
                             w[0].rearrange("d g p -> g d p")).then_inc(d_par, 16)
            sp.dma_start(dtrow, ssm_log_dt[0].rearrange("d g -> g d"), allow_slow_non_contiguous=True).then_inc(d_par, 16)
            sp.dma_start(drow[:, 0:CG], ssm_d[0].rearrange("(g c) -> g c", g=G)).then_inc(d_par, 16)

            def load_slab(n):
                key = plan[n][0]
                if n >= SLOTS:
                    b, k = place[plan[n - SLOTS][1]]
                    sp.wait_ge(filled[b], k + 1)
                for dst, src in slab_parts(key):
                    sp.dma_start(dst, src).then_inc(slab_in[n % SLOTS], 16)

            for n in range(SLOTS):
                load_slab(n)
            for r, w in enumerate((ssm_c_re, ssm_c_im)):
                for d in range(2):
                    sp.dma_start(Craw[r][:, :, 64 * d:64 * d + 64],
                                 w[0, d].rearrange("(b g) c p -> (g c) b p", b=NB)).then_inc(d_ssm, 16)
            for r, w in enumerate((ssm_b_re, ssm_b_im)):
                for d in range(2):
                    sp.dma_start(bb[r][64 * d:64 * d + 64, :, :],
                                 w[0, d].rearrange("g p c -> p g c")).then_inc(d_ssm, 16)
            load_slab(SLOTS)
            await_full(sp, ("Y", NB - 1))
            for k in range(3):
                src = w_uq[P * k:P * k + P, :].rearrange("p (h n) -> p h n", h=NH)
                sp.dma_start(wuq[:, k, :, 0:QD], src).then_inc(d_wuq, 16)
                sp.dma_start(wuq[:, k, :, QD:QD + 16], src[:, :, NOPE + 16:QD]).then_inc(d_wuq, 16)
                sp.dma_start(wuq[:, k, :, QD + 16:P], src[:, :, NOPE:NOPE + 16]).then_inc(d_wuq, 16)
            sp.dma_start(posb, positions[0].partition_broadcast(P)).then_inc(d_pos, 16)
            sp.dma_start(H[:, :, :], x[0].rearrange("(t p) d -> p t d", p=P)).then_inc(d_res, 16)
            for n in range(SLOTS + 1, len(plan)):
                if plan[n][0] == ("out", 0):
                    sp.wait_ge(mix_done, KD)
                    sp.dma_start(memx, mem[0].rearrange("(t p) d -> p t d", p=P)).then_inc(d_mem, 16)
                    sp.dma_start(keyraw, peer_sub_keys[0].rearrange("h s n d -> n (h s) d")).then_inc(d_key, 16)
                if plan[n][0] == ("mq", 0):
                    await_drained(sp, ("mT", KD - 1))
                    sp.dma_start(gprow, g_peer[0].partition_broadcast(P)).then_inc(d_grow, 16)
                    sp.dma_start(gfrow, g_final.partition_broadcast(P)).then_inc(d_grow, 16)
                load_slab(n)
            for t in range(NT):
                sp.wait_ge(final_done, t + 1)
                sp.dma_start(out[0, P * t:P * t + P, :], xn[:, t, :]).then_inc(d_out, 16)
            sp.wait_ge(d_out, 16 * NT)


        NORMS = (NT, 2, NT, NT, NT)
        before = [sum(NORMS[:k]) for k in range(6)]

        def sumsq(k, t):
            return stat[:, 16 * k + t:16 * k + t + 1]

        @block.scalar
        def _(act):
            own = [0]

            def settle(ins):
                own[0] += 1
                ins.then_inc(c_act, 1)
                act.wait_ge(c_act, own[0])

            def copy_out(key, dst, src, scale=1.0):
                act.activation(dst, src, ACT.Copy, scale=scale).then_inc(empty(key), 1)

            def squares(k, src, scratch, before_tile=None):
                for t in range(NORMS[k]):
                    if before_tile:
                        before_tile(t)
                    settle(act.activation(scratch, src[:, t, :], ACT.Square, accum_out=sumsq(k, t)))
                act.sem_inc(sq_done, 1)

            def roots(k):
                act.wait_ge(var_done, k + 1)
                n = NORMS[k]
                act.activation(stat[:, 16 * k + 8:16 * k + 8 + n], stat[:, 16 * k + 4:16 * k + 4 + n],
                               ACT.Sqrt).then_inc(std_done, 1)

            def features(name, key, dst, width):
                for k in range(KD):
                    b = await_full(act, (key, k))
                    c = VEC[name][0] + k
                    copy_out((key, k), dst[:, k, :], b[:, 0:width], scale=vec[:, c:c + 1])

            act.wait_ge(d_x, 16)
            squares(0, xn, FT[:, 0:2, :].rearrange("p k t -> p (k t)"))
            roots(0)
            act.wait_ge(d_par, 64)
            settle(act.activation(dtrow, dtrow, ACT.Exp))
            for d in range(2):
                settle(act.activation(parrow[2][:, 64 * d:64 * d + 64],
                                      dtrow[:, d:d + 1].to_broadcast([G, 64]), ACT.Copy))
            act.activation(parrow[3].rearrange("g (j c) -> g j c", j=CH),
                           drow[:, 0:CG].unsqueeze(1).to_broadcast([G, CH, CG]), ACT.Copy).then_inc(par_rows, 1)
            for r in range(2):
                b = await_full(act, ("C", r))
                copy_out(("C", r), Cc[r].rearrange("p g c -> p (g c)"), b[:, :])
            await_drained(act, ("vec",))
            features("g_mix", "xT", FT, T)
            act.wait_ge(args_done, 1)
            act.activation(sm[:, 6, :], sm[:, 4, :], ACT.Exp).then_inc(trig_done, 1)
            act.activation(sm[:, 12, :], sm[:, 4, :], ACT.Exp, scale=float(CH)).then_inc(trig_done, 1)
            act.activation(sm[:, 7:9, :], sm[:, 10:12, :], ACT.Sin).then_inc(trig_done, 1)
            for q in range(4):
                b = await_full(act, ("u", q))
                copy_out(("u", q), ustage[:, :, q, :], b[:, :].rearrange("p (g c) -> p g c", g=G))
            for q in range(G // 4):
                b = await_full(act, ("uT", q))
                src = b[0:64, :].rearrange("p (g m j) -> p g j m", g=4, j=2)
                settle(act.activation(U[0:64, 4 * q:4 * q + 4, :], src[:, :, 0, :], ACT.Copy))
                copy_out(("uT", q), U[64:128, 4 * q:4 * q + 4, :], src[:, :, 1, :])
            for m in range(3):
                b = await_full(act, ("cq", m))
                copy_out(("cq", m), cqT[:, m, :], b[:, :])
            for m in range(2):
                b = await_full(act, ("ckv", m))
                copy_out(("ckv", m), ckvT[:, m, :], b[:, :])
            b = await_full(act, ("kr",))
            copy_out(("kr",), krT, b[:, :])

            def block_prep(q):
                act.wait_ge(vb_done, 2 * (q + 1))
                act.wait_ge(zeros_set, 1)
                if q:
                    await_full(act, ("D", q - 1, 1))
                for r in range(2):
                    act.activation(EXT[r][0:64, :, 0:CH, :].rearrange("p g j c -> p g (j c)"),
                                   VB[r][0:64].rearrange("p g j c -> p g (j c)"), ACT.Copy).then_inc(ext_done, 1)
                    act.activation(EXT[r][64:128, :, CH - 1:, :].rearrange("p g j c -> p g (j c)"),
                                   VB[r][64:128].rearrange("p g j c -> p g (j c)"), ACT.Copy).then_inc(ext_done, 1)
                if q:
                    await_full(act, ("X", q - 1, 1))
                for r in range(2):
                    for s in range(2):
                        b = await_full(act, ("bT", q, r, s))
                        copy_out(("bT", q, r, s), BT[r][:, 4 * s:4 * s + 4, :].rearrange("p g n -> p (g n)"), b[:, :])
                if q:
                    await_full(act, ("Y", q - 1))
                for s in range(2):
                    b = await_full(act, ("D", q, s))
                    copy_out(("D", q, s), DTm[:, 4 * s:4 * s + 4, :].rearrange("p g n -> p (g n)"), b[:, :])

            block_prep(0)
            for q in range(NB):
                if q + 1 < NB:
                    block_prep(q + 1)
                await_drained(act, ("Y", q))
                yq = U[:, GB * q:GB * q + GB, :]
                act.activation(yq, yq, ACT.Gelu_apprx_tanh).then_inc(yg_done, 1)
            for m in range(3):
                act.activation(latsq[:, m, :], cqT[:, m, :], ACT.Square).then_inc(lat_sq, 1)
            for m in range(2):
                act.activation(latsq[:, 3 + m, :], ckvT[:, m, :], ACT.Square).then_inc(lat_sq, 1)
            act.wait_ge(s_done, 4 * NB)
            for q in range(G // 4):
                b = await_full(act, ("yt", q))
                for g in range(4):
                    ins = act.activation(ytok[:, :, 64 * q + 16 * g:64 * q + 16 * g + 16],
                                         b[0:M, P * g:P * g + P].rearrange("p (j c) -> p j c", j=CH), ACT.Copy)
                ins.then_inc(empty(("yt", q)), 1)
            for f in range(4):
                b = await_full(act, ("yT", f))
                copy_out(("yT", f), yT[:, f, :].rearrange("p (m j) -> p j m", j=CH),
                         b[:, :].rearrange("p (j m) -> p j m", j=CH))
            for k in range(2):
                act.wait_ge(lat_var, k + 1)
                act.activation(lat[k], lat[k], ACT.Sqrt).then_inc(lat_std, 1)
            act.wait_ge(rope_arg, 1)
            act.activation(TAB, tA, ACT.Sin).then_inc(rope_sin, 1)
            for kt in range(NT):
                b = await_full(act, ("V", kt))
                copy_out(("V", kt), V[:, kt, :], b[:, :])

            def head_in(h):
                b = await_full(act, ("Q", h))
                if h >= 2:
                    await_full(act, ("S", NT * (h - 1) - 1))
                copy_out(("Q", h), QT[h % 2], b[:, :])
                b = await_full(act, ("K", h))
                copy_out(("K", h), KT[h % 2][0:64, :], b[0:64, :])

            def exponentials(i, key, width, bufs, negs, scale, base, tkey):
                b = await_full(act, (key, i))
                act.wait_ge(negs, i + 1)
                if i >= 2:
                    await_full(act, (tkey, i - 2))
                act.activation(bufs[i % 2], b[:, 0:width], ACT.Exp, scale=scale,
                               bias=stat[:, base + i % 4:base + i % 4 + 1],
                               accum_out=stat[:, base + 4 + i % 4:base + 5 + i % 4]).then_inc(empty((key, i)), 1)

            head_in(0)
            for i in range(NH * NT + 2):
                if i < NH * NT:
                    exponentials(i, "S", T, Pm, negmax, QD ** -0.5, 80, "PT")
                    if i % NT == 1 and i // NT + 1 < NH:
                        head_in(i // NT + 1)
                if i >= 2:
                    h, qt = divmod(i - 2, NT)
                    if qt % 2:
                        b = await_full(act, ("PT", i - 2))
                        if h >= 2:
                            await_full(act, ("O", h - 2))
                        copy_out(("PT", i - 2), PT[h % 2][:, :, P * qt:P * qt + P],
                                 b[:, :].rearrange("p (k q) -> p k q", k=NT))
                    if qt == NT - 1:
                        b = await_full(act, ("O", h))
                        copy_out(("O", h), OT[64 * (h % 2):64 * (h % 2) + 64, h // 2, :], b[0:HV, :])
            for i in range(KD):
                s = mixtmp[i % 2]
                if i >= 2:
                    act.wait_ge(mix_done, i - 1)
                b = await_full(act, ("gate", i))
                act.activation(s[0], b[:, :], ACT.Sigmoid).then_inc(empty(("gate", i)), 1)
                for n, kind in enumerate(("gs", "gm")):
                    b = await_full(act, (kind, i))
                    c = VEC["b_gate"][0] + KD * n + i
                    act.activation(s[1 + n], b[:, :], ACT.Sigmoid,
                                   bias=vec[:, c:c + 1]).then_inc(empty((kind, i)), 1)
            act.wait_ge(d_mem, 16)
            squares(1, memx, junk)
            roots(1)

            def stream_tile(kind):
                def wait(t):
                    for n in range(4):
                        await_drained(act, (kind, n, t // 2))
                return wait

            squares(2, H, junk, stream_tile("out"))
            roots(2)
            features("g_mem_kv", "mT", memT, MT)
            act.wait_ge(mix_done, KD)
            for q in range(4):
                b = await_full(act, ("keyT", q))
                copy_out(("keyT", q), keysT[:, 4 * q:4 * q + 4, :].rearrange("p k n -> p (k n)"), b[:, :])
            features("g_mem_q", "hT", FT, T)
            for m in range(KD):
                b = await_full(act, ("Qm", m))
                copy_out(("Qm", m), QmT[:, m, :], b[:, :])
            for i in range(MH * NT + 2):
                if i < MH * NT:
                    exponentials(i, "Sm", MT, Pmm, mnegmax, MD ** -0.5, 92, "PTm")
                if i >= 2 and (i - 2) % NT == NT - 1:
                    h = (i - 2) // NT
                    for d in range(2):
                        b = await_full(act, ("Om", h, d))
                        copy_out(("Om", h, d), OmT[:, 2 * h + d, :], b[:, :])
            squares(3, H, junk, stream_tile("mo"))
            roots(3)
            features("g_peer", "pT", FT, T)
            for s in range(NHS):
                b = await_full(act, ("pq", s))
                if s >= 2:
                    await_full(act, ("ps", s - 2))
                copy_out(("pq", s), qhs[s % 2], b[:, :])

            def gate_exponentials(g):
                act.wait_ge(gates_neg, g + 1)
                act.activation(ex, cv, ACT.Exp, bias=nmx, accum_out=esum).then_inc(gates_exp, 1)

            def gelu_of(g):
                act.wait_ge(dots, TOPK * (g + 1))
                act.activation(gel, act_row, ACT.Gelu_apprx_tanh).then_inc(gelu_done, 1)

            def diagonals(g, par):
                act.wait_ge(w_ready, g + 1)
                for s in range(TOPK):
                    if not isinstance(g, int) or g or s >= 4:
                        act.wait_ge(v_summed, g * TOPK + (s - 3))
                    act.activation(diag[s % 4], ident, ACT.Copy,
                                   scale=wgt[par][:, s:s + 1]).then_inc(diag_done, 1)

            gate_exponentials(0)
            gate_exponentials(1)
            gelu_of(0)

            def group(g, par, topk=True, dot=True):
                if topk:
                    gate_exponentials(g + 2)
                diagonals(g, par)
                if dot:
                    gelu_of(g + 1)

            group(0, 0)
            group(1, 1)
            with act.Fori(1, NG // 2 - 1) as i:
                group(i * 2, 0)
                group(i * 2 + 1, 1)
            group(NG - 2, 0, topk=False)
            group(NG - 1, 1, topk=False, dot=False)

            def last_tile(t):
                act.wait_ge(acc_taken, NG)

            squares(4, H, junk, last_tile)
            roots(4)

        @block.vector
        def _(dve):
            own = [0]

            def step(ins):
                own[0] += 1
                ins.then_inc(c_dve, 1)
                dve.wait_ge(c_dve, own[0])

            def tt(out, a, b, op):
                step(dve.tensor_tensor(out, a, b, op))

            def signal(ins, s, n):
                ins.then_inc(s, 1)
                dve.wait_ge(s, n)

            def normalise(k, src, dst):
                n = NORMS[k]
                dve.wait_ge(sq_done, k + 1)
                v = stat[:, 16 * k + 4:16 * k + 4 + n]
                dve.tensor_scalar(v, stat[:, 16 * k:16 * k + n], 1.0 / D, EPS, ALU.mult, ALU.add).then_inc(var_done, 1)
                dve.wait_ge(std_done, k + 1)
                r = stat[:, 16 * k + 12:16 * k + 12 + n]
                step(dve.reciprocal(r, stat[:, 16 * k + 8:16 * k + 8 + n]))
                for t in range(n):
                    c = stat[:, 16 * k + 12 + t:16 * k + 13 + t]
                    dve.tensor_scalar(dst[:, t, :], src[:, t, :], c, None, ALU.mult).then_inc(xn_done, 1)

            def reduce_turns(src, dst, n, turn=0.0, angle=0.0):
                step(dve.tensor_scalar(n, src, 1.0 / TWO_PI, turn, ALU.mult, ALU.add))
                step(dve.tensor_scalar(n, n, ROUND, -ROUND, ALU.add, ALU.add))
                step(dve.scalar_tensor_tensor(dst, n, -PI_HI, src, ALU.mult, ALU.add))
                step(dve.scalar_tensor_tensor(dst, n, -PI_MID, dst, ALU.mult, ALU.add))
                step(dve.scalar_tensor_tensor(dst, n, -PI_LO, dst, ALU.mult, ALU.add))
                step(dve.tensor_scalar(dst, dst, angle, PI_CLAMP, ALU.add, ALU.min))
                step(dve.tensor_scalar(dst, dst, -PI_CLAMP, None, ALU.max))

            b = await_full(dve, ("vec",))
            dve.tensor_copy(vec[:, :], b[:, 0:NVEC]).then_inc(empty(("vec",)), 1)
            dve.wait_ge(d_x, 16)
            normalise(0, xn, xn)
            b = await_full(dve, ("par",))
            dve.tensor_copy(sm[:, 0:4, :].rearrange("p a g -> p (a g)"), b[:, 0:4 * G]).then_inc(empty(("par",)), 1)
            await_drained(dve, ("par",))
            lre, lim, dt, dsk = (sm[:, i, :] for i in range(4))
            tt(sm[:, 4, :], lre, dt, ALU.mult)
            tt(sm[:, 5, :], lim, dt, ALU.mult)
            reduce_turns(sm[:, 5, :], sm[:, 10, :], sm[:, 9, :], 0.25, math.pi / 2)
            reduce_turns(sm[:, 5, :], sm[:, 11, :], sm[:, 9, :])
            dve.sem_inc(args_done, 1)
            dve.wait_ge(trig_done, 3)
            mag, co, si = sm[:, 6, :], sm[:, 7, :], sm[:, 8, :]

            def pw(r, k):
                return sm[:, 16 + 9 * r + k, :]

            step(dve.memset(pw(0, 0), 1.0))
            step(dve.memset(pw(1, 0), 0.0))
            tt(pw(0, 1), mag, co, ALU.mult)
            tt(pw(1, 1), mag, si, ALU.mult)

            def cmul(o, a, b, tmp):
                tt(tmp[0], a[0], b[0], ALU.mult)
                tt(tmp[1], a[1], b[1], ALU.mult)
                tt(o[0], tmp[0], tmp[1], ALU.subtract)
                tt(tmp[0], a[0], b[1], ALU.mult)
                tt(tmp[1], a[1], b[0], ALU.mult)
                tt(o[1], tmp[0], tmp[1], ALU.add)

            n = 1
            while n < CH:
                def span(r, lo, m):
                    return sm[:, 16 + 9 * r + lo:16 + 9 * r + lo + m, :]
                top = [pw(r, n).unsqueeze(1).to_broadcast([P, n, G]) for r in range(2)]
                cmul([span(r, n + 1, n) for r in range(2)], [span(r, 1, n) for r in range(2)], top,
                     [sm[:, 78:78 + n, :], sm[:, 86:86 + n, :]])
                n *= 2
            for r in range(2):
                px, py = 34 + 8 * r, 50 + 8 * r
                base = 16 + 9 * r
                for k in range(CH):
                    step(dve.tensor_copy(sm[0:64, px + k, :], sm[0:64, base + CH - 1 - k, :]))
                    step(dve.tensor_copy(sm[64:128, py + k, :], sm[64:128, base + CH - k, :]))
                step(dve.tensor_copy(sm[64:128, px:px + CH, :], sm[64:128, base:base + CH, :]))
                step(dve.tensor_copy(sm[0:64, py:py + CH, :], sm[0:64, base + 1:base + 1 + CH, :]))
            step(dve.tensor_scalar(sm[:, 94, :], pw(0, 1), -1.0, None, ALU.add))
            tt(sm[:, 78, :], lre, lre, ALU.mult)
            tt(sm[:, 79, :], lim, lim, ALU.mult)
            tt(sm[:, 80, :], sm[:, 78, :], sm[:, 79, :], ALU.add)
            step(dve.reciprocal(sm[:, 81, :], sm[:, 80, :]))
            tt(sm[:, 82, :], sm[:, 94, :], lre, ALU.mult)
            tt(sm[:, 83, :], pw(1, 1), lim, ALU.mult)
            tt(sm[:, 84, :], sm[:, 82, :], sm[:, 83, :], ALU.add)
            tt(sm[:, 84, :], sm[:, 84, :], sm[:, 81, :], ALU.mult)
            tt(sm[:, 82, :], pw(1, 1), lre, ALU.mult)
            tt(sm[:, 83, :], sm[:, 94, :], lim, ALU.mult)
            tt(sm[:, 85, :], sm[:, 82, :], sm[:, 83, :], ALU.subtract)
            tt(sm[:, 85, :], sm[:, 85, :], sm[:, 81, :], ALU.mult)
            dve.wait_ge(d_ssm, 16 * 8)
            fr, fi = (sm[:, 84 + r, :].unsqueeze(2).to_broadcast([P, G, CG]) for r in range(2))
            tg = [t.rearrange("p (g c) -> p g c", g=G) for t in t4]
            tt(tg[0], bb[0], fr, ALU.mult)
            tt(tg[1], bb[1], fi, ALU.mult)
            tt(tg[2], bb[1], fr, ALU.mult)
            tt(tg[3], bb[0], fi, ALU.mult)
            tt(bb[0], tg[0], tg[1], ALU.subtract)
            tt(bb[1], tg[2], tg[3], ALU.add)
            await_drained(dve, ("C", 0))
            await_drained(dve, ("C", 1))
            signal(dve.tensor_scalar(negC, Cc[1], -1.0, None, ALU.mult), pow_done, 1)

            def contributions(q):
                gs = slice(GB * q, GB * q + GB)
                if q:
                    await_full(dve, ("bT", q - 1, 1, 1))
                    dve.wait_ge(ext_done, 4 * q)
                pr, pi = (sm[:, 34 + 8 * r:42 + 8 * r, gs].rearrange("p k g -> p g k").unsqueeze(3)
                          .to_broadcast([P, GB, CH, CG]) for r in range(2))
                br, bi = (bb[r][:, gs, :].unsqueeze(2).to_broadcast([P, GB, CH, CG]) for r in range(2))
                tt(ta, pr, br, ALU.mult)
                tt(tb, pi, bi, ALU.mult)
                signal(dve.tensor_tensor(VB[0], ta, tb, ALU.subtract), vb_done, 2 * q + 1)
                tt(ta, pr, bi, ALU.mult)
                tt(tb, pi, br, ALU.mult)
                signal(dve.tensor_tensor(VB[1], ta, tb, ALU.add), vb_done, 2 * q + 2)

            contributions(0)
            dve.wait_ge(table_done, 1)
            for q in range(NB):
                if q + 1 < NB:
                    contributions(q + 1)
                gs = slice(GB * q, GB * q + GB)
                tc, ts = (t[:, gs, :].rearrange("p g m -> p (g m)") for t in (Tre, Tim))
                tt(M8, mask.unsqueeze(1).to_broadcast([P, GB, M]),
                   sm[:, 12, gs].unsqueeze(2).to_broadcast([P, GB, M]), ALU.mult)
                xr = await_full(dve, ("X", q, 0))
                xi = await_full(dve, ("X", q, 1))
                tt(t4[0], xr[:, :], tc, ALU.mult)
                tt(t4[2], xr[:, :], ts, ALU.mult)
                dve.sem_inc(empty(("X", q, 0)), 1)
                tt(t4[1], xi[:, :], ts, ALU.mult)
                tt(t4[3], xi[:, :], tc, ALU.mult)
                dve.sem_inc(empty(("X", q, 1)), 1)
                tt(Z[0], t4[0], t4[1], ALU.add)
                tt(Z[1], t4[3], t4[2], ALU.subtract)
                m8 = M8.rearrange("p g m -> p (g m)")
                for r in range(2):
                    step(dve.tensor_tensor_scan(Zs[r][0:64, :], m8[0:64, :], Z[r][0:64, :], 0.0, ALU.mult, ALU.add))
                    step(dve.tensor_tensor_scan(Zs[r][64:128, ::-1], m8[64:128, ::-1], Z[r][64:128, ::-1], 0.0,
                                                ALU.mult, ALU.add))
                tt(t4[0], Zs[0], tc, ALU.mult)
                tt(t4[1], Zs[1], ts, ALU.mult)
                tt(t4[2], Zs[0], ts, ALU.mult)
                tt(t4[3], Zs[1], tc, ALU.mult)
                if q:
                    await_full(dve, ("Y", q - 1))
                tv4 = [t.rearrange("p (g m) -> p g m", g=GB) for t in t4]
                for r, op in ((0, ALU.subtract), (1, ALU.add)):
                    for lo, dst, src in ((0, slice(1, M), slice(0, M - 1)), (64, slice(0, M - 1), slice(1, M))):
                        dve.tensor_tensor(Sst[r][lo:lo + 64, :, dst], tv4[2 * r][lo:lo + 64, :, src],
                                          tv4[2 * r + 1][lo:lo + 64, :, src], op).then_inc(s_done, 1)
                dve.wait_ge(s_done, 4 * (q + 1))
                b = await_full(dve, ("Y", q))
                tt(tv4[0], U[:, gs, :], dsk[:, gs].unsqueeze(2).to_broadcast([P, GB, M]), ALU.mult)
                dve.tensor_tensor(U[:, gs, :], b[:, :].rearrange("p (g m) -> p g m", g=GB), tv4[0],
                                  ALU.add).then_inc(empty(("Y", q)), 1)
                await_drained(dve, ("Y", q))

            for k, (key, n) in enumerate(((("qn",), QL), (("kvn",), KVL))):
                b = await_full(dve, key)
                dve.tensor_scalar(lat[k], b[:, :], 1.0 / n, EPS, ALU.mult, ALU.add).then_inc(empty(key), 1)
                await_drained(dve, key)
                dve.sem_inc(lat_var, 1)
            dve.wait_ge(d_pos, 16)
            step(dve.tensor_copy(tC, posb))
            step(dve.tensor_scalar(tC, tC, cst[:, C_ROPE:C_ROPE + 1], None, ALU.mult))
            step(dve.tensor_scalar(tB, tC, 1.0 / TWO_PI, cst[:, C_ROPE + 1:C_ROPE + 2], ALU.mult, ALU.add))
            step(dve.tensor_scalar(tB, tB, ROUND, -ROUND, ALU.add, ALU.add))
            step(dve.scalar_tensor_tensor(tA, tB, -PI_HI, tC, ALU.mult, ALU.add))
            step(dve.scalar_tensor_tensor(tA, tB, -PI_MID, tA, ALU.mult, ALU.add))
            step(dve.scalar_tensor_tensor(tA, tB, -PI_LO, tA, ALU.mult, ALU.add))
            step(dve.tensor_scalar(tA, tA, cst[:, C_ROPE + 2:C_ROPE + 3], PI_CLAMP, ALU.add, ALU.min))
            signal(dve.tensor_scalar(tA, tA, -PI_CLAMP, None, ALU.max), rope_arg, 1)
            for k, (m0, n, src, name) in enumerate(((0, 3, cqT, "g_q_lora"), (3, 2, ckvT, "g_kv_lora"))):
                dve.wait_ge(lat_std, k + 1)
                step(dve.reciprocal(lat[k], lat[k]))
                for m in range(n):
                    c = VEC[name][0] + m
                    signal(dve.scalar_tensor_tensor(src[:, m, :], src[:, m, :], vec[:, c:c + 1], lat[k],
                                                    ALU.mult, ALU.mult), lat_done, m0 + m + 1)
            dve.wait_ge(rope_sin, 1)
            step(dve.tensor_scalar(TAB, TAB, cst[:, C_ROPE + 3:C_ROPE + 4], None, ALU.mult))

            def turn(src, dsts):
                step(dve.tensor_tensor(tA[64:96, :], src[64:96, :], TAB[64:96, :], ALU.mult))
                step(dve.tensor_tensor(tB[64:96, :], src[96:128, :], TAB[96:128, :], ALU.mult))
                return [dve.tensor_tensor(d[64:96, :], tA[64:96, :], tB[64:96, :], ALU.add) for d in dsts]

            for n, ins in enumerate(turn(krT, KT)):
                ins.then_inc(kr_done, 1)
            dve.wait_ge(kr_done, 2)

            def head_in(h):
                await_drained(dve, ("Q", h))
                signal(turn(QT[h % 2], [QT[h % 2]])[0], qk_done, h + 1)

            def row_max(i, key, width, negs, scale, base):
                b = await_full(dve, (key, i))
                c = stat[:, base + i % 4:base + i % 4 + 1]
                step(dve.tensor_reduce(c, b[:, 0:width], AX.X, ALU.max))
                dve.tensor_scalar(c, c, -scale, None, ALU.mult).then_inc(negs, 1)

            def normal(i, key, bufs, done, base):
                await_drained(dve, (key, i))
                c = stat[:, base + 8 + i % 4:base + 9 + i % 4]
                step(dve.reciprocal(c, stat[:, base + 4 + i % 4:base + 5 + i % 4]))
                dve.tensor_scalar(bufs[i % 2], bufs[i % 2], c, None, ALU.mult).then_inc(done, 1)

            head_in(0)
            for i in range(NH * NT + 2):
                if i < NH * NT:
                    row_max(i, "S", T, negmax, QD ** -0.5, 80)
                if 1 <= i <= NH * NT:
                    normal(i - 1, "S", Pm, p_done, 80)
                if i < NH * NT and i % NT == 1 and i // NT + 1 < NH:
                    head_in(i // NT + 1)
                if i >= 2:
                    h, qt = divmod(i - 2, NT)
                    if qt % 2 == 0:
                        b = await_full(dve, ("PT", i - 2))
                        if h >= 2:
                            await_full(dve, ("O", h - 2))
                        dve.tensor_copy(PT[h % 2][:, :, P * qt:P * qt + P],
                                        b[:, :].rearrange("p (k q) -> p k q", k=NT)).then_inc(empty(("PT", i - 2)), 1)
            for i in range(KD):
                s = mixtmp[i % 2]
                b = await_full(dve, ("val", i))
                await_drained(dve, ("gate", i))
                dve.tensor_tensor(s[3], b[:, :], s[0], ALU.mult).then_inc(empty(("val", i)), 1)
                await_drained(dve, ("val", i))
                await_drained(dve, ("gs", i))
                tt(s[3], s[3], s[1], ALU.mult)
                b = await_full(dve, ("mla", i))
                await_drained(dve, ("gm", i))
                dve.tensor_tensor(s[4], b[:, :], s[2], ALU.mult).then_inc(empty(("mla", i)), 1)
                await_drained(dve, ("mla", i))
                dve.tensor_tensor(mixT[:, i, :], s[3], s[4], ALU.add).then_inc(mix_done, 1)
            normalise(1, memx, memx)

            def residual(kind):
                for n in range(4):
                    for p in range(2):
                        b = await_full(dve, (kind, n, p))
                        h = H[:, 2 * p:2 * p + 2, 256 * n:256 * n + 256]
                        dve.tensor_tensor(h, b[:, :].rearrange("p (t n) -> p t n", t=2), h,
                                          ALU.add).then_inc(empty((kind, n, p)), 1)

            dve.wait_ge(d_res, 16)
            residual("out")
            for n in range(4):
                for p in range(2):
                    await_drained(dve, ("out", n, p))
            normalise(2, H, xn)
            for n in range(4):
                b = await_full(dve, ("Km", n))
                dve.tensor_copy(KmT[:, 2 * n:2 * n + 2, :].rearrange("p m t -> p (m t)"), b[:, :]).then_inc(empty(("Km", n)), 1)
            for n in range(4):
                b = await_full(dve, ("Vm", n))
                dve.tensor_copy(Vm[:, :, 256 * n:256 * n + 256],
                                b[:, :].rearrange("p (t n) -> p t n", t=2)).then_inc(empty(("Vm", n)), 1)
            for i in range(MH * NT + 2):
                if i < MH * NT:
                    row_max(i, "Sm", MT, mnegmax, MD ** -0.5, 92)
                if 1 <= i <= MH * NT:
                    normal(i - 1, "Sm", Pmm, mp_done, 92)
                if i >= 2:
                    h, qt = divmod(i - 2, NT)
                    b = await_full(dve, ("PTm", i - 2))
                    if h >= 2:
                        await_full(dve, ("Om", h - 2, 1))
                    dve.tensor_copy(PTm[h % 2][:, :, P * qt:P * qt + P],
                                    b[:, 0:MT].rearrange("p (k q) -> p k q", k=2)).then_inc(empty(("PTm", i - 2)), 1)
            residual("mo")
            for n in range(4):
                for p in range(2):
                    await_drained(dve, ("mo", n, p))
            normalise(3, H, xn)
            dve.wait_ge(xn_done, before[4])
            dve.wait_ge(d_grow, 32)
            for s in range(NHS):
                b = await_full(dve, ("ps", s))
                dst = SC.rearrange("p (t h) n -> p t h n", t=NT)[:, :, s // 2, NK * (s % 2):NK * (s % 2) + NK]
                dve.tensor_copy(dst, b[:, :].rearrange("p (t n) -> p t n", t=NT)).then_inc(empty(("ps", s)), 1)
            for s in range(NHS):
                await_drained(dve, ("ps", s))

            count = [0, None]

            def lstep(ins, apart=False):
                count[0] += 1
                ins.then_inc(c_loop, 1)
                dve.wait_ge(c_loop, count[1] + count[0])
                if apart:
                    dve.sem_inc(apart_dve, 1)

            def top16(vals, spare, v, ix):
                lstep(dve.max(v[:, 0:8], vals), apart=True)
                lstep(dve.max_index(ix[:, 0:8], v[:, 0:8], vals), apart=True)
                lstep(dve.match_replace(spare, v[:, 0:8], vals, NEG), apart=True)
                lstep(dve.max(v[:, 8:16], spare), apart=True)
                lstep(dve.max_index(ix[:, 8:16], v[:, 8:16], spare), apart=True)

            def topk(g, par):
                lstep(dve.tensor_copy(sc0.rearrange("p s n -> p (s n)"),
                                      SC[:, bass.ds(g, 1), :].rearrange("p a n -> p (a n)")), apart=True)
                for s in range(2):
                    top16(sc0[:, s, :], sc1[:, s, :], tv[:, s, :], ti[:, s, :])
                lstep(dve.tensor_copy(tif, ti))
                lstep(dve.tensor_tensor(cand.rearrange("p (a b) -> p a b", a=TOPK),
                                        tv[:, 0, :].unsqueeze(2).to_broadcast([P, TOPK, TOPK]),
                                        tv[:, 1, :].unsqueeze(1).to_broadcast([P, TOPK, TOPK]), ALU.add), apart=True)
                top16(cand, cand1, cv, cpos)
                lstep(dve.tensor_scalar(nmx, cv[:, 0:1], -1.0, None, ALU.mult))
                dve.sem_inc(gates_neg, 1)
                lstep(dve.tensor_scalar(cpp[:, 0:16], cpos, 4, None, ALU.logical_shift_right))
                lstep(dve.tensor_scalar(cpp[:, 16:32], cpos, 15, None, ALU.bitwise_and))
                lstep(dve.tensor_copy(cpf, cpp))
                lstep(dve.tensor_tensor(eq, iota16.unsqueeze(1).to_broadcast([P, 2 * TOPK, TOPK]),
                                        cpf.unsqueeze(2).to_broadcast([P, 2 * TOPK, TOPK]), ALU.is_equal))
                e4 = eq.rearrange("p (s k) a -> p s k a", s=2)
                lstep(dve.tensor_tensor(e4, e4, tif.unsqueeze(2).to_broadcast([P, 2, TOPK, TOPK]), ALU.mult))
                lstep(dve.tensor_reduce(isel, eq, AX.X, ALU.add))
                lstep(dve.scalar_tensor_tensor(idxu[par], isel[:, 0:16], float(NK), isel[:, 16:32], ALU.mult, ALU.add))
                dve.sem_inc(idxu_ready, 1)

            def gates_of(g, par):
                dve.wait_ge(gates_exp, g + 1)
                lstep(dve.reciprocal(rinv, esum))
                lstep(dve.tensor_scalar(gate[par], ex, rinv, None, ALU.mult))

            def dot_products(g, par):
                lstep(dve.tensor_tensor(XC, xn[:, bass.ds(g // PH, 1), :].rearrange("p a d -> p (a d)"), gprow, ALU.mult))
                for s in range(TOPK):
                    dve.wait_ge(ld_u[s % RING], (g * 2 + (s // RING + 1)) * 16)
                    dve.tensor_tensor_reduce(junk, Ub[s % RING], XC, 1.0, 0.0, ALU.mult, ALU.add,
                                             act_row[:, s:s + 1]).then_inc(dots, 1)
                    dve.wait_ge(dots, g * TOPK + (s + 1))

            def weights(g, par):
                dve.wait_ge(gelu_done, g + 1)
                lstep(dve.tensor_tensor(wgt[par], gel, gate[par], ALU.mult))
                dve.sem_inc(w_ready, 1)

            def take_sum(g, par):
                dve.wait_ge(v_summed, (g + 1) * TOPK)
                for n in range(2):
                    h = H[:, bass.ds(g // PH, 1), 512 * n:512 * n + 512].rearrange("p a d -> p (a d)")
                    lstep(dve.tensor_tensor(h, ps[2 * par + n][:, :], h, ALU.add))
                dve.sem_inc(acc_taken, 1)

            def group(g, par, topks=True, dot=True, sums=True):
                lstep(dve.tensor_copy(idxv[par], idxu[par]))
                dve.sem_inc(idxv_ready, 1)
                if topks:
                    topk(g + 2, par)
                if dot:
                    dot_products(g + 1, 1 - par)
                    weights(g + 1, 1 - par)
                if topks:
                    gates_of(g + 2, par)
                if sums:
                    take_sum(g + (-1), 1 - par)

            count[1] = 0
            topk(0, 0)
            gates_of(0, 0)
            topk(1, 1)
            gates_of(1, 1)
            dot_products(0, 0)
            weights(0, 0)
            group(0, 0, sums=False)
            group(1, 1)
            ahead = count[0]
            pair = 2 * (1 + TOPK_STEPS + 1 + 1 + 2 + 2)
            count[0] = 0
            with dve.Fori(1, NG // 2 - 1) as i:
                count[1] = (i - 1) * pair + ahead
                group(i * 2, 0)
                group(i * 2 + 1, 1)
                assert count[0] == pair, count
            count[1] = ahead + (NG // 2 - 2) * pair
            count[0] = 0
            group(NG - 2, 0, topks=False)
            group(NG - 1, 1, topks=False, dot=False)
            take_sum(NG - 1, 1)
            normalise(4, H, xn)
            for t in range(NT):
                dve.wait_ge(xn_done, before[4] + t + 1)
                dve.tensor_tensor(xn[:, t, :], xn[:, t, :], gfrow, ALU.mult).then_inc(final_done, 1)


        @block.tensor
        def _(pe):
            def turn(key, pieces):
                b = take(pe, key)
                for dst, src in pieces(b):
                    n = src.shape[0]
                    last = pe.transpose(dst, src, ident[0:n, 0:n])
                last.then_inc(full(key), 1)

            def product(key, groups):
                b = take(pe, key)
                for dst, terms in groups(b):
                    for n, (lhs, rhs) in enumerate(terms):
                        last = pe.matmul(dst, lhs, rhs, start=(n == 0), stop=(n == len(terms) - 1))
                last.then_inc(full(key), 1)

            def columns(t):
                return slice(P * t, P * t + P)

            pe.wait_ge(d_cst, 16)
            pe.wait_ge(d_vec, 16 * 7)
            turn(("vec",), lambda b: [(b[:, 0:NVEC], vecrow[:, :])])
            pe.wait_ge(par_rows, 1)
            turn(("par",), lambda b: [(b[:, G * i:G * i + G], parrow[i]) for i in range(4)])
            pe.wait_ge(d_ssm, 16 * 8)
            for r in range(2):
                turn(("C", r), lambda b: [(b[:, columns(q)], Craw[r][:, q, :]) for q in range(NB)])
            for k in range(KD):
                pe.wait_ge(xn_done, before[1])
                turn(("xT", k), lambda b: [(b[:, columns(t)], xn[:, t, columns(k)]) for t in range(NT)])
            for k in range(KD):
                await_drained(pe, ("xT", k))
            await_slab(pe, ("u", 0))
            await_slab(pe, ("u", 1))
            by_step = [FT[:, k, :].rearrange("p (n q) -> p q n", q=4) for k in range(KD)]
            for q in range(4):
                product(("u", q), lambda b: [
                    (b[:, 256 * n:256 * n + 256],
                     [(by_step[k][:, q, :], slab(("u", n), 8, 256)[:, k, :]) for k in range(KD)])
                    for n in range(2)])
            for q in range(4):
                await_drained(pe, ("u", q))
            for q in range(G // 4):
                turn(("uT", q), lambda b: [
                    (b[0:64, columns(g)], ustage[:, 4 * q + g, :, :].rearrange("p q c -> p (q c)")) for g in range(4)])
            for key, s, at in ((("cq", 0), 0, 0), (("cq", 1), 0, 128), (("cq", 2), 1, 0),
                               (("ckv", 0), 1, 128), (("ckv", 1), 2, 0), (("kr",), 2, 128)):
                await_slab(pe, ("c", s))
                w = slab(("c", s), 8, 256)
                product(key, lambda b: [(b[:, :], [(w[:, k, at:at + 128], FT[:, k, :]) for k in range(KD)])])

            def block_prep(q):
                pe.wait_ge(vb_done, 2 * (q + 1))
                for r in range(2):
                    for s in range(2):
                        turn(("bT", q, r, s), lambda b: [
                            (b[:, columns(g)], VB[r][:, 4 * s + g, :, :].rearrange("p j c -> p (j c)"))
                            for g in range(4)])
                pe.wait_ge(ext_done, 4 * (q + 1))
                pe.wait_ge(pow_done, 1)
                cmat = (Cc[0], negC)
                for s in range(2):
                    product(("D", q, s), lambda b: [
                        (b[:, P * g + CG * j:P * g + CG * j + CG],
                         [(EXT[r][:, 4 * s + g, CH - 1 - j:2 * CH - 1 - j, :].rearrange("p j c -> p (j c)"),
                           cmat[r][:, GB * q + 4 * s + g, :]) for r in range(2)])
                        for g in range(4) for j in range(CH)])

            def chunk_inputs(q):
                for r in range(2):
                    for s in range(2):
                        await_drained(pe, ("bT", q, r, s))
                for r in range(2):
                    product(("X", q, r), lambda b: [
                        (b[:, M * g:M * g + M], [(BT[r][:, g, :], U[:, GB * q + g, :])]) for g in range(GB)])

            block_prep(0)
            for q in range(G // 4):
                await_drained(pe, ("uT", q))
            chunk_inputs(0)
            for q in range(NB):
                if q + 1 < NB:
                    block_prep(q + 1)
                for s in range(2):
                    await_drained(pe, ("D", q, s))
                pe.wait_ge(w_done, q + 1)
                pe.wait_ge(s_done, 4 * (q + 1))
                wre, wim = (Wst[q % 2][r].rearrange("p g j c -> p g (j c)") for r in range(2))
                product(("Y", q), lambda b: [
                    (b[:, M * g:M * g + M], [(DTm[:, g, :], U[:, GB * q + g, :]), (wre[:, g, :], Sst[0][:, g, :]),
                                             (wim[:, g, :], Sst[1][:, g, :])]) for g in range(GB)])
                if q + 1 < NB:
                    chunk_inputs(q + 1)
            pe.wait_ge(yg_done, NB)
            for q in range(G // 4):
                turn(("yt", q), lambda b: [(b[0:M, columns(g)], U[:, 4 * q + g, :]) for g in range(4)])
            for q in range(G // 4):
                await_drained(pe, ("yt", q))
            for f in range(4):
                turn(("yT", f), lambda b: [(b[:, M * j:M * j + M], ytok[:, j, columns(f)]) for j in range(CH)])
            pe.wait_ge(lat_sq, 5)
            pe.wait_ge(ones_set, 1)
            product(("qn",), lambda b: [(b[:, :], [(ones[:, :], latsq[:, m, :]) for m in range(3)])])
            product(("kvn",), lambda b: [(b[:, :], [(ones[:, :], latsq[:, 3 + m, :]) for m in range(2)])])
            pe.wait_ge(lat_done, 5)
            await_slab(pe, ("ukv",))
            ukv = slab(("ukv",), 2, 1024)
            uv = ukv.rearrange("p k (h n) -> p k h n", h=NH)
            for kt in range(NT):
                product(("V", kt), lambda b: [
                    (b[:, :], [(ckvT[:, k, columns(kt)], uv[:, k, :, NOPE:NOPE + HV]) for k in range(2)])])
            pe.wait_ge(d_wuq, 16 * 9)

            def head_in(h):
                product(("Q", h), lambda b: [(b[:, :], [(wuq[:, k, h, :], cqT[:, k, :]) for k in range(3)])])
                product(("K", h), lambda b: [
                    (b[0:NOPE, :], [(ukv[:, k, P * h:P * h + NOPE], ckvT[:, k, :]) for k in range(2)])])

            head_in(0)
            for kt in range(NT):
                await_drained(pe, ("V", kt))
            pe.wait_ge(kr_done, 2)
            for i in range(NH * NT + 2):
                h, qt = divmod(i, NT)
                if i < NH * NT:
                    if qt == 0:
                        pe.wait_ge(qk_done, h + 1)
                        await_drained(pe, ("K", h))
                    product(("S", i), lambda b: [(b[:, :], [(QT[h % 2][0:QD, columns(qt)], KT[h % 2][0:QD, :])])])
                    if qt == 1 and h + 1 < NH:
                        head_in(h + 1)
                if i >= 2:
                    pe.wait_ge(p_done, i - 1)
                    turn(("PT", i - 2), lambda b: [(b[:, columns(k)], Pm[i % 2][:, columns(k)]) for k in range(NT)])
                    if (i - 2) % NT == NT - 1:
                        g = (i - 2) // NT
                        for n in range(NT):
                            await_drained(pe, ("PT", NT * g + n))
                        product(("O", g), lambda b: [
                            (b[0:HV, :], [(V[:, k, HV * g:HV * g + HV], PT[g % 2][:, k, :]) for k in range(NT)])])
            for f in range(4):
                await_drained(pe, ("yT", f))
            for i in range(KD):
                await_slab(pe, ("mix", i))
                w = slab(("mix", i), 4, 3 * P)
                for n, key in enumerate((("val", i), ("gate", i))):
                    product(key, lambda b: [(b[:, :], [(w[:, k, columns(n)], yT[:, k, :]) for k in range(4)])])
                await_slab(pe, ("gates", i))
                wg = slab(("gates", i), 8, 256)
                for n, key in enumerate((("gs", i), ("gm", i))):
                    product(key, lambda b: [(b[:, :], [(wg[:, k, columns(n)], FT[:, k, :]) for k in range(KD)])])
                if i == 0:
                    for h in range(NH):
                        await_drained(pe, ("O", h))
                product(("mla", i), lambda b: [
                    (b[:, :], [(w[:, k, columns(2)], OT[:, k, :]) for k in range(4)])])

            def token_major(kind, src):
                for n in range(4):
                    await_slab(pe, (kind, n))
                    w = slab((kind, n), 8, 256)
                    for p in range(2):
                        product((kind, n, p), lambda b: [
                            (b[:, 256 * t:256 * t + 256],
                             [(src[:, k, columns(2 * p + t)], w[:, k, :]) for k in range(KD)]) for t in range(2)])

            pe.wait_ge(mix_done, KD)
            token_major("out", mixT)
            pe.wait_ge(xn_done, before[2])
            for k in range(KD):
                turn(("mT", k), lambda b: [(b[:, columns(t)], memx[:, t, columns(k)]) for t in range(2)])
            for k in range(KD):
                await_drained(pe, ("mT", k))
            for n in range(4):
                await_slab(pe, ("mk", n))
                w = slab(("mk", n), 8, 256)
                product(("Km", n), lambda b: [
                    (b[:, 256 * m:256 * m + 256], [(w[:, k, columns(m)], memT[:, k, :]) for k in range(KD)])
                    for m in range(2)])
            for n in range(4):
                await_slab(pe, ("mv", n))
                w = slab(("mv", n), 8, 256)
                product(("Vm", n), lambda b: [
                    (b[:, 256 * t:256 * t + 256], [(memT[:, k, columns(t)], w[:, k, :]) for k in range(KD)])
                    for t in range(2)])
            pe.wait_ge(d_key, 16)
            for q in range(4):
                turn(("keyT", q), lambda b: [(b[:, columns(i)], keyraw[:, 4 * q + i, :]) for i in range(4)])
            pe.wait_ge(xn_done, before[3])
            for k in range(KD):
                turn(("hT", k), lambda b: [(b[:, columns(t)], xn[:, t, columns(k)]) for t in range(NT)])
            for k in range(KD):
                await_drained(pe, ("hT", k))
            for m in range(KD):
                await_slab(pe, ("mq", m // 2))
                w = slab(("mq", m // 2), 8, 256)
                product(("Qm", m), lambda b: [
                    (b[:, :], [(w[:, k, columns(m % 2)], FT[:, k, :]) for k in range(KD)])])
            for m in range(KD):
                await_drained(pe, ("Qm", m))
            for n in range(4):
                await_drained(pe, ("Km", n))
                await_drained(pe, ("Vm", n))
            for i in range(MH * NT + 2):
                h, qt = divmod(i, NT)
                if i < MH * NT:
                    product(("Sm", i), lambda b: [
                        (b[:, 0:MT], [(QmT[:, 2 * h + d, columns(qt)], KmT[:, 2 * h + d, :]) for d in range(2)])])
                if i >= 2:
                    pe.wait_ge(mp_done, i - 1)
                    turn(("PTm", i - 2), lambda b: [(b[:, columns(k)], Pmm[i % 2][:, columns(k)]) for k in range(2)])
                    if (i - 2) % NT == NT - 1:
                        g = (i - 2) // NT
                        for n in range(NT):
                            await_drained(pe, ("PTm", NT * g + n))
                        for d in range(2):
                            product(("Om", g, d), lambda b: [
                                (b[:, :], [(Vm[:, k, columns(2 * g + d)], PTm[g % 2][:, k, :]) for k in range(2)])])
            for h in range(MH):
                for d in range(2):
                    await_drained(pe, ("Om", h, d))
            token_major("mo", OmT)
            pe.wait_ge(xn_done, before[4])
            for k in range(KD):
                turn(("pT", k), lambda b: [(b[:, columns(t)], xn[:, t, columns(k)]) for t in range(NT)])
            for k in range(KD):
                await_drained(pe, ("pT", k))

            def queries(s):
                await_slab(pe, ("pq", s // 2))
                w = slab(("pq", s // 2), 8, 256)
                product(("pq", s), lambda b: [
                    (b[:, :], [(w[:, k, columns(s % 2)], FT[:, k, :]) for k in range(KD)])])

            queries(0)
            for q in range(4):
                await_drained(pe, ("keyT", q))
            for s in range(NHS):
                if s + 1 < NHS:
                    queries(s + 1)
                await_drained(pe, ("pq", s))
                product(("ps", s), lambda b: [
                    (b[:, columns(t)], [(qhs[s % 2][:, columns(t)], keysT[:, s, :])]) for t in range(NT)])

            def group(g, par, taken=True):
                if taken:
                    pe.wait_ge(acc_taken, g - 1)
                for s in range(TOPK):
                    pe.wait_ge(ld_v[s % RING], (g * 2 + (s // RING + 1)) * 16)
                    pe.wait_ge(diag_done, g * TOPK + (s + 1))
                    for n in range(2):
                        last = pe.matmul(ps[2 * par + n][:, :], diag[s % 4], Vb[s % RING][:, 512 * n:512 * n + 512],
                                         start=(s == 0), stop=(s == TOPK - 1))
                    last.then_inc(v_summed, 1)

            for b in range(4):
                pe.wait_ge(drained[b], uses[b])
            group(0, 0, taken=False)
            group(1, 1, taken=False)
            with pe.Fori(1, NG // 2) as i:
                group(i * 2, 0)
                group(i * 2 + 1, 1)

        @block.gpsimd
        def _(pool):
            own = [0]

            def step(ins):
                own[0] += 1
                ins.then_inc(c_pool, 1)
                pool.wait_ge(c_pool, own[0])

            def tt(out, a, b, op):
                step(pool.tensor_tensor(out, a, b, op))

            pool.memset(ones[:, :], 1.0).then_inc(ones_set, 1)
            step(pool.memset(mask, 1.0))
            step(pool.memset(mask[0:64, 0:1], 0.0))
            step(pool.memset(mask[64:128, M - 1:M], 0.0))
            for r in range(2):
                step(pool.memset(EXT[r], 0.0))
                step(pool.memset(Sst[r], 0.0))
            pool.sem_inc(zeros_set, 1)
            pool.wait_ge(trig_done, 3)
            one, two = (sm[:, 14, :], sm[:, 15, :]), (sm[:, 66, :], sm[:, 72, :])
            step(pool.tensor_copy(one[0], sm[:, 7, :]))
            step(pool.tensor_copy(one[1], sm[:, 8, :]))
            step(pool.tensor_scalar(one[1][64:128, :], sm[64:128, 8, :], -1.0, None, ALU.mult))

            def square(dst, src):
                t0, t1 = sm[:, 13, :], sm[:, 95, :]
                tt(t0, src[0], src[0], ALU.mult)
                tt(t1, src[1], src[1], ALU.mult)
                tt(dst[0], t0, t1, ALU.subtract)
                tt(t0, src[0], src[1], ALU.mult)
                tt(dst[1], t0, t0, ALU.add)

            square(two, one)
            square(one, two)
            square(two, one)
            levels = [(sm[:, 66 + n, :], sm[:, 72 + n, :]) for n in range(6)]
            for n in range(5):
                square(levels[n + 1], levels[n])
            await_full(pool, ("xT", KD - 1))
            step(pool.memset(Tre[:, :, 0:1], 1.0))
            step(pool.memset(Tim[:, :, 0:1], 0.0))
            for n in range(6):
                w = 1 << n
                tmp = [Hf[:, 1024 * i:1024 * i + G * w].rearrange("p (g m) -> p g m", g=G) for i in range(2)]
                lr, li = (levels[n][r].unsqueeze(2).to_broadcast([P, G, w]) for r in range(2))
                tr, tim = Tre[:, :, 0:w], Tim[:, :, 0:w]
                tt(tmp[0], tr, lr, ALU.mult)
                tt(tmp[1], tim, li, ALU.mult)
                tt(Tre[:, :, w:2 * w], tmp[0], tmp[1], ALU.subtract)
                tt(tmp[0], tr, li, ALU.mult)
                tt(tmp[1], tim, lr, ALU.mult)
                tt(Tim[:, :, w:2 * w], tmp[0], tmp[1], ALU.add)
            pool.sem_inc(table_done, 1)
            pool.wait_ge(pow_done, 1)
            await_full(pool, ("uT", G // 4 - 1))
            tmp = XN[:, 0:1024].rearrange("p (g j c) -> p g j c", g=GB, j=CH)
            for q in range(NB):
                gs = slice(GB * q, GB * q + GB)
                if q >= 2:
                    await_full(pool, ("Y", q - 2))
                pr, pi = (sm[:, 50 + 8 * r:58 + 8 * r, gs].rearrange("p k g -> p g k").unsqueeze(3)
                          .to_broadcast([P, GB, CH, CG]) for r in range(2))
                cr, ci = (c[:, gs, :].unsqueeze(2).to_broadcast([P, GB, CH, CG]) for c in (Cc[0], negC))
                wre, wim = Wst[q % 2]
                tt(wre, pr, cr, ALU.mult)
                tt(tmp, pi, ci, ALU.mult)
                tt(wre, wre, tmp, ALU.add)
                tt(wim, pr, ci, ALU.mult)
                tt(tmp, pi, cr, ALU.mult)
                tt(wim, wim, tmp, ALU.subtract)
                pool.sem_inc(w_done, 1)

            def gather(dst, table, ix, s, signal):
                pool.sem_inc(apart_pool, 1)
                pool.indirect_dma_start(out=dst, out_offset=None, in_=table,
                                        in_offset=bass.IndirectOffsetOnAxis(ap=ix[:, s:s + 1], axis=0)).then_inc(signal, 16)

            def u_row(g, par, s):
                if not isinstance(g, int) or g * TOPK + s >= RING:
                    pool.wait_ge(dots, g * TOPK + (s - (RING - 1)))
                gather(Ub[s % RING], peer_u, idxu[par], s, ld_u[s % RING])

            def v_row(g, par, s):
                if not isinstance(g, int) or g * TOPK + s >= RING:
                    pool.wait_ge(v_summed, g * TOPK + (s - (RING - 1)))
                gather(Vb[s % RING], peer_v, idxv[par], s, ld_v[s % RING])

            await_full(pool, ("pq", NHS - 1))
            await_full(pool, ("ps", NHS - 1))
            pool.wait_ge(idxu_ready, 1)
            for s in range(TOPK):
                u_row(0, 0, s)

            def group(g, par, more=True):
                if more:
                    pool.wait_ge(idxu_ready, g + 2)
                pool.wait_ge(idxv_ready, g + 1)
                for s in range(TOPK):
                    if more:
                        u_row(g + 1, 1 - par, s)
                    v_row(g, par, s)

            group(0, 0)
            group(1, 1)
            with pool.Fori(1, NG // 2 - 1) as i:
                group(i * 2, 0)
                group(i * 2 + 1, 1)
            group(NG - 2, 0)
            group(NG - 1, 1, more=False)


NAMES = ["x", "mem", "positions", "g_mix", "w_in", "b_gate", "ssm_lam_re", "ssm_lam_im", "ssm_log_dt",
         "ssm_b_re", "ssm_b_im", "ssm_c_re", "ssm_c_im", "ssm_d", "w_ssm_glu", "g_q_lora", "w_uq",
         "g_kv_lora", "w_ukv", "w_mla_o", "w_out", "g_mem_q", "g_mem_kv", "w_mem_q", "w_mem_kv",
         "w_mem_o", "g_peer", "w_peer_q", "peer_sub_keys", "peer_u", "peer_v", "g_final"]
WEIGHTS = {"w_in", "w_ssm_glu", "w_uq", "w_ukv", "w_mla_o", "w_out", "w_mem_q", "w_mem_kv", "w_mem_o",
           "w_peer_q", "peer_u", "peer_v"}


def kernel(**inputs):
    import concourse.bacc as bacc
    from concourse.bass_utils import run_bass_kernel_spmd

    nc = bacc.Bacc("TRN2", target_bir_lowering=False, num_devices=1)
    arrays = {n: np.ascontiguousarray(inputs[n]) for n in NAMES}
    for n in WEIGHTS:
        arrays[n] = arrays[n].reshape(arrays[n].shape[1:])
    arrays["consts"] = host_constants()
    args = [nc.dram_tensor(f"in_{n}", a.shape, mybir.dt.from_np(a.dtype), kind="ExternalInput").ap()
            for n, a in arrays.items()]
    out = nc.dram_tensor("out_0", (1, T, D), F32, kind="ExternalOutput").ap()
    encoder_layer(nc, *args, out)
    r = run_bass_kernel_spmd(nc, [{f"in_{n}": a for n, a in arrays.items()}], core_ids=[0])
    return r.results[0]["out_0"]
```

```python
import math
from contextlib import ExitStack

import numpy as np

import concourse.bass as bass
import concourse.mybir as mybir

F32 = mybir.dt.float32
I32 = mybir.dt.int32
U32 = mybir.dt.uint32
ALU = mybir.AluOpType
ACT = mybir.ActivationFunctionType
AX = mybir.AxisListType

P = 128
T, D = 512, 1024
NT, KD = T // P, D // P
EPS = 1e-6
SW, G, CG, NS = 512, 32, 16, 64
CH = P // CG
M = T // CH
LAGS = 2 * CH - 1
GB = 8
NB = G // GB
NH, NOPE, ROPE, HV = 8, 64, 32, 64
QL, KVL = 384, 256
QD = NOPE + ROPE
MT, MH, MD = 256, 4, 256
PH, NK, KH, TOPK = 8, 128, 128, 16
NHS = 2 * PH
NG = NT * PH

VEC = {}
_at = 0
for _n, _w in (("g_mix", 8), ("g_mem_q", 8), ("g_mem_kv", 8), ("g_peer", 8), ("b_gate", 16),
               ("g_q_lora", 3), ("g_kv_lora", 2)):
    VEC[_n] = (_at, _w)
    _at += _w
NVEC = _at

C_ID, C_IOTA, C_ROPE = 0, P, P + 16
NCONST = C_ROPE + 4

NEG = -3.0e38
TWO_PI = 2 * math.pi
PI_HI = 6.28125
PI_MID = round((TWO_PI - PI_HI) * 2 ** 20) / 2 ** 20
PI_LO = TWO_PI - PI_HI - PI_MID
ROUND = 1.5 * 2 ** 23
PI_CLAMP = 3.1415925
SLOTS = 5
TOPK_STEPS = 25
SLAB = 2048
URING, VRING = 8, TOPK
DRING = 8


def host_constants():
    c = np.zeros((P, NCONST), np.float32)
    c[:, C_ID:C_ID + P] = np.eye(P, dtype=np.float32)
    c[:, C_IOTA:C_IOTA + 16] = np.arange(16, dtype=np.float32)
    freq = 1.0 / (np.float32(10000.0) ** (np.arange(0, ROPE, 2, dtype=np.float32) / np.float32(ROPE)))
    c[:, C_ROPE] = freq.astype(np.float32)[np.arange(P) % 16]
    cos_rows = slice(64, 96)
    c[cos_rows, C_ROPE + 1] = 0.25
    c[cos_rows, C_ROPE + 2] = math.pi / 2
    c[:, C_ROPE + 3] = 1.0
    c[96:112, C_ROPE + 3] = -1.0
    return c


LATENT_JOBS = [(("cq", 0), 0, 0), (("cq", 1), 0, 128), (("cq", 2), 1, 0),
               (("ckv", 0), 1, 128), (("ckv", 1), 2, 0), (("kr",), 2, 128)]


def psum_jobs():
    j = [("vec",), ("par",)]
    j += [("xT", k) for k in range(KD)] + [("C", 0), ("C", 1)]
    j += [("u", q) for q in range(4)]
    j += [("uT", q) for q in range(G // 4)]

    def prep(b):
        return [("bT", b, r, s) for r in range(2) for s in range(2)] + [("D", b, s) for s in range(NB)]

    j += prep(0) + [("X", 0, 0), ("X", 0, 1)]
    for b in range(NB):
        if b + 1 < NB:
            j += [key for key, _, _ in LATENT_JOBS[2 * b:2 * b + 2]] + prep(b + 1)
        else:
            j += [("kvn",), ("qn",)]
        j += [("Y", b)]
        if b + 1 < NB:
            j += [("X", b + 1, 0), ("X", b + 1, 1)]
    j += [("yt", q) for q in range(G // 4)] + [("yT", f) for f in range(4)]
    j += [("V", kt) for kt in range(NT)] + [("Q", 0), ("K", 0)]
    for i in range(NH * NT + 3):
        h, qt = divmod(i, NT)
        if i < NH * NT:
            j.append(("S", i))
            if qt == 1 and h + 1 < NH:
                j += [("Q", h + 1), ("K", h + 1)]
        if 2 <= i < NH * NT + 2:
            j.append(("PT", i - 2))
        if i >= 3 and (i - 3) % NT == NT - 1:
            j.append(("O", (i - 3) // NT))
    for i in range(KD):
        j += [("val", i), ("gate", i), ("gs", i), ("gm", i), ("mla", i)]
    j += [("mT", k) for k in range(KD)] + [("Km", m) for m in range(4)]
    j += [("out", n, p) for p in range(2) for n in range(4)]
    j += [("Vm", n) for n in range(4)] + [("keyT", q) for q in range(4)]
    j += [("hT", k) for k in range(KD)] + [("Qm", m) for m in range(KD)]
    for i in range(MH * NT + 3):
        if i < MH * NT:
            j.append(("Sm", i))
        if 2 <= i < MH * NT + 2:
            j.append(("PTm", i - 2))
        if i >= 3 and (i - 3) % NT == NT - 1:
            j += [("Om", (i - 3) // NT, d) for d in range(2)]
    j += [("mo", n, p) for p in range(2) for n in range(4)]
    j += [("pT", k) for k in range(KD)]
    return j


def slab_plan():
    s = [(("u", 0), ("u", 3)), (("u", 1), ("u", 3)),
         (("c", 0), ("cq", 1)), (("c", 1), ("ckv", 0)), (("c", 2), ("kr",)),
         (("ukv",), ("K", NH - 1))]
    for i in range(KD):
        s.append((("mix", i), ("mla", i)))
        s.append((("gates", i), ("gm", i)))
    s += [(("mk", n), ("Km", n)) for n in range(4)]
    s += [(("out", n), ("out", n, 1)) for n in range(4)]
    s += [(("mv", n), ("Vm", n)) for n in range(4)]
    s += [(("mq", n), ("Qm", 2 * n + 1)) for n in range(4)]
    s += [(("mo", n), ("mo", n, 1)) for n in range(4)]
    s.append((("pq", 0), ("pT", KD - 1)))
    return s


def rows(w, lo, hi):
    return w[:, lo:hi].rearrange("(k p) n -> p k n", p=P)


def encoder_layer(nc, x, mem, positions, g_mix, w_in, b_gate, ssm_lam_re, ssm_lam_im, ssm_log_dt,
                  ssm_b_re, ssm_b_im, ssm_c_re, ssm_c_im, ssm_d, w_ssm_glu, g_q_lora, w_uq,
                  g_kv_lora, w_ukv, w_mla_o, w_out, g_mem_q, g_mem_kv, w_mem_q, w_mem_kv, w_mem_o,
                  g_peer, w_peer_q, peer_sub_keys, peer_u, peer_v, g_final, consts, out):
    ctx = ExitStack()
    with ctx:
        def sb(name, *shape, dt=F32):
            return ctx.enter_context(nc.sbuf_tensor(name, list(shape), dt))

        def sem(name):
            return ctx.enter_context(nc.semaphore(name))

        cst = sb("cst", P, NCONST)
        ident = cst[:, C_ID:C_ID + P]
        iota16 = cst[:, C_IOTA:C_IOTA + 16]
        ones = sb("ones", P, P)
        vecrow = sb("vecrow", NVEC, P)
        vec = sb("vec", P, NVEC)
        stat = sb("stat", P, 104)
        H = sb("H", P, NT, D)
        XN = sb("XN", P, NT * D)
        FT = sb("FT", P, KD, T)
        slabs = sb("slabs", P, SLOTS * SLAB)
        R = sb("R", P, 28416)
        xn = XN[:, :].rearrange("p (t d) -> p t d", t=NT)

        def reg(lo, *shape, base=R, parts=P):
            n = int(np.prod(shape))
            v = base[0:parts, lo:lo + n]
            names = "abcd"[:len(shape)]
            if len(shape) > 1:
                v = v.rearrange(f"p ({' '.join(names)}) -> p {' '.join(names)}",
                                **dict(zip(names, shape)))
            return v

        Hf = H[:, :, :].rearrange("p t d -> p (t d)")
        U = reg(0, G, M)
        cqT, ckvT = reg(2048, 3, T), reg(3584, 2, T)
        VB = [reg(4608, GB, CH, CG), reg(5632, GB, CH, CG)]
        bb = [reg(6656, G, CG), reg(7168, G, CG)]
        Cc = [reg(7680, G, CG), reg(8192, G, CG)]
        EXT = [reg(8704, GB, LAGS, CG), reg(10624, GB, LAGS, CG)]
        Wtmp = reg(27456, NB, CH, CG)
        BT = [reg(12544, GB, P), reg(13568, GB, P)]
        DTm = reg(14592, GB, P)
        t4 = [reg(16640 + 512 * i, GB * M) for i in range(4)]
        ta, tb = reg(16640, GB, CH, CG), reg(17664, GB, CH, CG)
        Z = [reg(18688, GB * M), reg(19200, GB * M)]
        Zs = [reg(15616, GB * M), reg(16128, GB * M)]
        Sst = [reg(19712, GB, M), reg(20224, GB, M)]
        M8 = reg(20736, GB, M)
        Tim = reg(21248, G, M)
        Craw = [reg(18688, NB, P), reg(19200, NB, P)]
        sm = reg(23296, 96, G)
        krT = reg(26368, T)
        mask = reg(26880, M)
        negC = reg(26944, G, CG)
        parrow = [reg(27456 + 128 * i, P, parts=G) for i in range(4)]
        drow = reg(27968, P, parts=G)
        dtrow = reg(28096, 2, parts=G)
        Wst = [[Hf[:, 2048 * q + 1024 * r:2048 * q + 1024 * (r + 1)].rearrange(
            "p (g j c) -> p g j c", g=GB, j=CH) for r in range(2)] for q in range(2)]
        ustage = XN[:, 0:2048].rearrange("p (g q c) -> p g q c", g=G, q=4)
        lags = XN[0:CG, 0:GB * LAGS * CG].rearrange("p (g l c) -> p g l c", g=GB, l=LAGS)
        ytok = XN[0:M, :].rearrange("p (j n) -> p j n", j=CH)
        Tre = XN[:, 2048:4096].rearrange("p (g m) -> p g m", g=G)
        yT = reg(0, 4, T)
        wuq = reg(4608, 3, NH, P)
        V = reg(7680, NT, NH * HV)
        OT = reg(9728, 4, T)
        posb = reg(11776, T).bitcast(I32)
        TAB = reg(12288, T)
        tA, tB, tC = reg(12800, T), reg(13312, T), reg(13824, T)
        QT = [reg(14336, T), reg(14848, T)]
        KT = [reg(15360, T), reg(15872, T)]
        Pm = [reg(16384, T), reg(16896, T)]
        PT = [reg(17408, NT, T), reg(19456, NT, T)]
        lat = [reg(21504, T), reg(22016, T)]
        latsq = slabs[:, 2 * SLAB:2 * SLAB + 5 * T].rearrange("p (k t) -> p k t", k=5)
        mixtmp = [[reg(21504 + 512 * (5 * q + i), T) for i in range(5)] for q in range(2)]
        mixT = reg(12288, KD, T)
        memx, memT = reg(4608, 2, D), reg(6656, KD, MT)
        KmT, Vm = reg(2048, KD, MT), reg(0, 2, D)
        QmT = reg(8192, KD, T)
        OmT = reg(12288, KD, T)
        Pmm = [reg(16384, MT), reg(16640, MT)]
        PTm = [reg(16896, 2, T), reg(17920, 2, T)]
        keyraw = reg(18944, NHS, KH)
        keysT = reg(20992, NHS, NK)
        qhs = [reg(0, T), reg(512, T)]
        SC = reg(1024, NT, 2, NK)
        Vb = [reg(3072 + D * i, D) for i in range(VRING)]
        diag = [reg(19456 + P * i, P) for i in range(DRING)]
        gprow = reg(23040, D)
        gfrow = reg(24064, D)
        prod = reg(25088, D)
        sc1, cand1 = reg(26112, NK), reg(26368, TOPK * TOPK)
        cand = reg(26624, TOPK * TOPK)
        eq = reg(26880, 2 * TOPK, TOPK)
        tv = reg(27392, 2, TOPK)
        ti = reg(27424, 2, TOPK).bitcast(U32)
        tif = reg(27456, 2, TOPK)
        cv = reg(27488, TOPK)
        cpos = reg(27504, TOPK).bitcast(U32)
        cpp = reg(27520, 2 * TOPK).bitcast(U32)
        cpf = reg(27552, 2 * TOPK)
        isel = reg(27584, 2 * TOPK)
        nmx, esum, rinv = reg(27616, 1), reg(27617, 1), reg(27618, 1)
        ex = reg(27632, TOPK)
        idx = [reg(27648 + TOPK * i, TOPK).bitcast(U32) for i in range(NT)]
        gate = [reg(27712 + TOPK * i, TOPK) for i in range(2)]
        wgt = [reg(27744 + TOPK * i, TOPK) for i in range(2)]
        act_row = reg(27776, TOPK)
        gel = reg(27792, TOPK)
        junk = reg(17408, D)

        ps = [ctx.enter_context(nc.psum_tensor(f"bank{i}", [P, 512], F32)) for i in range(8)]

        filled = [sem(f"filled{i}") for i in range(8)]
        drained = [sem(f"drained{i}") for i in range(8)]
        slab_in = [sem(f"slab_in{i}") for i in range(SLOTS)]
        ld_u = [sem(f"ld_u{i}") for i in range(URING)]
        ld_v = [sem(f"ld_v{i}") for i in range(VRING)]
        d_cst, d_vec, d_par, d_x, d_ssm = [sem(n) for n in ("d_cst", "d_vec", "d_par", "d_x", "d_ssm")]
        d_res, d_wuq, d_pos, d_mem, d_key = [sem(n) for n in ("d_res", "d_wuq", "d_pos", "d_mem", "d_key")]
        d_grow, d_out, d_within = sem("d_grow"), sem("d_out"), sem("d_within")
        c_dve, c_act, c_pool, c_loop = [sem(n) for n in ("c_dve", "c_act", "c_pool", "c_loop")]
        sq_done, var_done, std_done, xn_done = [sem(n) for n in ("sq_done", "var_done", "std_done", "xn_done")]
        ones_set, zeros_set, par_rows = [sem(n) for n in ("ones_set", "zeros_set", "par_rows")]
        args_done, trig_done, bb_done, table_done = [sem(n) for n in ("args_done", "trig_done", "bb_done", "table_done")]
        vb_done, ext_done, w_done, s_done, yg_done, pow_done = [
            sem(n) for n in ("vb_done", "ext_done", "w_done", "s_done", "yg_done", "pow_done")]
        lat_sq, lat_var, lat_std, lat_done = [sem(n) for n in ("lat_sq", "lat_var", "lat_std", "lat_done")]
        rope_arg, rope_sin, kr_done, qk_done = [sem(n) for n in ("rope_arg", "rope_sin", "kr_done", "qk_done")]
        negmax, p_done = sem("negmax"), sem("p_done")
        sig_done, mix_done = sem("sig_done"), sem("mix_done")
        mnegmax, mp_done = sem("mnegmax"), sem("mp_done")
        qw_in, q_filled, q_copied, s_filled, s_copied = [
            sem(n) for n in ("qw_in", "q_filled", "q_copied", "s_filled", "s_copied")]
        idx_ready, gates_neg, gates_exp = [sem(n) for n in ("idx_ready", "gates_neg", "gates_exp")]
        dots, gelu_done, w_ready, diag_done, v_summed = [
            sem(n) for n in ("dots", "gelu_done", "w_ready", "diag_done", "v_summed")]
        acc_taken, final_done = sem("acc_taken"), sem("final_done")
        apart_dve, apart_pool = sem("apart_dve"), sem("apart_pool")

        jobs = psum_jobs()
        place = {k: (i % 8, i // 8) for i, k in enumerate(jobs)}
        assert len(place) == len(jobs)
        uses = [sum(1 for i in range(len(jobs)) if i % 8 == b) for b in range(8)]

        def take(pe, key):
            b, n = place[key]
            if n:
                pe.wait_ge(drained[b], n)
            return ps[b]

        def full(key):
            return filled[place[key][0]]

        def await_full(eng, key):
            b, n = place[key]
            eng.wait_ge(filled[b], n + 1)
            return ps[b]

        def empty(key):
            return drained[place[key][0]]

        def await_drained(eng, key):
            b, n = place[key]
            eng.wait_ge(drained[b], n + 1)

        plan = slab_plan()
        slab_no = {k: i for i, (k, _) in enumerate(plan)}

        def slab(key, *shape):
            s = (slab_no[key] % SLOTS) * SLAB
            n = int(np.prod(shape))
            return slabs[:, s:s + n].rearrange("p (k n) -> p k n", k=shape[0])

        def slab_parts(key):
            kind = key[0]
            if kind == "u":
                return [(slab(key, 8, 256), rows(w_in, 256 * key[1], 256 * key[1] + 256))]
            if kind == "c" and key[1] < 2:
                lo = SW + 256 * key[1]
                return [(slab(key, 8, 256), rows(w_in, lo, lo + 256))]
            if kind == "c":
                lo = SW + 512
                kr = lo + 128
                s = slab(key, 8, 256)
                parts = [(s[:, :, 0:128], rows(w_in, lo, lo + 128))]
                for i in range(2):
                    at = 128 + 64 * i
                    parts += [(s[:, :, at:at + 32], rows(w_in, kr, kr + 32)),
                              (s[:, :, at + 32:at + 48], rows(w_in, kr + 16, kr + 32)),
                              (s[:, :, at + 48:at + 64], rows(w_in, kr, kr + 16))]
                return parts
            if kind == "ukv":
                return [(slab(key, 2, 1024), rows(w_ukv, 0, 1024))]
            if kind == "mix":
                lo = P * key[1]
                s = slab(key, 4, 3 * P)
                return [(s[:, :, 0:P], rows(w_ssm_glu, lo, lo + P)),
                        (s[:, :, P:2 * P], rows(w_ssm_glu, D + lo, D + lo + P)),
                        (s[:, :, 2 * P:3 * P], rows(w_mla_o, lo, lo + P))]
            if kind == "gates":
                lo = SW + QL + KVL + ROPE + 128 * key[1]
                s = slab(key, 8, 256)
                return [(s[:, :, 0:128], rows(w_in, lo, lo + 128)),
                        (s[:, :, 128:256], rows(w_in, lo + D, lo + D + 128))]
            w, lo = {"out": (w_out, 0), "mk": (w_mem_kv, 0), "mv": (w_mem_kv, D), "mq": (w_mem_q, 0),
                     "mo": (w_mem_o, 0), "pq": (w_peer_q, 0)}[kind]
            lo += 256 * key[1]
            return [(slab(key, 8, 256), rows(w, lo, lo + 256))]

        slab_need, had = [], [0] * SLOTS
        for n, (key, _) in enumerate(plan):
            had[n % SLOTS] += 16 * len(slab_parts(key))
            slab_need.append(had[n % SLOTS])

        def await_slab(pe, key):
            n = slab_no[key]
            pe.wait_ge(slab_in[n % SLOTS], slab_need[n])

        qw = slab(("pq", 0), 8, 256)
        Ub = [slabs[:, D * i:D * i + D] for i in range(2 * SLOTS)
              if i // 2 != slab_no[("pq", 0)] % SLOTS][:URING]

        block = ctx.enter_context(nc.Block())

        @block.sync
        def _(sp):
            sp.dma_start(cst[:, :], consts).then_inc(d_cst, 16)
            sp.dma_start(xn, x[0].rearrange("(t p) d -> p t d", p=P)).then_inc(d_x, 16)
            for name, w in (("g_mix", g_mix), ("g_mem_q", g_mem_q), ("g_mem_kv", g_mem_kv),
                            ("g_peer", g_peer), ("b_gate", b_gate), ("g_q_lora", g_q_lora),
                            ("g_kv_lora", g_kv_lora)):
                lo, n = VEC[name]
                sp.dma_start(vecrow[lo:lo + n, :], w[0].rearrange("(k p) -> k p", p=P)).then_inc(d_vec, 16)
            for i, w in enumerate((ssm_lam_re, ssm_lam_im)):
                sp.dma_start(parrow[i].rearrange("g (d p) -> g d p", d=2),
                             w[0].rearrange("d g p -> g d p")).then_inc(d_par, 16)
            sp.dma_start(dtrow, ssm_log_dt[0].rearrange("d g -> g d"), allow_slow_non_contiguous=True).then_inc(d_par, 16)
            sp.dma_start(drow[:, 0:CG], ssm_d[0].rearrange("(g c) -> g c", g=G)).then_inc(d_par, 16)

            def load_slab(n):
                key = plan[n][0]
                if n >= SLOTS:
                    b, k = place[plan[n - SLOTS][1]]
                    sp.wait_ge(filled[b], k + 1)
                for dst, src in slab_parts(key):
                    sp.dma_start(dst, src).then_inc(slab_in[n % SLOTS], 16)

            for n in range(SLOTS):
                load_slab(n)
            load_slab(SLOTS)
            for q in range(NB):
                await_drained(sp, ("D", q, NB - 1))
                if q:
                    await_full(sp, ("Y", q - 1))
                for s in range(CH):
                    sp.dma_start(DTm[CG * s:CG * s + CG, :, :],
                                 lags[:, :, CH - 1 - s:2 * CH - 1 - s, :].rearrange("p g l c -> p g (l c)")
                                 ).then_inc(d_within, 16)
            await_full(sp, ("Y", NB - 1))
            for k in range(3):
                src = w_uq[P * k:P * k + P, :].rearrange("p (h n) -> p h n", h=NH)
                sp.dma_start(wuq[:, k, :, 0:QD], src).then_inc(d_wuq, 16)
                sp.dma_start(wuq[:, k, :, QD:QD + 16], src[:, :, NOPE + 16:QD]).then_inc(d_wuq, 16)
                sp.dma_start(wuq[:, k, :, QD + 16:P], src[:, :, NOPE:NOPE + 16]).then_inc(d_wuq, 16)
            sp.dma_start(posb, positions[0].partition_broadcast(P)).then_inc(d_pos, 16)
            sp.dma_start(H[:, :, :], x[0].rearrange("(t p) d -> p t d", p=P)).then_inc(d_res, 16)
            for n in range(SLOTS + 1, len(plan)):
                if plan[n][0] == ("gates", 0):
                    await_full(sp, ("Q", NH - 1))
                    sp.dma_start(memx, mem[0].rearrange("(t p) d -> p t d", p=P)).then_inc(d_mem, 16)
                if plan[n][0] == ("mix", 1):
                    await_full(sp, ("O", NH - 1))
                    sp.dma_start(keyraw, peer_sub_keys[0].rearrange("h s n d -> n (h s) d")).then_inc(d_key, 16)
                if plan[n][0] == ("mq", 0):
                    sp.wait_ge(mix_done, KD)
                    sp.dma_start(gprow, g_peer[0].partition_broadcast(P)).then_inc(d_grow, 16)
                    sp.dma_start(gfrow, g_final.partition_broadcast(P)).then_inc(d_grow, 16)
                load_slab(n)
            with sp.Fori(1, PH) as h:
                sp.wait_ge(q_filled, h * 2)
                sp.dma_start(qw, w_peer_q[:, bass.ds(h * 256, 256)].rearrange("(k p) n -> p k n", p=P)).then_inc(qw_in, 16)
            for t in range(NT):
                sp.wait_ge(final_done, t + 1)
                sp.dma_start(out[0, P * t:P * t + P, :], xn[:, t, :]).then_inc(d_out, 16)
            sp.wait_ge(d_out, 16 * NT)


        NORMS = (NT, 2, NT, NT, NT)
        before = [sum(NORMS[:k]) for k in range(6)]
        PARTS = [(0, (0, 1, 2, 3)), (1, (0, 1)), (2, (0, 1)), (2, (2, 3)), (3, (0, 1)), (3, (2, 3))]

        def sumsq(k, t):
            return stat[:, 16 * k + t:16 * k + t + 1]

        @block.scalar
        def _(act):
            own = [0]

            def settle(ins):
                own[0] += 1
                ins.then_inc(c_act, 1)
                act.wait_ge(c_act, own[0])

            def copy_out(key, dst, src, scale=1.0):
                act.activation(dst, src, ACT.Copy, scale=scale).then_inc(empty(key), 1)

            def squares(part, src, scratch, kind=None):
                k, tiles = PARTS[part]
                for t in tiles:
                    if kind:
                        for n in range(4):
                            await_drained(act, (kind, n, t // 2))
                    settle(act.activation(scratch, src[:, t, :], ACT.Square, accum_out=sumsq(k, t)))
                act.sem_inc(sq_done, 1)
                act.wait_ge(var_done, part + 1)
                lo, hi = 16 * k + tiles[0], 16 * k + tiles[-1] + 1
                act.activation(stat[:, 8 + lo:8 + hi], stat[:, 4 + lo:4 + hi], ACT.Sqrt).then_inc(std_done, 1)

            def features(name, key, dst, width):
                for k in range(KD):
                    b = await_full(act, (key, k))
                    c = VEC[name][0] + k
                    copy_out((key, k), dst[:, k, :], b[:, 0:width], scale=vec[:, c:c + 1])

            act.wait_ge(d_par, 64)
            settle(act.activation(dtrow, dtrow, ACT.Exp))
            for d in range(2):
                settle(act.activation(parrow[2][:, 64 * d:64 * d + 64],
                                      dtrow[:, d:d + 1].to_broadcast([G, 64]), ACT.Copy))
            act.activation(parrow[3].rearrange("g (j c) -> g j c", j=CH),
                           drow[:, 0:CG].unsqueeze(1).to_broadcast([G, CH, CG]), ACT.Copy).then_inc(par_rows, 1)
            act.wait_ge(d_x, 16)
            squares(0, xn, FT[:, 0:2, :].rearrange("p k t -> p (k t)"))
            act.wait_ge(args_done, 1)
            act.activation(sm[:, 6, :], sm[:, 4, :], ACT.Exp).then_inc(trig_done, 1)
            act.activation(sm[:, 12, :], sm[:, 4, :], ACT.Exp, scale=float(CH)).then_inc(trig_done, 1)
            act.activation(sm[:, 7:9, :], sm[:, 10:12, :], ACT.Sin).then_inc(trig_done, 1)
            await_drained(act, ("vec",))
            features("g_mix", "xT", FT, T)
            for r in range(2):
                b = await_full(act, ("C", r))
                copy_out(("C", r), Cc[r].rearrange("p g c -> p (g c)"), b[:, :])
            for q in range(4):
                b = await_full(act, ("u", q))
                copy_out(("u", q), ustage[:, :, q, :], b[:, :].rearrange("p (g c) -> p g c", g=G))
            for q in range(G // 4):
                b = await_full(act, ("uT", q))
                src = b[0:64, :].rearrange("p (g m j) -> p g j m", g=4, j=2)
                settle(act.activation(U[0:64, 4 * q:4 * q + 4, :], src[:, :, 0, :], ACT.Copy))
                copy_out(("uT", q), U[64:128, 4 * q:4 * q + 4, :], src[:, :, 1, :])
            def latent(key):
                dst = krT if key == ("kr",) else (cqT if key[0] == "cq" else ckvT)[:, key[1], :]
                b = await_full(act, key)
                copy_out(key, dst, b[:, :])

            def block_prep(q):
                act.wait_ge(w_done, q + 1)
                act.wait_ge(zeros_set, 1)
                if q:
                    await_full(act, ("D", q - 1, NB - 1))
                for r, c in enumerate((Cc[0], negC)):
                    w = Wst[q % 2][r]
                    act.activation(EXT[r][:, :, CH - 1, :], c[:, GB * q:GB * q + GB, :], ACT.Copy).then_inc(ext_done, 1)
                    act.activation(EXT[r][0:64, :, CH:, :].rearrange("p g j c -> p g (j c)"),
                                   w[0:64, :, 0:CH - 1, :].rearrange("p g j c -> p g (j c)"), ACT.Copy).then_inc(ext_done, 1)
                    act.activation(EXT[r][64:128, :, 0:CH - 1, :].rearrange("p g j c -> p g (j c)"),
                                   w[64:128, :, 1:, :].rearrange("p g j c -> p g (j c)"), ACT.Copy).then_inc(ext_done, 1)
                if q:
                    await_full(act, ("X", q - 1, 1))
                for r in range(2):
                    for s in range(2):
                        b = await_full(act, ("bT", q, r, s))
                        copy_out(("bT", q, r, s), BT[r][:, 4 * s:4 * s + 4, :].rearrange("p g n -> p (g n)"), b[:, :])
                if q:
                    act.wait_ge(d_within, 16 * CH * q)
                for s in range(NB):
                    b = await_full(act, ("D", q, s))
                    copy_out(("D", q, s), lags[:, 2 * s:2 * s + 2, :, :].rearrange("p g l c -> p (g l c)"),
                             b[0:CG, 0:2 * LAGS * CG])

            block_prep(0)
            for q in range(NB):
                if q + 1 < NB:
                    for key, _, _ in LATENT_JOBS[2 * q:2 * q + 2]:
                        latent(key)
                    block_prep(q + 1)
                else:
                    for m in range(3):
                        act.activation(latsq[:, m, :], cqT[:, m, :], ACT.Square).then_inc(lat_sq, 1)
                    for m in range(2):
                        act.activation(latsq[:, 3 + m, :], ckvT[:, m, :], ACT.Square).then_inc(lat_sq, 1)
                await_drained(act, ("Y", q))
                yq = U[:, GB * q:GB * q + GB, :]
                act.activation(yq, yq, ACT.Gelu_apprx_tanh).then_inc(yg_done, 1)
            act.wait_ge(s_done, 4 * NB)
            for q in range(G // 4):
                b = await_full(act, ("yt", q))
                for g in range(4):
                    ins = act.activation(ytok[:, :, 64 * q + 16 * g:64 * q + 16 * g + 16],
                                         b[0:M, P * g:P * g + P].rearrange("p (j c) -> p j c", j=CH), ACT.Copy)
                ins.then_inc(empty(("yt", q)), 1)
            for f in range(4):
                b = await_full(act, ("yT", f))
                copy_out(("yT", f), yT[:, f, :].rearrange("p (m j) -> p j m", j=CH),
                         b[:, :].rearrange("p (j m) -> p j m", j=CH))
            for k in range(2):
                act.wait_ge(lat_var, k + 1)
                act.activation(lat[k], lat[k], ACT.Sqrt).then_inc(lat_std, 1)
            act.wait_ge(rope_arg, 1)
            act.activation(TAB, tA, ACT.Sin).then_inc(rope_sin, 1)
            for kt in range(NT):
                b = await_full(act, ("V", kt))
                copy_out(("V", kt), V[:, kt, :], b[:, :])

            def head_in(h):
                b = await_full(act, ("Q", h))
                if h >= 2:
                    await_full(act, ("S", NT * (h - 1) - 1))
                copy_out(("Q", h), QT[h % 2], b[:, :])
                b = await_full(act, ("K", h))
                copy_out(("K", h), KT[h % 2][0:64, :], b[0:64, :])

            def exponentials(i, key, width, bufs, negs, scale, base, tkey):
                b = await_full(act, (key, i))
                act.wait_ge(negs, i + 1)
                if i >= 2:
                    await_full(act, (tkey, i - 2))
                act.activation(bufs[i % 2], b[:, 0:width], ACT.Exp, scale=scale,
                               bias=stat[:, base + i % 4:base + i % 4 + 1],
                               accum_out=stat[:, base + 4 + i % 4:base + 5 + i % 4]).then_inc(empty((key, i)), 1)

            head_in(0)
            for i in range(NH * NT + 3):
                if i < NH * NT:
                    exponentials(i, "S", T, Pm, negmax, QD ** -0.5, 80, "PT")
                    if i % NT == 1 and i // NT + 1 < NH:
                        head_in(i // NT + 1)
                if 2 <= i < NH * NT + 2:
                    h, qt = divmod(i - 2, NT)
                    if qt % 2:
                        b = await_full(act, ("PT", i - 2))
                        if h >= 2:
                            await_full(act, ("O", h - 2))
                        copy_out(("PT", i - 2), PT[h % 2][:, :, P * qt:P * qt + P],
                                 b[:, :].rearrange("p (k q) -> p k q", k=NT))
                if i >= 3 and (i - 3) % NT == NT - 1:
                    h = (i - 3) // NT
                    b = await_full(act, ("O", h))
                    copy_out(("O", h), OT[64 * (h % 2):64 * (h % 2) + 64, h // 2, :], b[0:HV, :])
            act.wait_ge(d_mem, 16)
            squares(1, memx, junk)
            for i in range(KD):
                s = mixtmp[i % 2]
                if i >= 2:
                    act.wait_ge(mix_done, i - 1)
                b = await_full(act, ("gate", i))
                act.activation(s[0], b[:, :], ACT.Sigmoid).then_inc(empty(("gate", i)), 1)
                for n, kind in enumerate(("gs", "gm")):
                    b = await_full(act, (kind, i))
                    c = VEC["b_gate"][0] + KD * n + i
                    act.activation(s[1 + n], b[:, :], ACT.Sigmoid,
                                   bias=vec[:, c:c + 1]).then_inc(empty((kind, i)), 1)
            features("g_mem_kv", "mT", memT, MT)
            for part in (2, 3):
                squares(part, H, junk, "out")
            for q in range(4):
                b = await_full(act, ("keyT", q))
                copy_out(("keyT", q), keysT[:, 4 * q:4 * q + 4, :].rearrange("p k n -> p (k n)"), b[:, :])
            features("g_mem_q", "hT", FT, T)
            for m in range(KD):
                b = await_full(act, ("Qm", m))
                copy_out(("Qm", m), QmT[:, m, :], b[:, :])
            for i in range(MH * NT + 3):
                if i < MH * NT:
                    exponentials(i, "Sm", MT, Pmm, mnegmax, MD ** -0.5, 92, "PTm")
                if i >= 3 and (i - 3) % NT == NT - 1:
                    h = (i - 3) // NT
                    for d in range(2):
                        b = await_full(act, ("Om", h, d))
                        copy_out(("Om", h, d), OmT[:, 2 * h + d, :], b[:, :])
            for part in (4, 5):
                squares(part, H, junk, "mo")
            features("g_peer", "pT", FT, T)

            def queries_out(h, s, first=False):
                act.wait_ge(q_filled, h * 2 + (s + 1))
                if not first:
                    act.wait_ge(s_filled, h * 2 + (s - 1))
                act.activation(qhs[s], ps[4 + s][:, :], ACT.Copy).then_inc(q_copied, 1)

            def gate_exponentials(g):
                act.wait_ge(gates_neg, g + 1)
                act.activation(ex, cv, ACT.Exp, bias=nmx, accum_out=esum).then_inc(gates_exp, 1)

            def gelu_of(g):
                act.wait_ge(dots, (g + 1) * TOPK)
                act.activation(gel, act_row, ACT.Gelu_apprx_tanh).then_inc(gelu_done, 1)

            def diagonals(g, t, first=False):
                act.wait_ge(w_ready, g + 1)
                for s in range(TOPK):
                    if not first or s >= DRING:
                        act.wait_ge(v_summed, g * TOPK + (s - DRING + 1))
                    act.activation(diag[s % DRING], ident, ACT.Copy,
                                   scale=wgt[t % 2][:, s:s + 1]).then_inc(diag_done, 1)

            def head(h, first=False, last=False):
                for t in range(NT):
                    g = h * NT + t
                    if t < 2 and not last:
                        queries_out(h + 1, t)
                    if not last or t < 2:
                        gate_exponentials(g + 2)
                    if last and t == NT - 1:
                        final_root(0)
                        final_root(1)
                    diagonals(g, t, first and t == 0)
                    if not last or t < NT - 1:
                        gelu_of(g + 1)

            def final_root(t):
                act.wait_ge(var_done, len(PARTS) + t + 1)
                act.activation(stat[:, 72 + t:73 + t], stat[:, 68 + t:69 + t], ACT.Sqrt).then_inc(std_done, 1)

            queries_out(0, 0, True)
            queries_out(0, 1, True)
            gate_exponentials(0)
            gate_exponentials(1)
            gelu_of(0)
            head(0, first=True)
            with act.Fori(1, PH - 1) as h:
                head(h)
            head(PH - 1, last=True)
            final_root(2)
            final_root(3)

        @block.vector
        def _(dve):
            own = [0]

            def step(ins):
                own[0] += 1
                ins.then_inc(c_dve, 1)
                dve.wait_ge(c_dve, own[0])

            def tt(out, a, b, op):
                step(dve.tensor_tensor(out, a, b, op))

            def signal(ins, s, n):
                ins.then_inc(s, 1)
                dve.wait_ge(s, n)

            def normalise(part, src, dst):
                k, tiles = PARTS[part]
                lo, hi = 16 * k + tiles[0], 16 * k + tiles[-1] + 1
                dve.wait_ge(sq_done, part + 1)
                dve.tensor_scalar(stat[:, 4 + lo:4 + hi], stat[:, lo:hi], 1.0 / D, EPS,
                                  ALU.mult, ALU.add).then_inc(var_done, 1)
                dve.wait_ge(std_done, part + 1)
                step(dve.reciprocal(stat[:, 12 + lo:12 + hi], stat[:, 8 + lo:8 + hi]))
                for t in tiles:
                    c = stat[:, 16 * k + 12 + t:16 * k + 13 + t]
                    dve.tensor_scalar(dst[:, t, :], src[:, t, :], c, None, ALU.mult).then_inc(xn_done, 1)

            def reduce_turns(src, dst, n, turn=0.0, angle=0.0):
                step(dve.tensor_scalar(n, src, 1.0 / TWO_PI, turn, ALU.mult, ALU.add))
                step(dve.tensor_scalar(n, n, ROUND, -ROUND, ALU.add, ALU.add))
                step(dve.scalar_tensor_tensor(dst, n, -PI_HI, src, ALU.mult, ALU.add))
                step(dve.scalar_tensor_tensor(dst, n, -PI_MID, dst, ALU.mult, ALU.add))
                step(dve.scalar_tensor_tensor(dst, n, -PI_LO, dst, ALU.mult, ALU.add))
                step(dve.tensor_scalar(dst, dst, angle, PI_CLAMP, ALU.add, ALU.min))
                step(dve.tensor_scalar(dst, dst, -PI_CLAMP, None, ALU.max))

            b = await_full(dve, ("vec",))
            dve.tensor_copy(vec[:, :], b[:, 0:NVEC]).then_inc(empty(("vec",)), 1)
            b = await_full(dve, ("par",))
            dve.tensor_copy(sm[:, 0:4, :].rearrange("p a g -> p (a g)"), b[:, 0:4 * G]).then_inc(empty(("par",)), 1)
            await_drained(dve, ("par",))
            lre, lim, dt, dsk = (sm[:, i, :] for i in range(4))
            tt(sm[:, 4, :], lre, dt, ALU.mult)
            tt(sm[:, 5, :], lim, dt, ALU.mult)
            reduce_turns(sm[:, 5, :], sm[:, 10, :], sm[:, 9, :], 0.25, math.pi / 2)
            reduce_turns(sm[:, 5, :], sm[:, 11, :], sm[:, 9, :])
            dve.sem_inc(args_done, 1)
            dve.wait_ge(d_x, 16)
            normalise(0, xn, xn)
            dve.wait_ge(trig_done, 3)
            mag, co, si = sm[:, 6, :], sm[:, 7, :], sm[:, 8, :]

            def pw(r, k):
                return sm[:, 16 + 9 * r + k, :]

            step(dve.memset(pw(0, 0), 1.0))
            step(dve.memset(pw(1, 0), 0.0))
            tt(pw(0, 1), mag, co, ALU.mult)
            tt(pw(1, 1), mag, si, ALU.mult)

            def cmul(o, a, b, tmp):
                tt(tmp[0], a[0], b[0], ALU.mult)
                tt(tmp[1], a[1], b[1], ALU.mult)
                tt(o[0], tmp[0], tmp[1], ALU.subtract)
                tt(tmp[0], a[0], b[1], ALU.mult)
                tt(tmp[1], a[1], b[0], ALU.mult)
                tt(o[1], tmp[0], tmp[1], ALU.add)

            n = 1
            while n < CH:
                def span(r, lo, m):
                    return sm[:, 16 + 9 * r + lo:16 + 9 * r + lo + m, :]
                top = [pw(r, n).unsqueeze(1).to_broadcast([P, n, G]) for r in range(2)]
                cmul([span(r, n + 1, n) for r in range(2)], [span(r, 1, n) for r in range(2)], top,
                     [sm[:, 78:78 + n, :], sm[:, 86:86 + n, :]])
                n *= 2
            for r in range(2):
                px, py = 34 + 8 * r, 50 + 8 * r
                base = 16 + 9 * r
                for k in range(CH):
                    step(dve.tensor_copy(sm[0:64, px + k, :], sm[0:64, base + CH - 1 - k, :]))
                    step(dve.tensor_copy(sm[64:128, py + k, :], sm[64:128, base + CH - k, :]))
                step(dve.tensor_copy(sm[64:128, px:px + CH, :], sm[64:128, base:base + CH, :]))
                step(dve.tensor_copy(sm[0:64, py:py + CH, :], sm[0:64, base + 1:base + 1 + CH, :]))
            step(dve.tensor_scalar(sm[:, 94, :], pw(0, 1), -1.0, None, ALU.add))
            tt(sm[:, 78, :], lre, lre, ALU.mult)
            tt(sm[:, 79, :], lim, lim, ALU.mult)
            tt(sm[:, 80, :], sm[:, 78, :], sm[:, 79, :], ALU.add)
            step(dve.reciprocal(sm[:, 81, :], sm[:, 80, :]))
            tt(sm[:, 82, :], sm[:, 94, :], lre, ALU.mult)
            tt(sm[:, 83, :], pw(1, 1), lim, ALU.mult)
            tt(sm[:, 84, :], sm[:, 82, :], sm[:, 83, :], ALU.add)
            tt(sm[:, 84, :], sm[:, 84, :], sm[:, 81, :], ALU.mult)
            tt(sm[:, 82, :], pw(1, 1), lre, ALU.mult)
            tt(sm[:, 83, :], sm[:, 94, :], lim, ALU.mult)
            tt(sm[:, 85, :], sm[:, 82, :], sm[:, 83, :], ALU.subtract)
            tt(sm[:, 85, :], sm[:, 85, :], sm[:, 81, :], ALU.mult)
            dve.wait_ge(d_ssm, 16 * 8)
            fr, fi = (sm[:, 84 + r, :].unsqueeze(2).to_broadcast([P, G, CG]) for r in range(2))
            tg = [t.rearrange("p (g c) -> p g c", g=G) for t in t4]
            tt(tg[0], bb[0], fr, ALU.mult)
            tt(tg[1], bb[1], fi, ALU.mult)
            tt(tg[2], bb[1], fr, ALU.mult)
            tt(tg[3], bb[0], fi, ALU.mult)
            tt(bb[0], tg[0], tg[1], ALU.subtract)
            tt(bb[1], tg[2], tg[3], ALU.add)
            await_drained(dve, ("C", 0))
            await_drained(dve, ("C", 1))
            signal(dve.tensor_scalar(negC, Cc[1], -1.0, None, ALU.mult), pow_done, 1)

            def contributions(q):
                gs = slice(GB * q, GB * q + GB)
                if q:
                    await_full(dve, ("bT", q - 1, 1, 1))
                pr, pi = (sm[:, 34 + 8 * r:42 + 8 * r, gs].rearrange("p k g -> p g k").unsqueeze(3)
                          .to_broadcast([P, GB, CH, CG]) for r in range(2))
                br, bi = (bb[r][:, gs, :].unsqueeze(2).to_broadcast([P, GB, CH, CG]) for r in range(2))
                tt(ta, pr, br, ALU.mult)
                tt(tb, pi, bi, ALU.mult)
                signal(dve.tensor_tensor(VB[0], ta, tb, ALU.subtract), vb_done, 2 * q + 1)
                tt(ta, pr, bi, ALU.mult)
                tt(tb, pi, br, ALU.mult)
                signal(dve.tensor_tensor(VB[1], ta, tb, ALU.add), vb_done, 2 * q + 2)

            contributions(0)
            dve.wait_ge(table_done, 1)
            for q in range(NB):
                if q + 1 < NB:
                    contributions(q + 1)
                gs = slice(GB * q, GB * q + GB)
                tc, ts = (t[:, gs, :].rearrange("p g m -> p (g m)") for t in (Tre, Tim))
                tt(M8, mask.unsqueeze(1).to_broadcast([P, GB, M]),
                   sm[:, 12, gs].unsqueeze(2).to_broadcast([P, GB, M]), ALU.mult)
                xr = await_full(dve, ("X", q, 0))
                xi = await_full(dve, ("X", q, 1))
                tt(t4[0], xr[:, :], tc, ALU.mult)
                tt(t4[2], xr[:, :], ts, ALU.mult)
                dve.sem_inc(empty(("X", q, 0)), 1)
                tt(t4[1], xi[:, :], ts, ALU.mult)
                tt(t4[3], xi[:, :], tc, ALU.mult)
                dve.sem_inc(empty(("X", q, 1)), 1)
                tt(Z[0], t4[0], t4[1], ALU.add)
                tt(Z[1], t4[3], t4[2], ALU.subtract)
                m8 = M8.rearrange("p g m -> p (g m)")
                for r in range(2):
                    step(dve.tensor_tensor_scan(Zs[r][0:64, :], m8[0:64, :], Z[r][0:64, :], 0.0, ALU.mult, ALU.add))
                    step(dve.tensor_tensor_scan(Zs[r][64:128, ::-1], m8[64:128, ::-1], Z[r][64:128, ::-1], 0.0,
                                                ALU.mult, ALU.add))
                tt(t4[0], Zs[0], tc, ALU.mult)
                tt(t4[1], Zs[1], ts, ALU.mult)
                tt(t4[2], Zs[0], ts, ALU.mult)
                tt(t4[3], Zs[1], tc, ALU.mult)
                if q:
                    await_full(dve, ("Y", q - 1))
                tv4 = [t.rearrange("p (g m) -> p g m", g=GB) for t in t4]
                for r, op in ((0, ALU.subtract), (1, ALU.add)):
                    for lo, dst, src in ((0, slice(1, M), slice(0, M - 1)), (64, slice(0, M - 1), slice(1, M))):
                        dve.tensor_tensor(Sst[r][lo:lo + 64, :, dst], tv4[2 * r][lo:lo + 64, :, src],
                                          tv4[2 * r + 1][lo:lo + 64, :, src], op).then_inc(s_done, 1)
                dve.wait_ge(s_done, 4 * (q + 1))
                b = await_full(dve, ("Y", q))
                tt(tv4[0], U[:, gs, :], dsk[:, gs].unsqueeze(2).to_broadcast([P, GB, M]), ALU.mult)
                dve.tensor_tensor(U[:, gs, :], b[:, :].rearrange("p (g m) -> p g m", g=GB), tv4[0],
                                  ALU.add).then_inc(empty(("Y", q)), 1)
                await_drained(dve, ("Y", q))

            for k, (key, n) in enumerate(((("kvn",), KVL), (("qn",), QL))):
                b = await_full(dve, key)
                dve.tensor_scalar(lat[k], b[:, :], 1.0 / n, EPS, ALU.mult, ALU.add).then_inc(empty(key), 1)
                await_drained(dve, key)
                dve.sem_inc(lat_var, 1)
            for k, (m0, n, src, name) in enumerate(((0, 2, ckvT, "g_kv_lora"), (2, 3, cqT, "g_q_lora"))):
                dve.wait_ge(lat_std, k + 1)
                step(dve.reciprocal(lat[k], lat[k]))
                for m in range(n):
                    c = VEC[name][0] + m
                    signal(dve.scalar_tensor_tensor(src[:, m, :], src[:, m, :], vec[:, c:c + 1], lat[k],
                                                    ALU.mult, ALU.mult), lat_done, m0 + m + 1)
            dve.wait_ge(d_pos, 16)
            step(dve.tensor_copy(tC, posb))
            step(dve.tensor_scalar(tC, tC, cst[:, C_ROPE:C_ROPE + 1], None, ALU.mult))
            step(dve.tensor_scalar(tB, tC, 1.0 / TWO_PI, cst[:, C_ROPE + 1:C_ROPE + 2], ALU.mult, ALU.add))
            step(dve.tensor_scalar(tB, tB, ROUND, -ROUND, ALU.add, ALU.add))
            step(dve.scalar_tensor_tensor(tA, tB, -PI_HI, tC, ALU.mult, ALU.add))
            step(dve.scalar_tensor_tensor(tA, tB, -PI_MID, tA, ALU.mult, ALU.add))
            step(dve.scalar_tensor_tensor(tA, tB, -PI_LO, tA, ALU.mult, ALU.add))
            step(dve.tensor_scalar(tA, tA, cst[:, C_ROPE + 2:C_ROPE + 3], PI_CLAMP, ALU.add, ALU.min))
            signal(dve.tensor_scalar(tA, tA, -PI_CLAMP, None, ALU.max), rope_arg, 1)
            dve.wait_ge(rope_sin, 1)
            step(dve.tensor_scalar(TAB, TAB, cst[:, C_ROPE + 3:C_ROPE + 4], None, ALU.mult))

            def turn(src, dsts):
                step(dve.tensor_tensor(tA[64:96, :], src[64:96, :], TAB[64:96, :], ALU.mult))
                step(dve.tensor_tensor(tB[64:96, :], src[96:128, :], TAB[96:128, :], ALU.mult))
                return [dve.tensor_tensor(d[64:96, :], tA[64:96, :], tB[64:96, :], ALU.add) for d in dsts]

            for n, ins in enumerate(turn(krT, KT)):
                ins.then_inc(kr_done, 1)
            dve.wait_ge(kr_done, 2)

            def head_in(h):
                await_drained(dve, ("Q", h))
                signal(turn(QT[h % 2], [QT[h % 2]])[0], qk_done, h + 1)

            def row_max(i, key, width, negs, scale, base):
                b = await_full(dve, (key, i))
                c = stat[:, base + i % 4:base + i % 4 + 1]
                step(dve.tensor_reduce(c, b[:, 0:width], AX.X, ALU.max))
                dve.tensor_scalar(c, c, -scale, None, ALU.mult).then_inc(negs, 1)

            def normal(i, key, bufs, done, base):
                await_drained(dve, (key, i))
                c = stat[:, base + 8 + i % 4:base + 9 + i % 4]
                step(dve.reciprocal(c, stat[:, base + 4 + i % 4:base + 5 + i % 4]))
                dve.tensor_scalar(bufs[i % 2], bufs[i % 2], c, None, ALU.mult).then_inc(done, 1)

            head_in(0)
            for i in range(NH * NT + 2):
                if i < NH * NT:
                    row_max(i, "S", T, negmax, QD ** -0.5, 80)
                if 1 <= i <= NH * NT:
                    normal(i - 1, "S", Pm, p_done, 80)
                if i < NH * NT and i % NT == 1 and i // NT + 1 < NH:
                    head_in(i // NT + 1)
                if i >= 2:
                    h, qt = divmod(i - 2, NT)
                    if qt % 2 == 0:
                        b = await_full(dve, ("PT", i - 2))
                        if h >= 2:
                            await_full(dve, ("O", h - 2))
                        dve.tensor_copy(PT[h % 2][:, :, P * qt:P * qt + P],
                                        b[:, :].rearrange("p (k q) -> p k q", k=NT)).then_inc(empty(("PT", i - 2)), 1)
            normalise(1, memx, memx)
            for i in range(KD):
                s = mixtmp[i % 2]
                b = await_full(dve, ("val", i))
                await_drained(dve, ("gate", i))
                dve.tensor_tensor(s[3], b[:, :], s[0], ALU.mult).then_inc(empty(("val", i)), 1)
                await_drained(dve, ("val", i))
                await_drained(dve, ("gs", i))
                tt(s[3], s[3], s[1], ALU.mult)
                b = await_full(dve, ("mla", i))
                await_drained(dve, ("gm", i))
                dve.tensor_tensor(s[4], b[:, :], s[2], ALU.mult).then_inc(empty(("mla", i)), 1)
                await_drained(dve, ("mla", i))
                dve.tensor_tensor(mixT[:, i, :], s[3], s[4], ALU.add).then_inc(mix_done, 1)

            def residual(kind, part):
                for p in range(2):
                    for n in range(4):
                        b = await_full(dve, (kind, n, p))
                        h = H[:, 2 * p:2 * p + 2, 256 * n:256 * n + 256]
                        dve.tensor_tensor(h, b[:, :].rearrange("p (t n) -> p t n", t=2), h,
                                          ALU.add).then_inc(empty((kind, n, p)), 1)
                    for n in range(4):
                        await_drained(dve, (kind, n, p))
                    normalise(part + p, H, xn)

            for n in range(4):
                b = await_full(dve, ("Km", n))
                dve.tensor_copy(KmT[:, 2 * n:2 * n + 2, :].rearrange("p m t -> p (m t)"), b[:, :]).then_inc(empty(("Km", n)), 1)
            dve.wait_ge(d_res, 16)
            residual("out", 2)
            for n in range(4):
                b = await_full(dve, ("Vm", n))
                dve.tensor_copy(Vm[:, :, 256 * n:256 * n + 256],
                                b[:, :].rearrange("p (t n) -> p t n", t=2)).then_inc(empty(("Vm", n)), 1)
            for i in range(MH * NT + 2):
                if i < MH * NT:
                    row_max(i, "Sm", MT, mnegmax, MD ** -0.5, 92)
                if 1 <= i <= MH * NT:
                    normal(i - 1, "Sm", Pmm, mp_done, 92)
                if i >= 2:
                    h, qt = divmod(i - 2, NT)
                    b = await_full(dve, ("PTm", i - 2))
                    if h >= 2:
                        await_full(dve, ("Om", h - 2, 1))
                    dve.tensor_copy(PTm[h % 2][:, :, P * qt:P * qt + P],
                                    b[:, 0:MT].rearrange("p (k q) -> p k q", k=2)).then_inc(empty(("PTm", i - 2)), 1)
            residual("mo", 4)
            dve.wait_ge(d_grow, 32)

            count = [0, 0]

            def lstep(ins, apart=False):
                count[0] += 1
                ins.then_inc(c_loop, 1)
                dve.wait_ge(c_loop, count[1] + count[0])
                if apart:
                    dve.sem_inc(apart_dve, 1)

            def top16(vals, spare, v, ix):
                lstep(dve.max(v[:, 0:8], vals), apart=True)
                lstep(dve.max_index(ix[:, 0:8], v[:, 0:8], vals), apart=True)
                lstep(dve.match_replace(spare, v[:, 0:8], vals, NEG), apart=True)
                lstep(dve.max(v[:, 8:16], spare), apart=True)
                lstep(dve.max_index(ix[:, 8:16], v[:, 8:16], spare), apart=True)

            def scores(h):
                for s in range(2):
                    dve.wait_ge(s_filled, h * 2 + (s + 1))
                    lstep(dve.tensor_copy(SC[:, :, s, :], ps[6 + s][:, :].rearrange("p (t n) -> p t n", t=NT)),
                          apart=True)
                dve.sem_inc(s_copied, 1)

            def topk(t):
                dve.sem_inc(apart_dve, 1)
                for s in range(2):
                    top16(SC[:, t, s, :], sc1, tv[:, s, :], ti[:, s, :])
                lstep(dve.tensor_copy(tif, ti))
                lstep(dve.tensor_tensor(cand.rearrange("p (a b) -> p a b", a=TOPK),
                                        tv[:, 0, :].unsqueeze(2).to_broadcast([P, TOPK, TOPK]),
                                        tv[:, 1, :].unsqueeze(1).to_broadcast([P, TOPK, TOPK]), ALU.add), apart=True)
                top16(cand, cand1, cv, cpos)
                lstep(dve.tensor_scalar(nmx, cv[:, 0:1], -1.0, None, ALU.mult))
                dve.sem_inc(gates_neg, 1)
                lstep(dve.tensor_scalar(cpp[:, 0:16], cpos, 4, None, ALU.logical_shift_right))
                lstep(dve.tensor_scalar(cpp[:, 16:32], cpos, 15, None, ALU.bitwise_and))
                lstep(dve.tensor_copy(cpf, cpp))
                lstep(dve.tensor_tensor(eq, iota16.unsqueeze(1).to_broadcast([P, 2 * TOPK, TOPK]),
                                        cpf.unsqueeze(2).to_broadcast([P, 2 * TOPK, TOPK]), ALU.is_equal))
                e4 = eq.rearrange("p (s k) a -> p s k a", s=2)
                lstep(dve.tensor_tensor(e4, e4, tif.unsqueeze(2).to_broadcast([P, 2, TOPK, TOPK]), ALU.mult))
                lstep(dve.tensor_reduce(isel, eq, AX.X, ALU.add))
                lstep(dve.scalar_tensor_tensor(idx[t], isel[:, 0:16], float(NK), isel[:, 16:32], ALU.mult, ALU.add))
                dve.sem_inc(idx_ready, 1)

            def gates_of(g, t):
                dve.wait_ge(gates_exp, g + 1)
                lstep(dve.reciprocal(rinv, esum))
                lstep(dve.tensor_scalar(gate[t % 2], ex, rinv, None, ALU.mult))

            def dot_products(g, t):
                for s in range(TOPK):
                    dve.wait_ge(ld_u[s % URING], (g * 2 + (s // URING + 1)) * 16)
                    dve.tensor_tensor_reduce(prod, Ub[s % URING], xn[:, t, :], 1.0, 0.0, ALU.mult, ALU.add,
                                             act_row[:, s:s + 1]).then_inc(dots, 1)
                    dve.wait_ge(dots, g * TOPK + (s + 1))

            def weights(g, t):
                dve.wait_ge(gelu_done, g + 1)
                lstep(dve.tensor_tensor(wgt[t % 2], gel, gate[t % 2], ALU.mult))
                dve.sem_inc(w_ready, 1)

            def take_sum(g, t):
                dve.wait_ge(v_summed, (g + 1) * TOPK)
                for n in range(2):
                    h = H[:, t, 512 * n:512 * n + 512]
                    lstep(dve.tensor_tensor(h, ps[2 * (t % 2) + n][:, :], h, ALU.add))
                dve.sem_inc(acc_taken, 1)

            def head(h, first=False, last=False):
                for t in range(NT):
                    g = h * NT + t
                    ahead = not last or t < 2
                    if t == 2 and not last:
                        scores(h + 1)
                    if ahead:
                        topk((t + 2) % NT)
                    if not first or t:
                        take_sum(g + (-1), (t - 1) % NT)
                    if not last or t < NT - 1:
                        dot_products(g + 1, (t + 1) % NT)
                        weights(g + 1, (t + 1) % NT)
                    if ahead:
                        gates_of(g + 2, t)

            def final_variance(t):
                step(dve.tensor_tensor_reduce(prod, H[:, t, :], H[:, t, :], 1.0, 0.0, ALU.mult, ALU.add, sumsq(4, t)))
                dve.tensor_scalar(stat[:, 68 + t:69 + t], sumsq(4, t), 1.0 / D, EPS, ALU.mult, ALU.add).then_inc(var_done, 1)

            def final_rows(t):
                dve.wait_ge(std_done, len(PARTS) + t + 1)
                c = stat[:, 76 + t:77 + t]
                step(dve.reciprocal(c, stat[:, 72 + t:73 + t]))
                dve.scalar_tensor_tensor(xn[:, t, :], H[:, t, :], c, gfrow, ALU.mult, ALU.mult).then_inc(final_done, 1)

            scores(0)
            topk(0)
            await_full(dve, ("pT", KD - 1))
            for t in range(NT):
                step(dve.tensor_tensor(xn[:, t, :], xn[:, t, :], gprow, ALU.mult))
            gates_of(0, 0)
            topk(1)
            gates_of(1, 1)
            dot_products(0, 0)
            weights(0, 0)
            head(0, first=True)
            start = count[0]
            per_head = NT * (TOPK_STEPS + 2 + 1 + 2) + 2
            count[0] = 0
            with dve.Fori(1, PH - 1) as h:
                count[1] = (h - 1) * per_head + start
                head(h)
                assert count[0] == per_head, count
            count[1] = start + (PH - 2) * per_head
            count[0] = 0
            head(PH - 1, last=True)
            for t in range(NT - 1):
                final_variance(t)
            for t in range(2):
                final_rows(t)
            take_sum(NG - 1, NT - 1)
            final_variance(NT - 1)
            for t in range(2, NT):
                final_rows(t)

        @block.tensor
        def _(pe):
            def turn(key, pieces):
                b = take(pe, key)
                for dst, src in pieces(b):
                    n = src.shape[0]
                    last = pe.transpose(dst, src, ident[0:n, 0:n])
                last.then_inc(full(key), 1)

            def product(key, groups):
                b = take(pe, key)
                for dst, terms in groups(b):
                    for n, (lhs, rhs) in enumerate(terms):
                        last = pe.matmul(dst, lhs, rhs, start=(n == 0), stop=(n == len(terms) - 1))
                last.then_inc(full(key), 1)

            def columns(t):
                return slice(P * t, P * t + P)

            pe.wait_ge(d_cst, 16)
            pe.wait_ge(d_vec, 16 * 7)
            turn(("vec",), lambda b: [(b[:, 0:NVEC], vecrow[:, :])])
            pe.wait_ge(par_rows, 1)
            turn(("par",), lambda b: [(b[:, G * i:G * i + G], parrow[i]) for i in range(4)])
            for k in range(KD):
                pe.wait_ge(xn_done, before[1])
                turn(("xT", k), lambda b: [(b[:, columns(t)], xn[:, t, columns(k)]) for t in range(NT)])
            pe.wait_ge(d_ssm, 16 * 8)
            for r in range(2):
                turn(("C", r), lambda b: [(b[:, columns(q)], Craw[r][:, q, :]) for q in range(NB)])
            for k in range(KD):
                await_drained(pe, ("xT", k))
            await_slab(pe, ("u", 0))
            await_slab(pe, ("u", 1))
            by_step = [FT[:, k, :].rearrange("p (n q) -> p q n", q=4) for k in range(KD)]
            for q in range(4):
                product(("u", q), lambda b: [
                    (b[:, 256 * n:256 * n + 256],
                     [(by_step[k][:, q, :], slab(("u", n), 8, 256)[:, k, :]) for k in range(KD)])
                    for n in range(2)])
            for q in range(4):
                await_drained(pe, ("u", q))
            for q in range(G // 4):
                turn(("uT", q), lambda b: [
                    (b[0:64, columns(g)], ustage[:, 4 * q + g, :, :].rearrange("p q c -> p (q c)")) for g in range(4)])

            def latent(key, s, at):
                await_slab(pe, ("c", s))
                w = slab(("c", s), 8, 256)
                product(key, lambda b: [(b[:, :], [(w[:, k, at:at + 128], FT[:, k, :]) for k in range(KD)])])

            def block_prep(q):
                pe.wait_ge(vb_done, 2 * (q + 1))
                for r in range(2):
                    for s in range(2):
                        turn(("bT", q, r, s), lambda b: [
                            (b[:, columns(g)], VB[r][:, 4 * s + g, :, :].rearrange("p j c -> p (j c)"))
                            for g in range(4)])
                pe.wait_ge(ext_done, 6 * (q + 1))
                for s in range(NB):
                    product(("D", q, s), lambda b: [
                        (b[0:CG, LAGS * CG * g:LAGS * CG * (g + 1)],
                         [(bb[r][:, GB * q + 2 * s + g, :],
                           EXT[r][:, 2 * s + g, :, :].rearrange("p l c -> p (l c)")) for r in range(2)])
                        for g in range(2)])

            def chunk_inputs(q):
                for r in range(2):
                    for s in range(2):
                        await_drained(pe, ("bT", q, r, s))
                for r in range(2):
                    product(("X", q, r), lambda b: [
                        (b[:, M * g:M * g + M], [(BT[r][:, g, :], U[:, GB * q + g, :])]) for g in range(GB)])

            block_prep(0)
            for q in range(G // 4):
                await_drained(pe, ("uT", q))
            chunk_inputs(0)
            for q in range(NB):
                if q + 1 < NB:
                    for entry in LATENT_JOBS[2 * q:2 * q + 2]:
                        latent(*entry)
                    block_prep(q + 1)
                else:
                    pe.wait_ge(lat_sq, 5)
                    pe.wait_ge(ones_set, 1)
                    product(("kvn",), lambda b: [(b[:, :], [(ones[:, :], latsq[:, 3 + m, :]) for m in range(2)])])
                    product(("qn",), lambda b: [(b[:, :], [(ones[:, :], latsq[:, m, :]) for m in range(3)])])
                pe.wait_ge(d_within, 16 * CH * (q + 1))
                pe.wait_ge(w_done, q + 1)
                pe.wait_ge(s_done, 4 * (q + 1))
                wre, wim = (Wst[q % 2][r].rearrange("p g j c -> p g (j c)") for r in range(2))
                product(("Y", q), lambda b: [
                    (b[:, M * g:M * g + M], [(DTm[:, g, :], U[:, GB * q + g, :]), (wre[:, g, :], Sst[0][:, g, :]),
                                             (wim[:, g, :], Sst[1][:, g, :])]) for g in range(GB)])
                if q + 1 < NB:
                    chunk_inputs(q + 1)
            pe.wait_ge(yg_done, NB)
            for q in range(G // 4):
                turn(("yt", q), lambda b: [(b[0:M, columns(g)], U[:, 4 * q + g, :]) for g in range(4)])
            for q in range(G // 4):
                await_drained(pe, ("yt", q))
            for f in range(4):
                turn(("yT", f), lambda b: [(b[:, M * j:M * j + M], ytok[:, j, columns(f)]) for j in range(CH)])
            pe.wait_ge(lat_done, 2)
            await_slab(pe, ("ukv",))
            ukv = slab(("ukv",), 2, 1024)
            uv = ukv.rearrange("p k (h n) -> p k h n", h=NH)
            for kt in range(NT):
                product(("V", kt), lambda b: [
                    (b[:, :], [(ckvT[:, k, columns(kt)], uv[:, k, :, NOPE:NOPE + HV]) for k in range(2)])])
            pe.wait_ge(lat_done, 5)
            pe.wait_ge(d_wuq, 16 * 9)

            def head_in(h):
                product(("Q", h), lambda b: [(b[:, :], [(wuq[:, k, h, :], cqT[:, k, :]) for k in range(3)])])
                product(("K", h), lambda b: [
                    (b[0:NOPE, :], [(ukv[:, k, P * h:P * h + NOPE], ckvT[:, k, :]) for k in range(2)])])

            head_in(0)
            for kt in range(NT):
                await_drained(pe, ("V", kt))
            pe.wait_ge(kr_done, 2)
            for i in range(NH * NT + 3):
                h, qt = divmod(i, NT)
                if i < NH * NT:
                    if qt == 0:
                        pe.wait_ge(qk_done, h + 1)
                        await_drained(pe, ("K", h))
                    product(("S", i), lambda b: [(b[:, :], [(QT[h % 2][0:QD, columns(qt)], KT[h % 2][0:QD, :])])])
                    if qt == 1 and h + 1 < NH:
                        head_in(h + 1)
                if 2 <= i < NH * NT + 2:
                    pe.wait_ge(p_done, i - 1)
                    turn(("PT", i - 2), lambda b: [(b[:, columns(k)], Pm[i % 2][:, columns(k)]) for k in range(NT)])
                if i >= 3 and (i - 3) % NT == NT - 1:
                    g = (i - 3) // NT
                    for n in range(NT):
                        await_drained(pe, ("PT", NT * g + n))
                    product(("O", g), lambda b: [
                        (b[0:HV, :], [(V[:, k, HV * g:HV * g + HV], PT[g % 2][:, k, :]) for k in range(NT)])])
            for f in range(4):
                await_drained(pe, ("yT", f))
            for i in range(KD):
                await_slab(pe, ("mix", i))
                w = slab(("mix", i), 4, 3 * P)
                for n, key in enumerate((("val", i), ("gate", i))):
                    product(key, lambda b: [(b[:, :], [(w[:, k, columns(n)], yT[:, k, :]) for k in range(4)])])
                await_slab(pe, ("gates", i))
                wg = slab(("gates", i), 8, 256)
                for n, key in enumerate((("gs", i), ("gm", i))):
                    product(key, lambda b: [(b[:, :], [(wg[:, k, columns(n)], FT[:, k, :]) for k in range(KD)])])
                if i == 0:
                    for h in range(NH):
                        await_drained(pe, ("O", h))
                product(("mla", i), lambda b: [
                    (b[:, :], [(w[:, k, columns(2)], OT[:, k, :]) for k in range(4)])])

            def token_major(kind, src):
                for p in range(2):
                    for n in range(4):
                        await_slab(pe, (kind, n))
                        w = slab((kind, n), 8, 256)
                        product((kind, n, p), lambda b: [
                            (b[:, 256 * t:256 * t + 256],
                             [(src[:, k, columns(2 * p + t)], w[:, k, :]) for k in range(KD)]) for t in range(2)])

            pe.wait_ge(xn_done, before[2])
            for k in range(KD):
                turn(("mT", k), lambda b: [(b[:, columns(t)], memx[:, t, columns(k)]) for t in range(2)])
            for k in range(KD):
                await_drained(pe, ("mT", k))
            for n in range(4):
                await_slab(pe, ("mk", n))
                w = slab(("mk", n), 8, 256)
                product(("Km", n), lambda b: [
                    (b[:, 256 * m:256 * m + 256], [(w[:, k, columns(m)], memT[:, k, :]) for k in range(KD)])
                    for m in range(2)])
            pe.wait_ge(mix_done, KD)
            token_major("out", mixT)
            for n in range(4):
                await_slab(pe, ("mv", n))
                w = slab(("mv", n), 8, 256)
                product(("Vm", n), lambda b: [
                    (b[:, 256 * t:256 * t + 256], [(memT[:, k, columns(t)], w[:, k, :]) for k in range(KD)])
                    for t in range(2)])
            pe.wait_ge(d_key, 16)
            for q in range(4):
                turn(("keyT", q), lambda b: [(b[:, columns(i)], keyraw[:, 4 * q + i, :]) for i in range(4)])
            pe.wait_ge(xn_done, before[3])
            for k in range(KD):
                turn(("hT", k), lambda b: [(b[:, columns(t)], xn[:, t, columns(k)]) for t in range(NT)])
            for k in range(KD):
                await_drained(pe, ("hT", k))
            for m in range(KD):
                await_slab(pe, ("mq", m // 2))
                w = slab(("mq", m // 2), 8, 256)
                product(("Qm", m), lambda b: [
                    (b[:, :], [(w[:, k, columns(m % 2)], FT[:, k, :]) for k in range(KD)])])
            for m in range(KD):
                await_drained(pe, ("Qm", m))
            for n in range(4):
                await_drained(pe, ("Km", n))
                await_drained(pe, ("Vm", n))
            for i in range(MH * NT + 3):
                h, qt = divmod(i, NT)
                if i < MH * NT:
                    product(("Sm", i), lambda b: [
                        (b[:, 0:MT], [(QmT[:, 2 * h + d, columns(qt)], KmT[:, 2 * h + d, :]) for d in range(2)])])
                if 2 <= i < MH * NT + 2:
                    pe.wait_ge(mp_done, i - 1)
                    turn(("PTm", i - 2), lambda b: [(b[:, columns(k)], Pmm[i % 2][:, columns(k)]) for k in range(2)])
                if i >= 3 and (i - 3) % NT == NT - 1:
                    g = (i - 3) // NT
                    for n in range(NT):
                        await_drained(pe, ("PTm", NT * g + n))
                    for d in range(2):
                        product(("Om", g, d), lambda b: [
                            (b[:, :], [(Vm[:, k, columns(2 * g + d)], PTm[g % 2][:, k, :]) for k in range(2)])])
            for h in range(MH):
                for d in range(2):
                    await_drained(pe, ("Om", h, d))
            token_major("mo", OmT)
            pe.wait_ge(xn_done, before[4])
            for k in range(KD):
                turn(("pT", k), lambda b: [(b[:, columns(t)], xn[:, t, columns(k)]) for t in range(NT)])
            for k in range(KD):
                await_drained(pe, ("pT", k))

            def queries(h, s, first=False):
                if first and s == 0:
                    await_slab(pe, ("pq", 0))
                elif s == 0:
                    pe.wait_ge(qw_in, h * 16)
                for k in range(KD):
                    ins = pe.matmul(ps[4 + s][:, :], qw[:, k, columns(s)], FT[:, k, :], start=(k == 0), stop=(k == KD - 1))
                ins.then_inc(q_filled, 1)

            def scores(h, s, first=False):
                pe.wait_ge(q_copied, h * 2 + (s + 1))
                if not first:
                    pe.wait_ge(s_copied, h)
                for t in range(NT):
                    keys = keysT[:, s, :] if first else keysT[:, bass.ds(h * 2 + s, 1), :].rearrange("p a n -> p (a n)")
                    ins = pe.matmul(ps[6 + s][:, columns(t)], qhs[s][:, columns(t)], keys, start=True, stop=True)
                ins.then_inc(s_filled, 1)

            def group(g, t, taken=True):
                if taken:
                    pe.wait_ge(acc_taken, g - 1)
                for s in range(TOPK):
                    pe.wait_ge(ld_v[s], (g + 1) * 16)
                    pe.wait_ge(diag_done, g * TOPK + (s + 1))
                    for n in range(2):
                        last = pe.matmul(ps[2 * (t % 2) + n][:, :], diag[s % DRING], Vb[s][:, 512 * n:512 * n + 512],
                                         start=(s == 0), stop=(s == TOPK - 1))
                    last.then_inc(v_summed, 1)

            def head(h, first=False, last=False):
                for t in range(NT):
                    if t < 2 and not last:
                        queries(h + 1, t)
                        scores(h + 1, t)
                    group(h * NT + t, t, taken=not first or t >= 2)

            for q in range(4):
                await_drained(pe, ("keyT", q))
            for b in range(8):
                pe.wait_ge(drained[b], uses[b])
            queries(0, 0, first=True)
            queries(0, 1, first=True)
            scores(0, 0, first=True)
            scores(0, 1, first=True)
            head(0, first=True)
            with pe.Fori(1, PH - 1) as h:
                head(h)
            head(PH - 1, last=True)

        @block.gpsimd
        def _(pool):
            own = [0]

            def step(ins):
                own[0] += 1
                ins.then_inc(c_pool, 1)
                pool.wait_ge(c_pool, own[0])

            def tt(out, a, b, op):
                step(pool.tensor_tensor(out, a, b, op))

            pool.memset(ones[:, :], 1.0).then_inc(ones_set, 1)
            for r, w in enumerate((ssm_c_re, ssm_c_im)):
                for d in range(2):
                    pool.dma_start(Craw[r][:, :, 64 * d:64 * d + 64],
                                 w[0, d].rearrange("(b g) c p -> (g c) b p", b=NB)).then_inc(d_ssm, 16)
            for r, w in enumerate((ssm_b_re, ssm_b_im)):
                for d in range(2):
                    pool.dma_start(bb[r][64 * d:64 * d + 64, :, :],
                                 w[0, d].rearrange("g p c -> p g c")).then_inc(d_ssm, 16)
            step(pool.memset(mask, 1.0))
            step(pool.memset(mask[0:64, 0:1], 0.0))
            step(pool.memset(mask[64:128, M - 1:M], 0.0))
            for r in range(2):
                step(pool.memset(EXT[r], 0.0))
                step(pool.memset(Sst[r], 0.0))
            pool.sem_inc(zeros_set, 1)
            pool.wait_ge(trig_done, 3)
            one, two = (sm[:, 14, :], sm[:, 15, :]), (sm[:, 66, :], sm[:, 72, :])
            step(pool.tensor_copy(one[0], sm[:, 7, :]))
            step(pool.tensor_copy(one[1], sm[:, 8, :]))
            step(pool.tensor_scalar(one[1][64:128, :], sm[64:128, 8, :], -1.0, None, ALU.mult))

            def square(dst, src):
                t0, t1 = sm[:, 13, :], sm[:, 95, :]
                tt(t0, src[0], src[0], ALU.mult)
                tt(t1, src[1], src[1], ALU.mult)
                tt(dst[0], t0, t1, ALU.subtract)
                tt(t0, src[0], src[1], ALU.mult)
                tt(dst[1], t0, t0, ALU.add)

            square(two, one)
            square(one, two)
            square(two, one)
            levels = [(sm[:, 66 + n, :], sm[:, 72 + n, :]) for n in range(6)]
            for n in range(5):
                square(levels[n + 1], levels[n])
            await_full(pool, ("xT", KD - 1))
            step(pool.memset(Tre[:, :, 0:1], 1.0))
            step(pool.memset(Tim[:, :, 0:1], 0.0))
            for n in range(6):
                w = 1 << n
                tmp = [Hf[:, 1024 * i:1024 * i + G * w].rearrange("p (g m) -> p g m", g=G) for i in range(2)]
                lr, li = (levels[n][r].unsqueeze(2).to_broadcast([P, G, w]) for r in range(2))
                tr, tim = Tre[:, :, 0:w], Tim[:, :, 0:w]
                tt(tmp[0], tr, lr, ALU.mult)
                tt(tmp[1], tim, li, ALU.mult)
                tt(Tre[:, :, w:2 * w], tmp[0], tmp[1], ALU.subtract)
                tt(tmp[0], tr, li, ALU.mult)
                tt(tmp[1], tim, lr, ALU.mult)
                tt(Tim[:, :, w:2 * w], tmp[0], tmp[1], ALU.add)
            pool.sem_inc(table_done, 1)
            pool.wait_ge(pow_done, 1)
            for q in range(NB):
                if q >= 2:
                    await_full(pool, ("Y", q - 2))
                for half in range(2):
                    lo = GB * q + NB * half
                    gs, ws = slice(lo, lo + NB), slice(NB * half, NB * half + NB)
                    pr, pi = (sm[:, 50 + 8 * r:58 + 8 * r, gs].rearrange("p k g -> p g k").unsqueeze(3)
                              .to_broadcast([P, NB, CH, CG]) for r in range(2))
                    cr, ci = (c[:, gs, :].unsqueeze(2).to_broadcast([P, NB, CH, CG]) for c in (Cc[0], negC))
                    wre, wim = (w[:, ws] for w in Wst[q % 2])
                    tt(wre, pr, cr, ALU.mult)
                    tt(Wtmp, pi, ci, ALU.mult)
                    tt(wre, wre, Wtmp, ALU.add)
                    tt(wim, pr, ci, ALU.mult)
                    tt(Wtmp, pi, cr, ALU.mult)
                    tt(wim, wim, Wtmp, ALU.subtract)
                pool.sem_inc(w_done, 1)

            def gather(dst, table, ix, s, signal):
                pool.sem_inc(apart_pool, 1)
                pool.indirect_dma_start(out=dst, out_offset=None, in_=table,
                                        in_offset=bass.IndirectOffsetOnAxis(ap=ix[:, s:s + 1], axis=0)).then_inc(signal, 16)

            def u_row(g, t, s, first=False):
                if not first or s >= URING:
                    pool.wait_ge(dots, g * TOPK + (s - (URING - 1)))
                gather(Ub[s % URING], peer_u, idx[t], s, ld_u[s % URING])

            def v_row(g, t, s, first=False):
                if not first:
                    pool.wait_ge(v_summed, g * TOPK + (s - (VRING - 1)))
                gather(Vb[s], peer_v, idx[t], s, ld_v[s])

            def head(h, first=False, last=False):
                for t in range(NT):
                    g = h * NT + t
                    more = not last or t < NT - 1
                    if more:
                        pool.wait_ge(idx_ready, g + 2)
                    for s in range(TOPK):
                        if more:
                            u_row(g + 1, (t + 1) % NT, s)
                        if not first or t:
                            v_row(g, t, s)

            await_drained(pool, ("pT", KD - 1))
            await_full(pool, ("mo", 3, 1))
            pool.wait_ge(idx_ready, 1)
            for s in range(URING):
                u_row(0, 0, s, first=True)
            for s in range(VRING):
                v_row(0, 0, s, first=True)
            for s in range(URING, TOPK):
                u_row(0, 0, s, first=True)
            head(0, first=True)
            with pool.Fori(1, PH - 1) as h:
                head(h)
            head(PH - 1, last=True)


NAMES = ["x", "mem", "positions", "g_mix", "w_in", "b_gate", "ssm_lam_re", "ssm_lam_im", "ssm_log_dt",
         "ssm_b_re", "ssm_b_im", "ssm_c_re", "ssm_c_im", "ssm_d", "w_ssm_glu", "g_q_lora", "w_uq",
         "g_kv_lora", "w_ukv", "w_mla_o", "w_out", "g_mem_q", "g_mem_kv", "w_mem_q", "w_mem_kv",
         "w_mem_o", "g_peer", "w_peer_q", "peer_sub_keys", "peer_u", "peer_v", "g_final"]
WEIGHTS = {"w_in", "w_ssm_glu", "w_uq", "w_ukv", "w_mla_o", "w_out", "w_mem_q", "w_mem_kv", "w_mem_o",
           "w_peer_q", "peer_u", "peer_v"}


def kernel(**inputs):
    import concourse.bacc as bacc
    from concourse.bass_utils import run_bass_kernel_spmd

    nc = bacc.Bacc("TRN2", target_bir_lowering=False, num_devices=1)
    arrays = {n: np.ascontiguousarray(inputs[n]) for n in NAMES}
    for n in WEIGHTS:
        arrays[n] = arrays[n].reshape(arrays[n].shape[1:])
    arrays["consts"] = host_constants()
    args = [nc.dram_tensor(f"in_{n}", a.shape, mybir.dt.from_np(a.dtype), kind="ExternalInput").ap()
            for n, a in arrays.items()]
    out = nc.dram_tensor("out_0", (1, T, D), F32, kind="ExternalOutput").ap()
    encoder_layer(nc, *args, out)
    r = run_bass_kernel_spmd(nc, [{f"in_{n}": a for n, a in arrays.items()}], core_ids=[0])
    return r.results[0]["out_0"]
```

```python
import math
from contextlib import ExitStack

import numpy as np

import concourse.bass as bass
import concourse.mybir as mybir

F32 = mybir.dt.float32
F32R = mybir.dt.float32r
I32 = mybir.dt.int32
U32 = mybir.dt.uint32
ALU = mybir.AluOpType
ACT = mybir.ActivationFunctionType
AX = mybir.AxisListType

P = 128
T, D = 512, 1024
NT, KD = T // P, D // P
EPS = 1e-6
SW, G, CG = 512, 32, 16
CH = P // CG
M = T // CH
LAGS = 2 * CH - 1
GB = 8
NB = G // GB
NH, NOPE, ROPE, HV = 8, 64, 32, 64
QL, KVL = 384, 256
QD = NOPE + ROPE
MT, MH, MD = 256, 4, 256
PH, NK, KH, TOPK = 8, 128, 128, 16
NHS = 2 * PH
NG = NT * PH

VEC = {}
_at = 0
for _n, _w in (("g_mix", 8), ("g_mem_q", 8), ("g_mem_kv", 8), ("g_peer", 8), ("b_gate", 16),
               ("g_q_lora", 3), ("g_kv_lora", 2)):
    VEC[_n] = (_at, _w)
    _at += _w
NVEC = _at

C_ID, C_IOTA, C_ROPE = 0, P, P + 16
NCONST = C_ROPE + 4

NEG = -3.0e38
TWO_PI = 2 * math.pi
PI_HI = 6.28125
PI_MID = round((TWO_PI - PI_HI) * 2 ** 20) / 2 ** 20
PI_LO = TWO_PI - PI_HI - PI_MID
ROUND = 1.5 * 2 ** 23
PI_CLAMP = 3.1415925
SLOTS = 3
TOPK_STEPS = 25
SLAB = 2048
URING, VRING = 8, TOPK
DRING = 8


def host_constants():
    c = np.zeros((P, NCONST), np.float32)
    c[:, C_ID:C_ID + P] = np.eye(P, dtype=np.float32)
    c[:, C_IOTA:C_IOTA + 16] = np.arange(16, dtype=np.float32)
    freq = 1.0 / (np.float32(10000.0) ** (np.arange(0, ROPE, 2, dtype=np.float32) / np.float32(ROPE)))
    c[:, C_ROPE] = freq.astype(np.float32)[np.arange(P) % 16]
    cos_rows = slice(64, 96)
    c[cos_rows, C_ROPE + 1] = 0.25
    c[cos_rows, C_ROPE + 2] = math.pi / 2
    c[:, C_ROPE + 3] = 1.0
    c[96:112, C_ROPE + 3] = -1.0
    return c


LATENT_JOBS = [(("cq", 0), 0, 0), (("cq", 1), 0, 128), (("cq", 2), 1, 0),
               (("ckv", 0), 1, 128), (("ckv", 1), 2, 0), (("kr",), 2, 128)]


def psum_jobs():
    j = [("vec",), ("par",)]
    j += [("xT", k) for k in range(KD)]
    j += [("u", q) for q in range(4)] + [("C", 0), ("C", 1)]
    j += [("uT", q) for q in range(G // 4)]

    def latents(n):
        return [key for key, _, _ in LATENT_JOBS[2 * n:2 * n + 2]]

    def prep(b):
        return [("bT", b, r, s) for r in range(2) for s in range(2)] + [("D", b, s) for s in range(NB)]

    j += latents(0) + prep(0) + [("X", 0, 0), ("X", 0, 1)]
    for b in range(NB):
        if b + 1 < NB:
            j += latents(b + 1) + prep(b + 1) + [("X", b + 1, 0), ("X", b + 1, 1)]
        else:
            j += [("kvn",), ("qn",)]
        j += [("Y", b)]
    j += [("yt", q) for q in range(G // 4)] + [("yT", f) for f in range(4)]
    j += [("V", kt) for kt in range(NT)] + [("Q", 0), ("K", 0)]
    for i in range(NH * NT + 3):
        h, qt = divmod(i, NT)
        if i < NH * NT:
            j.append(("S", i))
        if 2 <= i < NH * NT + 2:
            j.append(("PT", i - 2))
        if qt == 2 and h + 1 < NH:
            j += [("Q", h + 1)] + [("K", h + 1)] * (h % 2)
        if i >= 3 and (i - 3) % NT == NT - 1:
            j.append(("O", (i - 3) // NT))
    for i in range(KD):
        j += [("gs", i), ("gm", i), ("val", i), ("gate", i), ("mla", i)]
    j += [("out", n, p) for n in range(4) for p in range(2)]
    j += [("mT", k) for k in range(KD)] + [("Km", m) for m in range(4)]
    j += [("Vm", n) for n in range(4)] + [("keyT", q) for q in range(4)]
    j += [("hT", k) for k in range(KD)] + [("Qm", m) for m in range(KD)]
    for i in range(MH * NT + 3):
        if i < MH * NT:
            j.append(("Sm", i))
        if 2 <= i < MH * NT + 2:
            j.append(("PTm", i - 2))
        if i >= 3 and (i - 3) % NT == NT - 1:
            j += [("Om", (i - 3) // NT, d) for d in range(2)]
    j += [("mo", n, p) for n in range(4) for p in range(2)]
    j += [("p0", 0), ("p0", 1), ("q0", 0), ("q0", 1), ("s0",)]
    j += [("pT", k) for k in range(KD)]
    return j


def split_units():
    u = []
    for i in range(KD):
        u += [(("gs", i), [("gs", i)], False), (("gm", i), [("gm", i)], False),
              (("glu", i), [("val", i), ("gate", i)], False), (("mla", i), [("mla", i)], False)]
    u += [(("out", n), [("out", n, 0), ("out", n, 1)], True) for n in range(4)]
    u += [(("mk", n), [("Km", n)], True) for n in range(4)]
    u += [(("mv", n), [("Vm", n)], True) for n in range(4)]
    u += [(("mq", m), [("Qm", m)], False) for m in range(KD)]
    u += [(("mo", n), [("mo", n, 0), ("mo", n, 1)], True) for n in range(4)]
    return u


def slab_plan():
    s = [(("u", 0), ("u", 3)), (("u", 1), ("u", 3)),
         (("c", 0), ("cq", 1)), (("c", 1), ("ckv", 0)), (("c", 2), ("kr",)),
         (("ukv",), ("K", NH - 2))]
    for i in range(KD):
        s.append((("gates", i), ("split", "gm", i)))
        s.append((("mix", i), ("split", "mla", i)))
    for kind in ("out", "mk", "mv"):
        s += [((kind, n), ("split", kind, n)) for n in range(4)]
    s += [(("mq", n), ("split", "mq", 2 * n + 1)) for n in range(4)]
    s += [(("mo", n), ("split", "mo", n)) for n in range(4)]
    s.append((("pq", 0), ("pT", KD - 1)))
    return s


def rows(w, lo, hi):
    return w[:, lo:hi].rearrange("(k p) n -> p k n", p=P)


def encoder_layer(nc, x, mem, positions, g_mix, w_in, b_gate, ssm_lam_re, ssm_lam_im, ssm_log_dt,
                  ssm_b_re, ssm_b_im, ssm_c_re, ssm_c_im, ssm_d, w_ssm_glu, g_q_lora, w_uq,
                  g_kv_lora, w_ukv, w_mla_o, w_out, g_mem_q, g_mem_kv, w_mem_q, w_mem_kv, w_mem_o,
                  g_peer, w_peer_q, peer_sub_keys, peer_u, peer_v, g_final, consts, out):
    ctx = ExitStack()
    with ctx:
        def sb(name, *shape, dt=F32):
            return ctx.enter_context(nc.sbuf_tensor(name, list(shape), dt))

        def sem(name):
            return ctx.enter_context(nc.semaphore(name))

        cst = sb("cst", P, NCONST)
        ident = cst[:, C_ID:C_ID + P]
        iota16 = cst[:, C_IOTA:C_IOTA + 16]
        ones = sb("ones", P, P)
        vecrow = sb("vecrow", NVEC, P)
        vec = sb("vec", P, NVEC)
        stat = sb("stat", P, 104)
        H = sb("H", P, NT, D)

        def shared(name, n, alias):
            with nc.sbuf_tensor(name, [P, n], F32) as plain:
                pass
            return plain, sb(alias, P, n, dt=F32R)

        XN, XNr = shared("XN", NT * D, "XNr")
        FTm, FTr = shared("FT", KD * T, "FTr")
        FT = FTm[:, :].rearrange("p (k t) -> p k t", k=KD)
        slabs = sb("slabs", P, SLOTS * SLAB)
        WS, WSr = shared("WS", 2 * SLAB, "WSr")
        R, Rr = shared("R", 28416, "Rr")
        xn = XN[:, :].rearrange("p (t d) -> p t d", t=NT)

        def reg(lo, *shape, base=R, parts=P):
            n = int(np.prod(shape))
            v = base[0:parts, lo:lo + n]
            names = "abcd"[:len(shape)]
            if len(shape) > 1:
                v = v.rearrange(f"p ({' '.join(names)}) -> p {' '.join(names)}",
                                **dict(zip(names, shape)))
            return v

        Hf = H[:, :, :].rearrange("p t d -> p (t d)")
        U = reg(0, G, M)
        cqT, ckvT = reg(2048, 3, T), reg(3584, 2, T)
        VB = [reg(4608, GB, CH, CG), reg(5632, GB, CH, CG)]
        bb = [reg(6656, G, CG), reg(7168, G, CG)]
        Cc = [reg(7680, G, CG), reg(8192, G, CG)]
        EXT = [reg(8704, GB, LAGS, CG), reg(10624, GB, LAGS, CG)]
        Wtmp = reg(27456, NB, CH, CG)
        BT = [reg(12544, GB, P), reg(13568, GB, P)]
        DTm = reg(14592, GB, P)
        t4 = [reg(16640 + 512 * i, GB * M) for i in range(4)]
        ta, tb = reg(16640, GB, CH, CG), reg(17664, GB, CH, CG)
        Z = [reg(18688, GB * M), reg(19200, GB * M)]
        Zs = [reg(15616, GB * M), reg(16128, GB * M)]
        Sst = [reg(19712, GB, M), reg(20224, GB, M)]
        M8 = reg(20736, GB, M)
        Tim = reg(21248, G, M)
        Craw = [reg(18688, NB, P), reg(19200, NB, P)]
        sm = reg(23296, 96, G)
        krT = reg(26368, T)
        mask = reg(26880, M)
        negC = reg(26944, G, CG)
        parrow = [reg(27456 + 128 * i, P, parts=G) for i in range(4)]
        drow = reg(27968, P, parts=G)
        dtrow = reg(28096, 2, parts=G)
        Wst = [[m[:, at + 1024 * r:at + 1024 * (r + 1)].rearrange("p (g j c) -> p g j c", g=GB, j=CH)
                for r in range(2)] for m, at in ((Hf, 0), (Hf, 2048), (WS, 0), (WS, 2048))]
        ustage = XN[:, 0:2048].rearrange("p (g q c) -> p g q c", g=G, q=4)
        lags = XN[0:CG, 0:GB * LAGS * CG].rearrange("p (g l c) -> p g l c", g=GB, l=LAGS)
        ytok = XN[0:M, :].rearrange("p (j n) -> p j n", j=CH)
        Tre = XN[:, 2048:4096].rearrange("p (g m) -> p g m", g=G)
        yTs = [reg(0, 4, T, base=Rr), reg(22528, 4, T, base=Rr)]
        FTs = [XNr[:, :].rearrange("p (k t) -> p k t", k=KD), FTr[:, :].rearrange("p (k t) -> p k t", k=KD)]
        wuq = reg(4608, 3, NH, P)
        V = reg(7680, NT, NH * HV)
        OTs = [reg(9728, 4, T, base=Rr), reg(26368, 4, T, base=Rr)]
        posb = reg(11776, T).bitcast(I32)
        TAB = reg(12288, T)
        tA, tB, tC = reg(12800, T), reg(13312, T), reg(13824, T)
        QT = [reg(14336, T), reg(14848, T)]
        KT = [reg(at, T) for at in (15360, 15872, 24576, 25088)]
        Pm = [reg(16384, T), reg(16896, T)]
        PT = [reg(17408, NT, T), reg(19456, NT, T)]
        lat = [reg(21504, T), reg(22016, T)]
        latsq = Hf[:, 0:5 * T].rearrange("p (k t) -> p k t", k=5)
        mixtmp = [[reg(16384 + 512 * (5 * q + i), T) for i in range(5)] for q in range(2)]
        mixTs = [reg(12288, KD, T, base=Rr), reg(4608, KD, T, base=Rr)]
        memx = reg(0, 2, D)
        memTs = [reg(26368, KD, MT, base=Rr), reg(22528, KD, MT, base=Rr)]
        KmT, Vm = reg(2048, KD, MT), reg(9728, 2, D)
        hTs = [FTs[1], reg(4608, KD, T, base=Rr)]
        QmT = reg(12288, KD, T)
        OmTs = [reg(4608, KD, T, base=Rr), reg(24320, KD, T, base=Rr)]
        Pmm = [reg(16384, MT), reg(16640, MT)]
        PTm = [reg(16896, 2, T), reg(17920, 2, T)]
        keyraw = reg(18944, NHS, KH)
        keysT = reg(20992, NHS, NK)
        qhs = [reg(0, T), reg(512, T)]
        SC = reg(1024, NT, 2, NK)
        Vb = [reg(3072 + D * i, D) for i in range(VRING)]
        diag = [reg(19456 + P * i, P) for i in range(DRING)]
        gprow = reg(23040, D)
        gfrow = reg(24064, D)
        prod = reg(25088, D)
        sc1, cand1 = reg(26112, NK), reg(26368, TOPK * TOPK)
        cand = reg(26624, TOPK * TOPK)
        eq = reg(26880, 2 * TOPK, TOPK)
        tv = reg(27392, 2, TOPK)
        ti = reg(27424, 2, TOPK).bitcast(U32)
        tif = reg(27456, 2, TOPK)
        cv = reg(27488, TOPK)
        cpos = reg(27504, TOPK).bitcast(U32)
        cpp = reg(27520, 2 * TOPK).bitcast(U32)
        cpf = reg(27552, 2 * TOPK)
        isel = reg(27584, 2 * TOPK)
        nmx, esum, rinv = reg(27616, 1), reg(27617, 1), reg(27618, 1)
        ex = reg(27632, TOPK)
        idx = [reg(27648 + TOPK * i, TOPK).bitcast(U32) for i in range(NT)]
        gate = [reg(27712 + TOPK * i, TOPK) for i in range(2)]
        wgt = [reg(27744 + TOPK * i, TOPK) for i in range(2)]
        act_row = reg(27776, TOPK)
        gel = reg(27792, TOPK)
        junk = reg(17408, D)

        ps = [ctx.enter_context(nc.psum_tensor(f"bank{i}", [P, 512], F32)) for i in range(8)]

        filled = [sem(f"filled{i}") for i in range(8)]
        drained = [sem(f"drained{i}") for i in range(8)]
        slab_in = [sem(f"slab_in{i}") for i in range(SLOTS)]
        ld_u = [sem(f"ld_u{i}") for i in range(URING)]
        ld_v = [sem(f"ld_v{i}") for i in range(VRING)]
        d_cst, d_vec, d_par, d_ssm = [sem(n) for n in ("d_cst", "d_vec", "d_par", "d_ssm")]
        d_x = [sem(f"d_x{t}") for t in range(NT)]
        d_res, d_wuq, d_pos, d_mem, d_key = [sem(n) for n in ("d_res", "d_wuq", "d_pos", "d_mem", "d_key")]
        d_grow, d_out, d_within = sem("d_grow"), sem("d_out"), sem("d_within")
        c_dve, c_act, c_pool, c_loop = [sem(n) for n in ("c_dve", "c_act", "c_pool", "c_loop")]
        sq_done, var_done, std_done, xn_done = [sem(n) for n in ("sq_done", "var_done", "std_done", "xn_done")]
        ones_set, zeros_set, par_rows = [sem(n) for n in ("ones_set", "zeros_set", "par_rows")]
        args_done, trig_done, table_done = [sem(n) for n in ("args_done", "trig_done", "table_done")]
        vb_done, ext_done, w_done, s_done, yg_done, pow_done = [
            sem(n) for n in ("vb_done", "ext_done", "w_done", "s_done", "yg_done", "pow_done")]
        lat_sq, lat_var, lat_std, lat_done = [sem(n) for n in ("lat_sq", "lat_var", "lat_std", "lat_done")]
        rope_arg, rope_sin, kr_done, qk_done = [sem(n) for n in ("rope_arg", "rope_sin", "kr_done", "qk_done")]
        negmax, p_done = sem("negmax"), sem("p_done")
        mix_done = sem("mix_done")
        x_hi, f_hi, f_lo = sem("x_hi"), sem("f_hi"), sem("f_lo")
        w_hi, w_lo = sem("w_hi"), sem("w_lo")
        mnegmax, mp_done = sem("mnegmax"), sem("mp_done")
        qw_in, q_filled, q_copied, s_filled, s_copied = [
            sem(n) for n in ("qw_in", "q_filled", "q_copied", "s_filled", "s_copied")]
        idx_ready, gates_neg, gates_exp = [sem(n) for n in ("idx_ready", "gates_neg", "gates_exp")]
        dots, gelu_done, w_ready, diag_done, v_summed = [
            sem(n) for n in ("dots", "gelu_done", "w_ready", "diag_done", "v_summed")]
        acc_taken, final_done = sem("acc_taken"), sem("final_done")
        apart_dve, apart_pool = sem("apart_dve"), sem("apart_pool")

        jobs = psum_jobs()
        place = {k: (i % 8, i // 8) for i, k in enumerate(jobs)}
        assert len(place) == len(jobs)
        uses = [sum(1 for i in range(len(jobs)) if i % 8 == b) for b in range(8)]

        def take(pe, key):
            b, n = place[key]
            if n:
                pe.wait_ge(drained[b], n)
            return ps[b]

        def full(key):
            return filled[place[key][0]]

        def await_full(eng, key):
            b, n = place[key]
            eng.wait_ge(filled[b], n + 1)
            return ps[b]

        def empty(key):
            return drained[place[key][0]]

        def await_drained(eng, key):
            b, n = place[key]
            eng.wait_ge(drained[b], n + 1)

        plan = slab_plan()
        slab_no = {k: i for i, (k, _) in enumerate(plan)}

        def slab(key, *shape):
            s = (slab_no[key] % SLOTS) * SLAB
            n = int(np.prod(shape))
            return slabs[:, s:s + n].rearrange("p (k n) -> p k n", k=shape[0])

        def slab_parts(key):
            kind = key[0]
            if kind == "u":
                return [(slab(key, 8, 256), rows(w_in, 256 * key[1], 256 * key[1] + 256))]
            if kind == "c" and key[1] < 2:
                lo = SW + 256 * key[1]
                return [(slab(key, 8, 256), rows(w_in, lo, lo + 256))]
            if kind == "c":
                lo = SW + 512
                kr = lo + 128
                s = slab(key, 8, 256)
                parts = [(s[:, :, 0:128], rows(w_in, lo, lo + 128))]
                for i in range(2):
                    at = 128 + 64 * i
                    parts += [(s[:, :, at:at + 32], rows(w_in, kr, kr + 32)),
                              (s[:, :, at + 32:at + 48], rows(w_in, kr + 16, kr + 32)),
                              (s[:, :, at + 48:at + 64], rows(w_in, kr, kr + 16))]
                return parts
            if kind == "ukv":
                s = slab(key, 2, 1024)
                w = w_ukv.rearrange("(k p) (h c n) -> p k c h n", p=P, c=2, n=NOPE)
                return [(s[:, k, 512 * c:512 * c + 512].rearrange("p (h n) -> p h n", h=NH), w[:, k, c])
                        for k in range(2) for c in range(2)]
            if kind == "mix":
                lo = P * key[1]
                s = slab(key, 4, 3 * P)
                return [(s[:, :, 0:P], rows(w_ssm_glu, lo, lo + P)),
                        (s[:, :, P:2 * P], rows(w_ssm_glu, D + lo, D + lo + P)),
                        (s[:, :, 2 * P:3 * P], rows(w_mla_o, lo, lo + P))]
            if kind == "gates":
                lo = SW + QL + KVL + ROPE + 128 * key[1]
                s = slab(key, 8, 256)
                return [(s[:, :, 0:128], rows(w_in, lo, lo + 128)),
                        (s[:, :, 128:256], rows(w_in, lo + D, lo + D + 128))]
            w, lo = {"out": (w_out, 0), "mk": (w_mem_kv, 0), "mv": (w_mem_kv, D), "mq": (w_mem_q, 0),
                     "mo": (w_mem_o, 0), "pq": (w_peer_q, 0)}[kind]
            lo += 256 * key[1]
            return [(slab(key, 8, 256), rows(w, lo, lo + 256))]

        slab_need, had = [], [0] * SLOTS
        for n, (key, _) in enumerate(plan):
            had[n % SLOTS] += 16 * len(slab_parts(key))
            slab_need.append(had[n % SLOTS])

        def await_slab(pe, key):
            n = slab_no[key]
            pe.wait_ge(slab_in[n % SLOTS], slab_need[n])

        units = split_units()
        unit_no = {k: i for i, (k, _, _) in enumerate(units)}

        def unit(key):
            kind, i = key
            whole = units[unit_no[key]][2]
            if kind in ("glu", "mla"):
                src = slab(("mix", i), 4, 3 * P)[:, :, 0:2 * P] if kind == "glu" else slab(("mix", i), 4, 3 * P)[:, :, 2 * P:]
            elif kind in ("gs", "gm"):
                src = slab(("gates", i), 8, 256)[:, :, P * (kind == "gm"):P * (kind == "gm") + P]
            elif kind == "mq":
                src = slab(("mq", i // 2), 8, 256)[:, :, P * (i % 2):P * (i % 2) + P]
            else:
                src = slab((kind, i), 8, 256)
            n = int(np.prod(src.shape[1:]))
            no = unit_no[key]
            if whole:
                base, at, step = (FTr, WSr)[no % 2], 0, SLAB
            else:
                base, at, step = WSr, SLAB * (no % 2), SLAB // 2
            return src, [base[:, at + step * q:at + step * q + n].rearrange("p (k n) -> p k n", k=src.shape[1])
                         for q in range(2)]

        def unit_slab(key):
            kind, i = key
            return {"glu": ("mix", i), "mla": ("mix", i), "gs": ("gates", i), "gm": ("gates", i),
                    "mq": ("mq", i // 2)}.get(kind, key)

        def await_place(eng, no):
            key, _, whole = units[no]
            if no == 0:
                return
            if key == ("out", 0):
                await_full(eng, ("gm", KD - 1))
            elif whole != units[no - 1][2] or key == ("out", 1):
                await_full(eng, units[no - 1 - (key == ("out", 1))][1][-1])
            elif no >= 2:
                await_full(eng, units[no - 2][1][-1])

        qw = slab(("pq", 0), 8, 256)
        Ub = [slabs[:, D * i:D * i + D] for i in range(2 * SLOTS)
              if i // 2 != slab_no[("pq", 0)] % SLOTS] + [WS[:, D * i:D * i + D] for i in range(4)]
        assert len(Ub) == URING

        block = ctx.enter_context(nc.Block())

        @block.sync
        def _(sp):
            sp.dma_start(cst[:, :], consts).then_inc(d_cst, 16)
            for t in range(NT):
                sp.dma_start(xn[:, t, :], x[0, P * t:P * t + P, :]).then_inc(d_x[t], 16)
            for name, w in (("g_mix", g_mix), ("g_mem_q", g_mem_q), ("g_mem_kv", g_mem_kv),
                            ("g_peer", g_peer), ("b_gate", b_gate), ("g_q_lora", g_q_lora),
                            ("g_kv_lora", g_kv_lora)):
                lo, n = VEC[name]
                sp.dma_start(vecrow[lo:lo + n, :], w[0].rearrange("(k p) -> k p", p=P)).then_inc(d_vec, 16)
            for i, w in enumerate((ssm_lam_re, ssm_lam_im)):
                sp.dma_start(parrow[i].rearrange("g (d p) -> g d p", d=2),
                             w[0].rearrange("d g p -> g d p")).then_inc(d_par, 16)
            sp.dma_start(dtrow, ssm_log_dt[0].rearrange("d g -> g d"), allow_slow_non_contiguous=True).then_inc(d_par, 16)
            sp.dma_start(drow[:, 0:CG], ssm_d[0].rearrange("(g c) -> g c", g=G)).then_inc(d_par, 16)

            def load_slab(n):
                key = plan[n][0]
                if n >= SLOTS:
                    last = plan[n - SLOTS][1]
                    if last[0] == "split":
                        sp.wait_ge(w_lo, unit_no[last[1:]] + 1)
                    else:
                        await_full(sp, last)
                for dst, src in slab_parts(key):
                    sp.dma_start(dst, src).then_inc(slab_in[n % SLOTS], 16)

            for n in range(SLOTS):
                load_slab(n)
            for n in range(SLOTS, 5):
                load_slab(n)
            for q in range(NB):
                await_drained(sp, ("D", q, NB - 1))
                if q:
                    await_full(sp, ("Y", q - 1))
                for s in range(CH):
                    sp.dma_start(DTm[CG * s:CG * s + CG, :, :],
                                 lags[:, :, CH - 1 - s:2 * CH - 1 - s, :].rearrange("p g l c -> p g (l c)")
                                 ).then_inc(d_within, 16)
                if q == 0:
                    load_slab(5)
            await_full(sp, ("Y", NB - 1))
            for k in range(3):
                src = w_uq[P * k:P * k + P, :].rearrange("p (h n) -> p h n", h=NH)
                sp.dma_start(wuq[:, k, :, 0:QD], src).then_inc(d_wuq, 16)
                sp.dma_start(wuq[:, k, :, QD:QD + 16], src[:, :, NOPE + 16:QD]).then_inc(d_wuq, 16)
                sp.dma_start(wuq[:, k, :, QD + 16:P], src[:, :, NOPE:NOPE + 16]).then_inc(d_wuq, 16)
            sp.dma_start(posb, positions[0].partition_broadcast(P)).then_inc(d_pos, 16)
            sp.dma_start(H[:, :, :], x[0].rearrange("(t p) d -> p t d", p=P)).then_inc(d_res, 16)
            for n in range(6, len(plan)):
                if plan[n][0] == ("mk", 0):
                    sp.wait_ge(mix_done, KD)
                    sp.dma_start(memx, mem[0].rearrange("(t p) d -> p t d", p=P)).then_inc(d_mem, 16)
                    sp.dma_start(keyraw, peer_sub_keys[0].rearrange("h s n d -> n (h s) d")).then_inc(d_key, 16)
                load_slab(n)
            await_full(sp, ("mo", 3, 1))
            sp.dma_start(gprow, g_peer[0].partition_broadcast(P)).then_inc(d_grow, 16)
            sp.dma_start(gfrow, g_final.partition_broadcast(P)).then_inc(d_grow, 16)
            with sp.Fori(1, PH) as h:
                sp.wait_ge(q_filled, h * 2)
                sp.dma_start(qw, w_peer_q[:, bass.ds(h * 256, 256)].rearrange("(k p) n -> p k n", p=P)).then_inc(qw_in, 16)
            for t in range(NT):
                sp.wait_ge(final_done, t + 1)
                sp.dma_start(out[0, P * t:P * t + P, :], xn[:, t, :]).then_inc(d_out, 16)
            sp.wait_ge(d_out, 16 * NT)


        NORMS = (NT, 2, NT, NT, NT)
        before = [sum(NORMS[:k]) for k in range(6)]
        PARTS = [(0, (0, 1, 2, 3)), (1, (0, 1)), (2, (0, 1)), (2, (2, 3)), (3, (0,)), (3, (1, 2, 3))]

        def sumsq(k, t):
            return stat[:, 16 * k + t:16 * k + t + 1]

        @block.scalar
        def _(act):
            own = [0]

            def settle(ins):
                own[0] += 1
                ins.then_inc(c_act, 1)
                act.wait_ge(c_act, own[0])

            def copy_out(key, dst, src, scale=1.0):
                act.activation(dst, src, ACT.Copy, scale=scale).then_inc(empty(key), 1)

            def squares(part, src, scratch, kind=None):
                k, tiles = PARTS[part]
                for t in tiles:
                    if part == 0:
                        act.wait_ge(d_x[t], 16)
                    if kind:
                        for n in range(4):
                            await_drained(act, (kind, n, t // 2))
                    settle(act.activation(scratch, src[:, t, :], ACT.Square, accum_out=sumsq(k, t)))
                act.sem_inc(sq_done, 1)
                act.wait_ge(var_done, part + 1)
                lo, hi = 16 * k + tiles[0], 16 * k + tiles[-1] + 1
                act.activation(stat[:, 8 + lo:8 + hi], stat[:, 4 + lo:4 + hi], ACT.Sqrt).then_inc(std_done, 1)

            def high(key, dst, src, scale=1.0):
                act.activation(dst, src, ACT.Copy, scale=scale).then_inc(x_hi, 1)

            def split(no):
                if no >= len(units):
                    return
                src, (hi, lo) = unit(units[no][0])
                await_slab(act, unit_slab(units[no][0]))
                await_place(act, no)
                act.activation(hi, src, ACT.Copy).then_inc(w_hi, 1)

            def features(name, key, dst, width, parts=False):
                for k in range(KD):
                    b = await_full(act, (key, k))
                    c = VEC[name][0] + k
                    (high if parts else copy_out)((key, k), dst[:, k, :], b[:, 0:width], scale=vec[:, c:c + 1])

            squares(0, xn, FT[:, 0:2, :].rearrange("p k t -> p (k t)"))
            act.wait_ge(d_par, 64)
            settle(act.activation(dtrow, dtrow, ACT.Exp))
            for d in range(2):
                settle(act.activation(parrow[2][:, 64 * d:64 * d + 64],
                                      dtrow[:, d:d + 1].to_broadcast([G, 64]), ACT.Copy))
            act.activation(parrow[3].rearrange("g (j c) -> g j c", j=CH),
                           drow[:, 0:CG].unsqueeze(1).to_broadcast([G, CH, CG]), ACT.Copy).then_inc(par_rows, 1)
            await_drained(act, ("vec",))
            for k in range(0, KD, 2):
                b = await_full(act, ("xT", k))
                c = VEC["g_mix"][0] + k
                copy_out(("xT", k), FT[:, k, :], b[:, :], scale=vec[:, c:c + 1])
            act.wait_ge(args_done, 1)
            act.activation(sm[:, 6, :], sm[:, 4, :], ACT.Exp).then_inc(trig_done, 1)
            act.activation(sm[:, 12, :], sm[:, 4, :], ACT.Exp, scale=float(CH)).then_inc(trig_done, 1)
            act.activation(sm[:, 7:9, :], sm[:, 10:12, :], ACT.Sin).then_inc(trig_done, 1)
            for q in range(4):
                b = await_full(act, ("u", q))
                copy_out(("u", q), ustage[:, :, q, :], b[:, :].rearrange("p (g c) -> p g c", g=G))
            for r in range(2):
                b = await_full(act, ("C", r))
                copy_out(("C", r), Cc[r].rearrange("p g c -> p (g c)"), b[:, :])
            for q in range(G // 4):
                b = await_full(act, ("uT", q))
                src = b[0:64, :].rearrange("p (g m j) -> p g j m", g=4, j=2)
                settle(act.activation(U[0:64, 4 * q:4 * q + 4, :], src[:, :, 0, :], ACT.Copy))
                copy_out(("uT", q), U[64:128, 4 * q:4 * q + 4, :], src[:, :, 1, :])
            def latent(key):
                dst = krT if key == ("kr",) else (cqT if key[0] == "cq" else ckvT)[:, key[1], :]
                b = await_full(act, key)
                copy_out(key, dst, b[:, :])

            def windows(q):
                act.wait_ge(w_done, q + 1)
                act.wait_ge(zeros_set, 1)
                if q:
                    await_full(act, ("D", q - 1, NB - 1))
                for r, c in enumerate((Cc[0], negC)):
                    w = Wst[q][r]
                    act.activation(EXT[r][:, :, CH - 1, :], c[:, GB * q:GB * q + GB, :], ACT.Copy).then_inc(ext_done, 1)
                    act.activation(EXT[r][0:64, :, CH:, :].rearrange("p g j c -> p g (j c)"),
                                   w[0:64, :, 0:CH - 1, :].rearrange("p g j c -> p g (j c)"), ACT.Copy).then_inc(ext_done, 1)
                    act.activation(EXT[r][64:128, :, 0:CH - 1, :].rearrange("p g j c -> p g (j c)"),
                                   w[64:128, :, 1:, :].rearrange("p g j c -> p g (j c)"), ACT.Copy).then_inc(ext_done, 1)

            def block_prep(q):
                if q:
                    await_full(act, ("X", q - 1, 1))
                for r in range(2):
                    for s in range(2):
                        b = await_full(act, ("bT", q, r, s))
                        copy_out(("bT", q, r, s), BT[r][:, 4 * s:4 * s + 4, :].rearrange("p g n -> p (g n)"), b[:, :])
                if q:
                    act.wait_ge(d_within, 16 * CH * q)
                for s in range(NB):
                    b = await_full(act, ("D", q, s))
                    copy_out(("D", q, s), lags[:, 2 * s:2 * s + 2, :, :].rearrange("p g l c -> p (g l c)"),
                             b[0:CG, 0:2 * LAGS * CG])

            def gelu(q):
                await_drained(act, ("Y", q))
                yq = U[:, GB * q:GB * q + GB, :]
                act.activation(yq, yq, ACT.Gelu_apprx_tanh).then_inc(yg_done, 1)

            for key, _, _ in LATENT_JOBS[0:2]:
                latent(key)
            windows(0)
            block_prep(0)
            for q in range(NB):
                if q + 1 < NB:
                    windows(q + 1)
                    for key, _, _ in LATENT_JOBS[2 * q + 2:2 * q + 4]:
                        latent(key)
                    block_prep(q + 1)
                else:
                    for m in range(3):
                        act.activation(latsq[:, m, :], cqT[:, m, :], ACT.Square).then_inc(lat_sq, 1)
                    for m in range(2):
                        act.activation(latsq[:, 3 + m, :], ckvT[:, m, :], ACT.Square).then_inc(lat_sq, 1)
                    for k in range(2):
                        act.wait_ge(lat_var, k + 1)
                        act.activation(lat[k], lat[k], ACT.Sqrt).then_inc(lat_std, 1)
                if q:
                    gelu(q - 1)
            gelu(NB - 1)
            act.wait_ge(s_done, 4 * NB)
            for q in range(G // 4):
                b = await_full(act, ("yt", q))
                for g in range(4):
                    ins = act.activation(ytok[:, :, 64 * q + 16 * g:64 * q + 16 * g + 16],
                                         b[0:M, P * g:P * g + P].rearrange("p (j c) -> p j c", j=CH), ACT.Copy)
                ins.then_inc(empty(("yt", q)), 1)
            for f in range(4):
                b = await_full(act, ("yT", f))
                high(("yT", f), yTs[0][:, f, :].rearrange("p (m j) -> p j m", j=CH),
                     b[:, :].rearrange("p (j m) -> p j m", j=CH))
            act.wait_ge(rope_arg, 1)
            act.activation(TAB, tA, ACT.Sin).then_inc(rope_sin, 1)
            for kt in range(NT):
                b = await_full(act, ("V", kt))
                copy_out(("V", kt), V[:, kt, :], b[:, :])

            def head_in(h):
                b = await_full(act, ("Q", h))
                if h >= 2:
                    await_full(act, ("S", NT * (h - 1) - 1))
                copy_out(("Q", h), QT[h % 2], b[:, :])
                if h % 2 == 0:
                    b = await_full(act, ("K", h))
                    if h >= 4:
                        await_full(act, ("S", NT * (h - 2) - 1))
                    settle(act.activation(KT[h % 4][0:64, :], b[0:64, :], ACT.Copy))
                    copy_out(("K", h), KT[(h + 1) % 4][0:64, :], b[64:128, :])

            def exponentials(i, key, width, bufs, negs, scale, base, tkey):
                b = await_full(act, (key, i))
                act.wait_ge(negs, i + 1)
                if i >= 2:
                    await_full(act, (tkey, i - 2))
                act.activation(bufs[i % 2], b[:, 0:width], ACT.Exp, scale=scale,
                               bias=stat[:, base + i % 4:base + i % 4 + 1],
                               accum_out=stat[:, base + 4 + i % 4:base + 5 + i % 4]).then_inc(empty((key, i)), 1)

            head_in(0)
            for i in range(NH * NT + 3):
                if i < NH * NT:
                    exponentials(i, "S", T, Pm, negmax, QD ** -0.5, 80, "PT")
                if 2 <= i < NH * NT + 2:
                    h, qt = divmod(i - 2, NT)
                    if qt % 2:
                        b = await_full(act, ("PT", i - 2))
                        if h >= 2:
                            await_full(act, ("O", h - 2))
                        copy_out(("PT", i - 2), PT[h % 2][:, :, P * qt:P * qt + P],
                                 b[:, :].rearrange("p (k q) -> p k q", k=NT))
                if i % NT == 2 and i // NT + 1 < NH:
                    head_in(i // NT + 1)
                if i >= 3 and (i - 3) % NT == NT - 1:
                    h = (i - 3) // NT
                    b = await_full(act, ("O", h))
                    high(("O", h), OTs[0][64 * (h % 2):64 * (h % 2) + 64, h // 2, :], b[0:HV, :])
                if i % 4 == 0 and 4 <= i <= 16:
                    for f in range(4):
                        await_full(act, ("yT", f))
                    k = 2 * (i // 4 - 1)
                    act.activation(FTs[0][:, k:k + 2, :], FT[:, k:k + 2, :], ACT.Copy).then_inc(f_hi, 1)
                if i == 20:
                    split(0)
                if i == 24:
                    split(1)
            for i in range(KD):
                s = mixtmp[i % 2]
                if i >= 2:
                    act.wait_ge(mix_done, i - 1)
                for n, kind in enumerate(("gs", "gm")):
                    b = await_full(act, (kind, i))
                    c = VEC["b_gate"][0] + KD * n + i
                    act.activation(s[1 + n], b[:, :], ACT.Sigmoid,
                                   bias=vec[:, c:c + 1]).then_inc(empty((kind, i)), 1)
                    split(4 * i + 2 + n)
                b = await_full(act, ("gate", i))
                act.activation(s[0], b[:, :], ACT.Sigmoid).then_inc(empty(("gate", i)), 1)
                split(4 * i + 4)
                split(4 * i + 5)
            for n in range(2, 6):
                split(unit_no[("out", 0)] + n)
                if n == 3:
                    act.wait_ge(d_mem, 16)
                    squares(1, memx, junk)
            features("g_mem_kv", "mT", memTs[0], MT, parts=True)
            for part in (2, 3):
                squares(part, H, junk, "out")
            for n in range(2, 4):
                split(unit_no[("mk", 0)] + n)
            for n in range(4):
                split(unit_no[("mv", 0)] + n)
            split(unit_no[("mq", 0)])
            split(unit_no[("mq", 1)])
            for q in range(4):
                b = await_full(act, ("keyT", q))
                copy_out(("keyT", q), keysT[:, 4 * q:4 * q + 4, :].rearrange("p k n -> p (k n)"), b[:, :])
            features("g_mem_q", "hT", hTs[0], T, parts=True)
            for m in range(KD):
                b = await_full(act, ("Qm", m))
                copy_out(("Qm", m), QmT[:, m, :], b[:, :])
                if m + 2 < KD:
                    split(unit_no[("mq", m + 2)])
            for i in range(MH * NT + 3):
                if i < MH * NT:
                    exponentials(i, "Sm", MT, Pmm, mnegmax, MD ** -0.5, 92, "PTm")
                if i in (3, 7):
                    split(unit_no[("mo", i // 4)])
                if i >= 3 and (i - 3) % NT == NT - 1:
                    h = (i - 3) // NT
                    for d in range(2):
                        b = await_full(act, ("Om", h, d))
                        high(("Om", h, d), OmTs[0][:, 2 * h + d, :], b[:, :])
            split(unit_no[("mo", 2)])
            split(unit_no[("mo", 3)])
            for part in (4, 5):
                squares(part, H, junk, "mo")
            for half in range(2):
                b = await_full(act, ("p0", half))
                for n in range(4):
                    c = VEC["g_peer"][0] + 4 * half + n
                    ins = act.activation(FT[:, 4 * half + n, 0:P], b[:, P * n:P * n + P], ACT.Copy, scale=vec[:, c:c + 1])
                ins.then_inc(empty(("p0", half)), 1)
            for s in range(2):
                b = await_full(act, ("q0", s))
                copy_out(("q0", s), qhs[s][:, 0:P], b[:, 0:P])
            for k in range(KD):
                b = await_full(act, ("pT", k))
                c = VEC["g_peer"][0] + k
                copy_out(("pT", k), FT[:, k, P:T], b[:, P:T], scale=vec[:, c:c + 1])

            def queries_out(h, s, first=False):
                act.wait_ge(q_filled, h * 2 + (s + 1))
                if not first:
                    act.wait_ge(s_filled, h * 2 + (s - 1))
                cols = slice(P if first else 0, T)
                act.activation(qhs[s][:, cols], ps[4 + s][:, cols], ACT.Copy).then_inc(q_copied, 1)

            def gate_exponentials(g):
                act.wait_ge(gates_neg, g + 1)
                act.activation(ex, cv, ACT.Exp, bias=nmx, accum_out=esum).then_inc(gates_exp, 1)

            def gelu_of(g):
                act.wait_ge(dots, (g + 1) * TOPK)
                act.activation(gel, act_row, ACT.Gelu_apprx_tanh).then_inc(gelu_done, 1)

            def diagonals(g, t, first=False, slots=range(TOPK)):
                act.wait_ge(w_ready, g + 1)
                for s in slots:
                    if not first or s >= DRING:
                        act.wait_ge(v_summed, g * TOPK + (s - DRING + 1))
                    act.activation(diag[s % DRING], ident, ACT.Copy,
                                   scale=wgt[t % 2][:, s:s + 1]).then_inc(diag_done, 1)

            def head(h, first=False, last=False):
                for t in range(NT):
                    g = h * NT + t
                    if t < 2 and not last:
                        queries_out(h + 1, t)
                    if not last or t < 2:
                        gate_exponentials(g + 2)
                    if last and t == NT - 1:
                        diagonals(g, t, slots=range(DRING))
                        final_root(0)
                        final_root(1)
                        diagonals(g, t, slots=range(DRING, TOPK))
                    else:
                        diagonals(g, t, first and t == 0)
                    if not last or t < NT - 1:
                        gelu_of(g + 1)

            def final_root(t):
                act.wait_ge(var_done, len(PARTS) + t + 1)
                act.activation(stat[:, 72 + t:73 + t], stat[:, 68 + t:69 + t], ACT.Sqrt).then_inc(std_done, 1)

            queries_out(0, 0, True)
            queries_out(0, 1, True)
            gate_exponentials(0)
            gate_exponentials(1)
            gelu_of(0)
            head(0, first=True)
            with act.Fori(1, PH - 1) as h:
                head(h)
            head(PH - 1, last=True)
            final_root(2)
            final_root(3)

        @block.vector
        def _(dve):
            own = [0]

            def step(ins):
                own[0] += 1
                ins.then_inc(c_dve, 1)
                dve.wait_ge(c_dve, own[0])

            def tt(out, a, b, op):
                step(dve.tensor_tensor(out, a, b, op))

            def signal(ins, s, n):
                ins.then_inc(s, 1)
                dve.wait_ge(s, n)

            highs = [0]

            def low(key, dst, src, hi, scale=None):
                highs[0] += 1
                dve.wait_ge(x_hi, highs[0])
                if scale is None:
                    ins = dve.tensor_tensor(dst, src, hi, ALU.subtract)
                else:
                    ins = dve.scalar_tensor_tensor(dst, src, scale, hi, ALU.mult, ALU.subtract)
                ins.then_inc(empty(key), 1)

            def low_features(name, key, parts, width):
                for k in range(KD):
                    b = await_full(dve, (key, k))
                    c = VEC[name][0] + k
                    low((key, k), parts[1][:, k, :], b[:, 0:width], parts[0][:, k, :], vec[:, c:c + 1])

            def split(no):
                if no >= len(units):
                    return
                src, (hi, lo) = unit(units[no][0])
                await_slab(dve, unit_slab(units[no][0]))
                await_place(dve, no)
                dve.wait_ge(w_hi, no + 1)
                dve.tensor_tensor(lo, src, hi, ALU.subtract).then_inc(w_lo, 1)

            def normalise(part, src, dst):
                k, tiles = PARTS[part]
                lo, hi = 16 * k + tiles[0], 16 * k + tiles[-1] + 1
                dve.wait_ge(sq_done, part + 1)
                dve.tensor_scalar(stat[:, 4 + lo:4 + hi], stat[:, lo:hi], 1.0 / D, EPS,
                                  ALU.mult, ALU.add).then_inc(var_done, 1)
                dve.wait_ge(std_done, part + 1)
                step(dve.reciprocal(stat[:, 12 + lo:12 + hi], stat[:, 8 + lo:8 + hi]))
                for t in tiles:
                    c = stat[:, 16 * k + 12 + t:16 * k + 13 + t]
                    dve.tensor_scalar(dst[:, t, :], src[:, t, :], c, None, ALU.mult).then_inc(xn_done, 1)

            def reduce_turns(src, dst, n, turn=0.0, angle=0.0):
                step(dve.tensor_scalar(n, src, 1.0 / TWO_PI, turn, ALU.mult, ALU.add))
                step(dve.tensor_scalar(n, n, ROUND, -ROUND, ALU.add, ALU.add))
                step(dve.scalar_tensor_tensor(dst, n, -PI_HI, src, ALU.mult, ALU.add))
                step(dve.scalar_tensor_tensor(dst, n, -PI_MID, dst, ALU.mult, ALU.add))
                step(dve.scalar_tensor_tensor(dst, n, -PI_LO, dst, ALU.mult, ALU.add))
                step(dve.tensor_scalar(dst, dst, angle, PI_CLAMP, ALU.add, ALU.min))
                step(dve.tensor_scalar(dst, dst, -PI_CLAMP, None, ALU.max))

            for t in range(NT):
                dve.wait_ge(d_x[t], 16)
            normalise(0, xn, xn)
            b = await_full(dve, ("vec",))
            dve.tensor_copy(vec[:, :], b[:, 0:NVEC]).then_inc(empty(("vec",)), 1)
            b = await_full(dve, ("par",))
            dve.tensor_copy(sm[:, 0:4, :].rearrange("p a g -> p (a g)"), b[:, 0:4 * G]).then_inc(empty(("par",)), 1)
            await_drained(dve, ("par",))
            lre, lim, dt, dsk = (sm[:, i, :] for i in range(4))
            tt(sm[:, 4, :], lre, dt, ALU.mult)
            tt(sm[:, 5, :], lim, dt, ALU.mult)
            reduce_turns(sm[:, 5, :], sm[:, 10, :], sm[:, 9, :], 0.25, math.pi / 2)
            reduce_turns(sm[:, 5, :], sm[:, 11, :], sm[:, 9, :])
            dve.sem_inc(args_done, 1)
            for k in range(1, KD, 2):
                b = await_full(dve, ("xT", k))
                c = VEC["g_mix"][0] + k
                dve.tensor_scalar(FT[:, k, :], b[:, :], vec[:, c:c + 1], None, ALU.mult).then_inc(empty(("xT", k)), 1)
            dve.wait_ge(trig_done, 3)
            mag, co, si = sm[:, 6, :], sm[:, 7, :], sm[:, 8, :]

            def pw(r, k):
                return sm[:, 16 + 9 * r + k, :]

            step(dve.memset(pw(0, 0), 1.0))
            step(dve.memset(pw(1, 0), 0.0))
            tt(pw(0, 1), mag, co, ALU.mult)
            tt(pw(1, 1), mag, si, ALU.mult)

            def cmul(o, a, b, tmp):
                tt(tmp[0], a[0], b[0], ALU.mult)
                tt(tmp[1], a[1], b[1], ALU.mult)
                tt(o[0], tmp[0], tmp[1], ALU.subtract)
                tt(tmp[0], a[0], b[1], ALU.mult)
                tt(tmp[1], a[1], b[0], ALU.mult)
                tt(o[1], tmp[0], tmp[1], ALU.add)

            n = 1
            while n < CH:
                def span(r, lo, m):
                    return sm[:, 16 + 9 * r + lo:16 + 9 * r + lo + m, :]
                top = [pw(r, n).unsqueeze(1).to_broadcast([P, n, G]) for r in range(2)]
                cmul([span(r, n + 1, n) for r in range(2)], [span(r, 1, n) for r in range(2)], top,
                     [sm[:, 78:78 + n, :], sm[:, 86:86 + n, :]])
                n *= 2
            for r in range(2):
                px, py = 34 + 8 * r, 50 + 8 * r
                base = 16 + 9 * r
                for k in range(CH):
                    step(dve.tensor_copy(sm[0:64, px + k, :], sm[0:64, base + CH - 1 - k, :]))
                    step(dve.tensor_copy(sm[64:128, py + k, :], sm[64:128, base + CH - k, :]))
                step(dve.tensor_copy(sm[64:128, px:px + CH, :], sm[64:128, base:base + CH, :]))
                step(dve.tensor_copy(sm[0:64, py:py + CH, :], sm[0:64, base + 1:base + 1 + CH, :]))
            step(dve.tensor_scalar(sm[:, 94, :], pw(0, 1), -1.0, None, ALU.add))
            tt(sm[:, 78, :], lre, lre, ALU.mult)
            tt(sm[:, 79, :], lim, lim, ALU.mult)
            tt(sm[:, 80, :], sm[:, 78, :], sm[:, 79, :], ALU.add)
            step(dve.reciprocal(sm[:, 81, :], sm[:, 80, :]))
            tt(sm[:, 82, :], sm[:, 94, :], lre, ALU.mult)
            tt(sm[:, 83, :], pw(1, 1), lim, ALU.mult)
            tt(sm[:, 84, :], sm[:, 82, :], sm[:, 83, :], ALU.add)
            tt(sm[:, 84, :], sm[:, 84, :], sm[:, 81, :], ALU.mult)
            tt(sm[:, 82, :], pw(1, 1), lre, ALU.mult)
            tt(sm[:, 83, :], sm[:, 94, :], lim, ALU.mult)
            tt(sm[:, 85, :], sm[:, 82, :], sm[:, 83, :], ALU.subtract)
            tt(sm[:, 85, :], sm[:, 85, :], sm[:, 81, :], ALU.mult)
            dve.wait_ge(d_ssm, 16 * 8)
            fr, fi = (sm[:, 84 + r, :].unsqueeze(2).to_broadcast([P, G, CG]) for r in range(2))
            tg = [t.rearrange("p (g c) -> p g c", g=G) for t in t4]
            tt(tg[0], bb[0], fr, ALU.mult)
            tt(tg[1], bb[1], fi, ALU.mult)
            tt(tg[2], bb[1], fr, ALU.mult)
            tt(tg[3], bb[0], fi, ALU.mult)
            tt(bb[0], tg[0], tg[1], ALU.subtract)
            tt(bb[1], tg[2], tg[3], ALU.add)
            await_drained(dve, ("C", 0))
            await_drained(dve, ("C", 1))
            signal(dve.tensor_scalar(negC, Cc[1], -1.0, None, ALU.mult), pow_done, 1)

            def contributions(q):
                gs = slice(GB * q, GB * q + GB)
                if q:
                    await_full(dve, ("bT", q - 1, 1, 1))
                pr, pi = (sm[:, 34 + 8 * r:42 + 8 * r, gs].rearrange("p k g -> p g k").unsqueeze(3)
                          .to_broadcast([P, GB, CH, CG]) for r in range(2))
                br, bi = (bb[r][:, gs, :].unsqueeze(2).to_broadcast([P, GB, CH, CG]) for r in range(2))
                tt(ta, pr, br, ALU.mult)
                tt(tb, pi, bi, ALU.mult)
                signal(dve.tensor_tensor(VB[0], ta, tb, ALU.subtract), vb_done, 2 * q + 1)
                tt(ta, pr, bi, ALU.mult)
                tt(tb, pi, br, ALU.mult)
                signal(dve.tensor_tensor(VB[1], ta, tb, ALU.add), vb_done, 2 * q + 2)

            def outputs(q):
                gs = slice(GB * q, GB * q + GB)
                b = await_full(dve, ("Y", q))
                skip = t4[0].rearrange("p (g m) -> p g m", g=GB)
                tt(skip, U[:, gs, :], dsk[:, gs].unsqueeze(2).to_broadcast([P, GB, M]), ALU.mult)
                dve.tensor_tensor(U[:, gs, :], b[:, :].rearrange("p (g m) -> p g m", g=GB), skip,
                                  ALU.add).then_inc(empty(("Y", q)), 1)
                await_drained(dve, ("Y", q))

            def scaled_latents(k):
                first, n, src, name = ((0, 2, ckvT, "g_kv_lora"), (2, 3, cqT, "g_q_lora"))[k]
                dve.wait_ge(lat_std, k + 1)
                step(dve.reciprocal(lat[k], lat[k]))
                for m in range(n):
                    c = VEC[name][0] + m
                    signal(dve.scalar_tensor_tensor(src[:, m, :], src[:, m, :], vec[:, c:c + 1], lat[k],
                                                    ALU.mult, ALU.mult), lat_done, first + m + 1)

            contributions(0)
            dve.wait_ge(table_done, 1)
            for q in range(NB):
                if q + 1 < NB:
                    contributions(q + 1)
                gs = slice(GB * q, GB * q + GB)
                tc, ts = (t[:, gs, :].rearrange("p g m -> p (g m)") for t in (Tre, Tim))
                tt(M8, mask.unsqueeze(1).to_broadcast([P, GB, M]),
                   sm[:, 12, gs].unsqueeze(2).to_broadcast([P, GB, M]), ALU.mult)
                xr = await_full(dve, ("X", q, 0))
                xi = await_full(dve, ("X", q, 1))
                tt(t4[0], xr[:, :], tc, ALU.mult)
                tt(t4[2], xr[:, :], ts, ALU.mult)
                dve.sem_inc(empty(("X", q, 0)), 1)
                tt(t4[1], xi[:, :], ts, ALU.mult)
                tt(t4[3], xi[:, :], tc, ALU.mult)
                dve.sem_inc(empty(("X", q, 1)), 1)
                tt(Z[0], t4[0], t4[1], ALU.add)
                tt(Z[1], t4[3], t4[2], ALU.subtract)
                m8 = M8.rearrange("p g m -> p (g m)")
                for r in range(2):
                    step(dve.tensor_tensor_scan(Zs[r][0:64, :], m8[0:64, :], Z[r][0:64, :], 0.0, ALU.mult, ALU.add))
                    step(dve.tensor_tensor_scan(Zs[r][64:128, ::-1], m8[64:128, ::-1], Z[r][64:128, ::-1], 0.0,
                                                ALU.mult, ALU.add))
                tt(t4[0], Zs[0], tc, ALU.mult)
                tt(t4[1], Zs[1], ts, ALU.mult)
                tt(t4[2], Zs[0], ts, ALU.mult)
                tt(t4[3], Zs[1], tc, ALU.mult)
                if q:
                    await_full(dve, ("Y", q - 1))
                tv4 = [t.rearrange("p (g m) -> p g m", g=GB) for t in t4]
                for r, op in ((0, ALU.subtract), (1, ALU.add)):
                    for lo, dst, src in ((0, slice(1, M), slice(0, M - 1)), (64, slice(0, M - 1), slice(1, M))):
                        dve.tensor_tensor(Sst[r][lo:lo + 64, :, dst], tv4[2 * r][lo:lo + 64, :, src],
                                          tv4[2 * r + 1][lo:lo + 64, :, src], op).then_inc(s_done, 1)
                dve.wait_ge(s_done, 4 * (q + 1))
                if q == NB - 1:
                    for k, (key, n) in enumerate(((("kvn",), KVL), (("qn",), QL))):
                        b = await_full(dve, key)
                        dve.tensor_scalar(lat[k], b[:, :], 1.0 / n, EPS, ALU.mult, ALU.add).then_inc(empty(key), 1)
                        await_drained(dve, key)
                        dve.sem_inc(lat_var, 1)
                    scaled_latents(0)
                if q:
                    outputs(q - 1)
            outputs(NB - 1)
            scaled_latents(1)

            for f in range(4):
                b = await_full(dve, ("yT", f))
                low(("yT", f), yTs[1][:, f, :].rearrange("p (m j) -> p j m", j=CH),
                    b[:, :].rearrange("p (j m) -> p j m", j=CH), yTs[0][:, f, :].rearrange("p (m j) -> p j m", j=CH))
            dve.wait_ge(d_pos, 16)
            step(dve.tensor_copy(tC, posb))
            step(dve.tensor_scalar(tC, tC, cst[:, C_ROPE:C_ROPE + 1], None, ALU.mult))
            step(dve.tensor_scalar(tB, tC, 1.0 / TWO_PI, cst[:, C_ROPE + 1:C_ROPE + 2], ALU.mult, ALU.add))
            step(dve.tensor_scalar(tB, tB, ROUND, -ROUND, ALU.add, ALU.add))
            step(dve.scalar_tensor_tensor(tA, tB, -PI_HI, tC, ALU.mult, ALU.add))
            step(dve.scalar_tensor_tensor(tA, tB, -PI_MID, tA, ALU.mult, ALU.add))
            step(dve.scalar_tensor_tensor(tA, tB, -PI_LO, tA, ALU.mult, ALU.add))
            step(dve.tensor_scalar(tA, tA, cst[:, C_ROPE + 2:C_ROPE + 3], PI_CLAMP, ALU.add, ALU.min))
            signal(dve.tensor_scalar(tA, tA, -PI_CLAMP, None, ALU.max), rope_arg, 1)
            dve.wait_ge(rope_sin, 1)
            step(dve.tensor_scalar(TAB, TAB, cst[:, C_ROPE + 3:C_ROPE + 4], None, ALU.mult))

            def turn(src, dsts):
                step(dve.tensor_tensor(tA[64:96, :], src[64:96, :], TAB[64:96, :], ALU.mult))
                step(dve.tensor_tensor(tB[64:96, :], src[96:128, :], TAB[96:128, :], ALU.mult))
                return [dve.tensor_tensor(d[64:96, :], tA[64:96, :], tB[64:96, :], ALU.add) for d in dsts]

            for n, ins in enumerate(turn(krT, KT)):
                ins.then_inc(kr_done, 1)
            dve.wait_ge(kr_done, 4)

            def head_in(h):
                await_drained(dve, ("Q", h))
                signal(turn(QT[h % 2], [QT[h % 2]])[0], qk_done, h + 1)

            def row_max(i, key, width, negs, scale, base):
                b = await_full(dve, (key, i))
                c = stat[:, base + i % 4:base + i % 4 + 1]
                step(dve.tensor_reduce(c, b[:, 0:width], AX.X, ALU.max))
                dve.tensor_scalar(c, c, -scale, None, ALU.mult).then_inc(negs, 1)

            def normal(i, key, bufs, done, base):
                await_drained(dve, (key, i))
                c = stat[:, base + 8 + i % 4:base + 9 + i % 4]
                step(dve.reciprocal(c, stat[:, base + 4 + i % 4:base + 5 + i % 4]))
                dve.tensor_scalar(bufs[i % 2], bufs[i % 2], c, None, ALU.mult).then_inc(done, 1)

            head_in(0)
            for i in range(NH * NT + 3):
                if i < NH * NT:
                    row_max(i, "S", T, negmax, QD ** -0.5, 80)
                if 1 <= i <= NH * NT:
                    normal(i - 1, "S", Pm, p_done, 80)
                if 2 <= i < NH * NT + 2:
                    h, qt = divmod(i - 2, NT)
                    if qt % 2 == 0:
                        b = await_full(dve, ("PT", i - 2))
                        if h >= 2:
                            await_full(dve, ("O", h - 2))
                        dve.tensor_copy(PT[h % 2][:, :, P * qt:P * qt + P],
                                        b[:, :].rearrange("p (k q) -> p k q", k=NT)).then_inc(empty(("PT", i - 2)), 1)
                if i % NT == 2 and i // NT + 1 < NH:
                    head_in(i // NT + 1)
                if i >= 3 and (i - 3) % NT == NT - 1:
                    h = (i - 3) // NT
                    b = await_full(dve, ("O", h))
                    rows64 = slice(64 * (h % 2), 64 * (h % 2) + 64)
                    low(("O", h), OTs[1][rows64, h // 2, :], b[0:HV, :], OTs[0][rows64, h // 2, :])
                if i % 4 == 1 and 5 <= i <= 17:
                    k = 2 * (i // 4 - 1)
                    dve.wait_ge(f_hi, i // 4)
                    dve.tensor_tensor(FTs[1][:, k:k + 2, :], FT[:, k:k + 2, :], FTs[0][:, k:k + 2, :],
                                      ALU.subtract).then_inc(f_lo, 1)
                if i == 21:
                    split(0)
                if i == 25:
                    split(1)
            for i in range(KD):
                s = mixtmp[i % 2]
                split(4 * i + 2)
                split(4 * i + 3)
                b = await_full(dve, ("val", i))
                await_drained(dve, ("gate", i))
                dve.tensor_tensor(s[3], b[:, :], s[0], ALU.mult).then_inc(empty(("val", i)), 1)
                split(4 * i + 4)
                await_drained(dve, ("val", i))
                await_drained(dve, ("gs", i))
                tt(s[3], s[3], s[1], ALU.mult)
                b = await_full(dve, ("mla", i))
                await_drained(dve, ("gm", i))
                dve.tensor_tensor(s[4], b[:, :], s[2], ALU.mult).then_inc(empty(("mla", i)), 1)
                await_drained(dve, ("mla", i))
                tt(s[4], s[3], s[4], ALU.add)
                step(dve.tensor_copy(mixTs[0][:, i, :], s[4]))
                dve.tensor_tensor(mixTs[1][:, i, :], s[4], mixTs[0][:, i, :], ALU.subtract).then_inc(mix_done, 1)
                split(4 * i + 5)

            def residual(kind, part):
                for n in range(4):
                    for p in range(2):
                        b = await_full(dve, (kind, n, p))
                        h = H[:, 2 * p:2 * p + 2, 256 * n:256 * n + 256]
                        dve.tensor_tensor(h, b[:, :].rearrange("p (t n) -> p t n", t=2), h,
                                          ALU.add).then_inc(empty((kind, n, p)), 1)
                    if kind == "out":
                        split(unit_no[("out", 0)] + n + 2)
                        if n == 1:
                            normalise(1, memx, memx)
                    elif n < 2:
                        if n == 0:
                            dve.wait_ge(w_lo, unit_no[("mo", 2)])
                        split(unit_no[("mo", 2)] + n)
                if kind == "out":
                    low_features("g_mem_kv", "mT", memTs, MT)
                for p in range(2):
                    for n in range(4):
                        await_drained(dve, (kind, n, p))
                    normalise(part + p, H, xn)

            dve.wait_ge(d_res, 16)
            residual("out", 2)
            for n in range(4):
                b = await_full(dve, ("Km", n))
                dve.tensor_copy(KmT[:, 2 * n:2 * n + 2, :].rearrange("p m t -> p (m t)"), b[:, :]).then_inc(empty(("Km", n)), 1)
                split(unit_no[("mk", 0)] + n + 2)
            for n in range(4):
                b = await_full(dve, ("Vm", n))
                dve.tensor_copy(Vm[:, :, 256 * n:256 * n + 256],
                                b[:, :].rearrange("p (t n) -> p t n", t=2)).then_inc(empty(("Vm", n)), 1)
                split(unit_no[("mv", 0)] + n + 2)
            low_features("g_mem_q", "hT", hTs, T)
            for m in range(2, KD):
                split(unit_no[("mq", m)])
            for i in range(MH * NT + 3):
                if i < MH * NT:
                    row_max(i, "Sm", MT, mnegmax, MD ** -0.5, 92)
                if 1 <= i <= MH * NT:
                    normal(i - 1, "Sm", Pmm, mp_done, 92)
                if 2 <= i < MH * NT + 2:
                    h, qt = divmod(i - 2, NT)
                    b = await_full(dve, ("PTm", i - 2))
                    if h >= 2:
                        await_full(dve, ("Om", h - 2, 1))
                    dve.tensor_copy(PTm[h % 2][:, :, P * qt:P * qt + P],
                                    b[:, 0:MT].rearrange("p (k q) -> p k q", k=2)).then_inc(empty(("PTm", i - 2)), 1)
                if i >= 3 and (i - 3) % NT == NT - 1:
                    h = (i - 3) // NT
                    for d in range(2):
                        b = await_full(dve, ("Om", h, d))
                        low(("Om", h, d), OmTs[1][:, 2 * h + d, :], b[:, :], OmTs[0][:, 2 * h + d, :])
            residual("mo", 4)
            dve.wait_ge(d_grow, 32)

            count = [0, 0]

            def lstep(ins, apart=False):
                count[0] += 1
                ins.then_inc(c_loop, 1)
                dve.wait_ge(c_loop, count[1] + count[0])
                if apart:
                    dve.sem_inc(apart_dve, 1)

            def top16(vals, spare, v, ix):
                lstep(dve.max(v[:, 0:8], vals), apart=True)
                lstep(dve.max_index(ix[:, 0:8], v[:, 0:8], vals), apart=True)
                lstep(dve.match_replace(spare, v[:, 0:8], vals, NEG), apart=True)
                lstep(dve.max(v[:, 8:16], spare), apart=True)
                lstep(dve.max_index(ix[:, 8:16], v[:, 8:16], spare), apart=True)

            def scores(h, first=False):
                for s in range(2):
                    dve.wait_ge(s_filled, h * 2 + (s + 1))
                    t0 = 1 if first else 0
                    lstep(dve.tensor_copy(SC[:, t0:, s, :],
                                          ps[6 + s][:, P * t0:].rearrange("p (t n) -> p t n", n=NK)),
                          apart=True)
                dve.sem_inc(s_copied, 1)

            def topk(t):
                dve.sem_inc(apart_dve, 1)
                for s in range(2):
                    top16(SC[:, t, s, :], sc1, tv[:, s, :], ti[:, s, :])
                lstep(dve.tensor_copy(tif, ti))
                lstep(dve.tensor_tensor(cand.rearrange("p (a b) -> p a b", a=TOPK),
                                        tv[:, 0, :].unsqueeze(2).to_broadcast([P, TOPK, TOPK]),
                                        tv[:, 1, :].unsqueeze(1).to_broadcast([P, TOPK, TOPK]), ALU.add), apart=True)
                top16(cand, cand1, cv, cpos)
                lstep(dve.tensor_scalar(nmx, cv[:, 0:1], -1.0, None, ALU.mult))
                dve.sem_inc(gates_neg, 1)
                lstep(dve.tensor_scalar(cpp[:, 0:16], cpos, 4, None, ALU.logical_shift_right))
                lstep(dve.tensor_scalar(cpp[:, 16:32], cpos, 15, None, ALU.bitwise_and))
                lstep(dve.tensor_copy(cpf, cpp))
                lstep(dve.tensor_tensor(eq, iota16.unsqueeze(1).to_broadcast([P, 2 * TOPK, TOPK]),
                                        cpf.unsqueeze(2).to_broadcast([P, 2 * TOPK, TOPK]), ALU.is_equal))
                e4 = eq.rearrange("p (s k) a -> p s k a", s=2)
                lstep(dve.tensor_tensor(e4, e4, tif.unsqueeze(2).to_broadcast([P, 2, TOPK, TOPK]), ALU.mult))
                lstep(dve.tensor_reduce(isel, eq, AX.X, ALU.add))
                lstep(dve.scalar_tensor_tensor(idx[t], isel[:, 0:16], float(NK), isel[:, 16:32], ALU.mult, ALU.add))
                dve.sem_inc(idx_ready, 1)

            def gates_of(g, t):
                dve.wait_ge(gates_exp, g + 1)
                lstep(dve.reciprocal(rinv, esum))
                lstep(dve.tensor_scalar(gate[t % 2], ex, rinv, None, ALU.mult))

            def dot_products(g, t):
                for s in range(TOPK):
                    dve.wait_ge(ld_u[s % URING], (g * 2 + (s // URING + 1)) * 16)
                    dve.tensor_tensor_reduce(prod, Ub[s % URING], xn[:, t, :], 1.0, 0.0, ALU.mult, ALU.add,
                                             act_row[:, s:s + 1]).then_inc(dots, 1)
                    dve.wait_ge(dots, g * TOPK + (s + 1))

            def weights(g, t):
                dve.wait_ge(gelu_done, g + 1)
                lstep(dve.tensor_tensor(wgt[t % 2], gel, gate[t % 2], ALU.mult))
                dve.sem_inc(w_ready, 1)

            def take_sum(g, t):
                dve.wait_ge(v_summed, (g + 1) * TOPK)
                for n in range(2):
                    h = H[:, t, 512 * n:512 * n + 512]
                    lstep(dve.tensor_tensor(h, ps[2 * (t % 2) + n][:, :], h, ALU.add))
                dve.sem_inc(acc_taken, 1)

            def head(h, first=False, last=False):
                for t in range(NT):
                    g = h * NT + t
                    ahead = not last or t < 2
                    if t == 2 and not last:
                        scores(h + 1)
                    if ahead:
                        topk((t + 2) % NT)
                    if not first or t:
                        take_sum(g + (-1), (t - 1) % NT)
                    if not last or t < NT - 1:
                        dot_products(g + 1, (t + 1) % NT)
                        weights(g + 1, (t + 1) % NT)
                    if ahead:
                        gates_of(g + 2, t)

            def final_variance(t):
                step(dve.tensor_tensor_reduce(prod, H[:, t, :], H[:, t, :], 1.0, 0.0, ALU.mult, ALU.add, sumsq(4, t)))
                dve.tensor_scalar(stat[:, 68 + t:69 + t], sumsq(4, t), 1.0 / D, EPS, ALU.mult, ALU.add).then_inc(var_done, 1)

            def final_rows(t):
                dve.wait_ge(std_done, len(PARTS) + t + 1)
                c = stat[:, 76 + t:77 + t]
                step(dve.reciprocal(c, stat[:, 72 + t:73 + t]))
                dve.scalar_tensor_tensor(xn[:, t, :], H[:, t, :], c, gfrow, ALU.mult, ALU.mult).then_inc(final_done, 1)

            b = await_full(dve, ("s0",))
            lstep(dve.tensor_copy(SC[:, 0, :, :], b[:, 0:2 * NK].rearrange("p (s n) -> p s n", s=2)), apart=True)
            dve.sem_inc(empty(("s0",)), 1)
            topk(0)
            await_full(dve, ("pT", KD - 1))
            for t in range(NT):
                step(dve.tensor_tensor(xn[:, t, :], xn[:, t, :], gprow, ALU.mult))
            gates_of(0, 0)
            scores(0, first=True)
            topk(1)
            gates_of(1, 1)
            dot_products(0, 0)
            weights(0, 0)
            head(0, first=True)
            start = count[0]
            per_head = NT * (TOPK_STEPS + 2 + 1 + 2) + 2
            count[0] = 0
            with dve.Fori(1, PH - 1) as h:
                count[1] = (h - 1) * per_head + start
                head(h)
                assert count[0] == per_head, count
            count[1] = start + (PH - 2) * per_head
            count[0] = 0
            head(PH - 1, last=True)
            for t in range(NT - 1):
                final_variance(t)
            for t in range(2):
                final_rows(t)
            take_sum(NG - 1, NT - 1)
            final_variance(NT - 1)
            for t in range(2, NT):
                final_rows(t)

        @block.tensor
        def _(pe):
            def turn(key, pieces):
                b = take(pe, key)
                for dst, src in pieces(b):
                    n = src.shape[0]
                    last = pe.transpose(dst, src, ident[0:n, 0:n])
                last.then_inc(full(key), 1)

            def product(key, groups, ready=None):
                b = take(pe, key)
                for m, (dst, terms) in enumerate(groups(b)):
                    for n, (lhs, rhs) in enumerate(terms):
                        if ready and m == 0 and n * KD % len(terms) == 0:
                            ready(n * KD // len(terms))
                        last = pe.matmul(dst, lhs, rhs, start=(n == 0), stop=(n == len(terms) - 1))
                last.then_inc(full(key), 1)

            def columns(t):
                return slice(P * t, P * t + P)

            def three(lhs, rhs):
                def terms(ks, by_tile=False):
                    pairs = ((0, 0), (1, 0), (0, 1))
                    order = [(k, q) for k in range(ks) for q in pairs] if by_tile else [(k, q) for q in pairs for k in range(ks)]
                    return [(lhs(a, k), rhs(b, k)) for k, (a, b) in order]
                return terms

            pe.wait_ge(d_cst, 16)
            pe.wait_ge(d_vec, 16 * 7)
            turn(("vec",), lambda b: [(b[:, 0:NVEC], vecrow[:, :])])
            pe.wait_ge(par_rows, 1)
            turn(("par",), lambda b: [(b[:, G * i:G * i + G], parrow[i]) for i in range(4)])
            for k in range(KD):
                pe.wait_ge(xn_done, before[1])
                turn(("xT", k), lambda b: [(b[:, columns(t)], xn[:, t, columns(k)]) for t in range(NT)])
            await_slab(pe, ("u", 0))
            await_slab(pe, ("u", 1))
            by_step = [FT[:, k, :].rearrange("p (n q) -> p q n", q=4) for k in range(KD)]
            for q in range(4):
                product(("u", q), lambda b: [
                    (b[:, 256 * n:256 * n + 256],
                     [(by_step[k][:, q, :], slab(("u", n), 8, 256)[:, k, :]) for k in range(KD)])
                    for n in range(2)], None if q else lambda k: await_drained(pe, ("xT", k)))
            pe.wait_ge(d_ssm, 16 * 8)
            for r in range(2):
                turn(("C", r), lambda b: [(b[:, columns(q)], Craw[r][:, q, :]) for q in range(NB)])
            for q in range(4):
                await_drained(pe, ("u", q))
            for q in range(G // 4):
                turn(("uT", q), lambda b: [
                    (b[0:64, columns(g)], ustage[:, 4 * q + g, :, :].rearrange("p q c -> p (q c)")) for g in range(4)])

            def latent(key, s, at):
                await_slab(pe, ("c", s))
                w = slab(("c", s), 8, 256)
                product(key, lambda b: [(b[:, :], [(w[:, k, at:at + 128], FT[:, k, :]) for k in range(KD)])])

            def block_prep(q):
                pe.wait_ge(vb_done, 2 * (q + 1))
                for r in range(2):
                    for s in range(2):
                        turn(("bT", q, r, s), lambda b: [
                            (b[:, columns(g)], VB[r][:, 4 * s + g, :, :].rearrange("p j c -> p (j c)"))
                            for g in range(4)])
                pe.wait_ge(ext_done, 6 * (q + 1))
                for s in range(NB):
                    product(("D", q, s), lambda b: [
                        (b[0:CG, LAGS * CG * g:LAGS * CG * (g + 1)],
                         [(bb[r][:, GB * q + 2 * s + g, :],
                           EXT[r][:, 2 * s + g, :, :].rearrange("p l c -> p (l c)")) for r in range(2)])
                        for g in range(2)])

            def chunk_inputs(q):
                for r in range(2):
                    for s in range(2):
                        await_drained(pe, ("bT", q, r, s))
                for r in range(2):
                    product(("X", q, r), lambda b: [
                        (b[:, M * g:M * g + M], [(BT[r][:, g, :], U[:, GB * q + g, :])]) for g in range(GB)])

            for entry in LATENT_JOBS[0:2]:
                latent(*entry)
            block_prep(0)
            for q in range(G // 4):
                await_drained(pe, ("uT", q))
            chunk_inputs(0)
            for q in range(NB):
                if q + 1 < NB:
                    for entry in LATENT_JOBS[2 * q + 2:2 * q + 4]:
                        latent(*entry)
                    block_prep(q + 1)
                    chunk_inputs(q + 1)
                else:
                    pe.wait_ge(lat_sq, 5)
                    pe.wait_ge(ones_set, 1)
                    product(("kvn",), lambda b: [(b[:, :], [(ones[:, :], latsq[:, 3 + m, :]) for m in range(2)])])
                    product(("qn",), lambda b: [(b[:, :], [(ones[:, :], latsq[:, m, :]) for m in range(3)])])
                pe.wait_ge(d_within, 16 * CH * (q + 1))
                pe.wait_ge(w_done, q + 1)
                pe.wait_ge(s_done, 4 * (q + 1))
                wre, wim = (Wst[q][r].rearrange("p g j c -> p g (j c)") for r in range(2))
                product(("Y", q), lambda b: [
                    (b[:, M * g:M * g + M], [(DTm[:, g, :], U[:, GB * q + g, :]), (wre[:, g, :], Sst[0][:, g, :]),
                                             (wim[:, g, :], Sst[1][:, g, :])]) for g in range(GB)])
            pe.wait_ge(yg_done, NB)
            for q in range(G // 4):
                turn(("yt", q), lambda b: [(b[0:M, columns(g)], U[:, 4 * q + g, :]) for g in range(4)])
            for q in range(G // 4):
                await_drained(pe, ("yt", q))
            for f in range(4):
                turn(("yT", f), lambda b: [(b[:, M * j:M * j + M], ytok[:, j, columns(f)]) for j in range(CH)])
            pe.wait_ge(lat_done, 2)
            await_slab(pe, ("ukv",))
            ukv = slab(("ukv",), 2, 1024)
            for kt in range(NT):
                product(("V", kt), lambda b: [
                    (b[:, :], [(ckvT[:, k, columns(kt)], ukv[:, k, 512:1024]) for k in range(2)])])
            pe.wait_ge(lat_done, 5)
            pe.wait_ge(d_wuq, 16 * 9)

            def head_in(h):
                product(("Q", h), lambda b: [(b[:, :], [(wuq[:, k, h, :], cqT[:, k, :]) for k in range(3)])])
                if h % 2 == 0:
                    product(("K", h), lambda b: [
                        (b[:, :], [(ukv[:, k, NOPE * h:NOPE * h + P], ckvT[:, k, :]) for k in range(2)])])

            head_in(0)
            for kt in range(NT):
                await_drained(pe, ("V", kt))
            pe.wait_ge(kr_done, 4)
            for i in range(NH * NT + 3):
                h, qt = divmod(i, NT)
                if i < NH * NT:
                    if qt == 0:
                        pe.wait_ge(qk_done, h + 1)
                        await_drained(pe, ("K", h - h % 2))
                    product(("S", i), lambda b: [(b[:, :], [(QT[h % 2][0:QD, columns(qt)], KT[h % 4][0:QD, :])])])
                if 2 <= i < NH * NT + 2:
                    pe.wait_ge(p_done, i - 1)
                    turn(("PT", i - 2), lambda b: [(b[:, columns(k)], Pm[i % 2][:, columns(k)]) for k in range(NT)])
                if qt == 2 and h + 1 < NH:
                    head_in(h + 1)
                if i >= 3 and (i - 3) % NT == NT - 1:
                    g = (i - 3) // NT
                    for n in range(NT):
                        await_drained(pe, ("PT", NT * g + n))
                    product(("O", g), lambda b: [
                        (b[0:HV, :], [(V[:, k, HV * g:HV * g + HV], PT[g % 2][:, k, :]) for k in range(NT)])])
            for f in range(4):
                await_drained(pe, ("yT", f))
            for i in range(KD):
                if i == 0:
                    pe.wait_ge(f_lo, 4)
                for kind in ("gs", "gm"):
                    pe.wait_ge(w_lo, unit_no[(kind, i)] + 1)
                    w = unit((kind, i))[1]
                    product((kind, i), lambda b: [(b[:, :], three(lambda a, k: w[a][:, k, :],
                                                                  lambda a, k: FTs[a][:, k, :])(KD))])
                pe.wait_ge(w_lo, unit_no[("glu", i)] + 1)
                w = unit(("glu", i))[1]
                for n, key in enumerate((("val", i), ("gate", i))):
                    product(key, lambda b: [(b[:, :], three(lambda a, k: w[a][:, k, columns(n)],
                                                            lambda a, k: yTs[a][:, k, :])(4))])
                if i == 0:
                    for h in range(NH):
                        await_drained(pe, ("O", h))
                pe.wait_ge(w_lo, unit_no[("mla", i)] + 1)
                w = unit(("mla", i))[1]
                product(("mla", i), lambda b: [(b[:, :], three(lambda a, k: w[a][:, k, :],
                                                               lambda a, k: OTs[a][:, k, :])(4))])

            def token_major(kind, src, ready):
                for n in range(4):
                    pe.wait_ge(w_lo, unit_no[(kind, n)] + 1)
                    w = unit((kind, n))[1]
                    for p in range(2):
                        first = (n, p) == (0, 0)
                        product((kind, n, p), lambda b: [
                            (b[:, 256 * t:256 * t + 256],
                             three(lambda a, k: src[a][:, k, columns(2 * p + t)], lambda a, k: w[a][:, k, :])(KD, first))
                            for t in range(2)], ready if first else None)

            token_major("out", mixTs, lambda k: pe.wait_ge(mix_done, k + 1))
            pe.wait_ge(xn_done, before[2])
            for k in range(KD):
                turn(("mT", k), lambda b: [(b[:, columns(t)], memx[:, t, columns(k)]) for t in range(2)])
            for n in range(4):
                pe.wait_ge(w_lo, unit_no[("mk", n)] + 1)
                w = unit(("mk", n))[1]
                product(("Km", n), lambda b: [
                    (b[:, 256 * m:256 * m + 256], three(lambda a, k: w[a][:, k, columns(m)],
                                                        lambda a, k: memTs[a][:, k, :])(KD, n == 0))
                    for m in range(2)], None if n else lambda k: await_drained(pe, ("mT", k)))
            for n in range(4):
                pe.wait_ge(w_lo, unit_no[("mv", n)] + 1)
                w = unit(("mv", n))[1]
                product(("Vm", n), lambda b: [
                    (b[:, 256 * t:256 * t + 256], three(lambda a, k: memTs[a][:, k, columns(t)],
                                                        lambda a, k: w[a][:, k, :])(KD))
                    for t in range(2)])
            pe.wait_ge(d_key, 16)
            for q in range(4):
                turn(("keyT", q), lambda b: [(b[:, columns(i)], keyraw[:, 4 * q + i, :]) for i in range(4)])
            pe.wait_ge(xn_done, before[3])
            for k in range(KD):
                turn(("hT", k), lambda b: [(b[:, columns(t)], xn[:, t, columns(k)]) for t in range(NT)])
            for m in range(KD):
                pe.wait_ge(w_lo, unit_no[("mq", m)] + 1)
                w = unit(("mq", m))[1]
                product(("Qm", m), lambda b: [(b[:, :], three(lambda a, k: w[a][:, k, :],
                                                              lambda a, k: hTs[a][:, k, :])(KD, m == 0))],
                        None if m else lambda k: await_drained(pe, ("hT", k)))
            for m in range(KD):
                await_drained(pe, ("Qm", m))
            for n in range(4):
                await_drained(pe, ("Km", n))
                await_drained(pe, ("Vm", n))
            for i in range(MH * NT + 3):
                h, qt = divmod(i, NT)
                if i < MH * NT:
                    product(("Sm", i), lambda b: [
                        (b[:, 0:MT], [(QmT[:, 2 * h + d, columns(qt)], KmT[:, 2 * h + d, :]) for d in range(2)])])
                if 2 <= i < MH * NT + 2:
                    pe.wait_ge(mp_done, i - 1)
                    turn(("PTm", i - 2), lambda b: [(b[:, columns(k)], Pmm[i % 2][:, columns(k)]) for k in range(2)])
                if i >= 3 and (i - 3) % NT == NT - 1:
                    g = (i - 3) // NT
                    for n in range(NT):
                        await_drained(pe, ("PTm", NT * g + n))
                    for d in range(2):
                        product(("Om", g, d), lambda b: [
                            (b[:, :], [(Vm[:, k, columns(2 * g + d)], PTm[g % 2][:, k, :]) for k in range(2)])])
            token_major("mo", OmTs, lambda k: await_drained(pe, ("Om", k // 2, k % 2)))
            pe.wait_ge(xn_done, before[3] + 1)
            for half in range(2):
                turn(("p0", half), lambda b: [(b[:, columns(n)], xn[:, 0, columns(4 * half + n)]) for n in range(4)])
            await_slab(pe, ("pq", 0))
            for s in range(2):
                product(("q0", s), lambda b: [
                    (b[:, 0:P], [(qw[:, k, columns(s)], FT[:, k, 0:P]) for k in range(KD)])],
                        None if s else lambda k: await_drained(pe, ("p0", k // 4)))
            for q in range(4):
                await_drained(pe, ("keyT", q))
            for s in range(2):
                await_drained(pe, ("q0", s))
            product(("s0",), lambda b: [(b[:, columns(s)], [(qhs[s][:, 0:P], keysT[:, s, :])]) for s in range(2)])
            pe.wait_ge(xn_done, before[4])
            for k in range(KD):
                turn(("pT", k), lambda b: [(b[:, columns(t)], xn[:, t, columns(k)]) for t in range(1, NT)])
            for k in range(KD):
                await_drained(pe, ("pT", k))

            def queries(h, s, first=False):
                if s == 0 and not first:
                    pe.wait_ge(qw_in, h * 16)
                cols = slice(P if first else 0, T)
                for k in range(KD):
                    ins = pe.matmul(ps[4 + s][:, cols], qw[:, k, columns(s)], FT[:, k, cols],
                                    start=(k == 0), stop=(k == KD - 1))
                ins.then_inc(q_filled, 1)

            def scores(h, s, first=False):
                pe.wait_ge(q_copied, h * 2 + (s + 1))
                if not first:
                    pe.wait_ge(s_copied, h)
                for t in range(1 if first else 0, NT):
                    keys = keysT[:, s, :] if first else keysT[:, bass.ds(h * 2 + s, 1), :].rearrange("p a n -> p (a n)")
                    ins = pe.matmul(ps[6 + s][:, columns(t)], qhs[s][:, columns(t)], keys, start=True, stop=True)
                ins.then_inc(s_filled, 1)

            def group(g, t, taken=True):
                if taken:
                    pe.wait_ge(acc_taken, g - 1)
                for s in range(TOPK):
                    pe.wait_ge(ld_v[s], (g + 1) * 16)
                    pe.wait_ge(diag_done, g * TOPK + (s + 1))
                    for n in range(2):
                        last = pe.matmul(ps[2 * (t % 2) + n][:, :], diag[s % DRING], Vb[s][:, 512 * n:512 * n + 512],
                                         start=(s == 0), stop=(s == TOPK - 1))
                    last.then_inc(v_summed, 1)

            def head(h, first=False, last=False):
                for t in range(NT):
                    if t < 2 and not last:
                        queries(h + 1, t)
                        scores(h + 1, t)
                    group(h * NT + t, t, taken=not first or t >= 2)

            for b in range(8):
                pe.wait_ge(drained[b], uses[b])
            queries(0, 0, first=True)
            queries(0, 1, first=True)
            scores(0, 0, first=True)
            scores(0, 1, first=True)
            head(0, first=True)
            with pe.Fori(1, PH - 1) as h:
                head(h)
            head(PH - 1, last=True)

        @block.gpsimd
        def _(pool):
            own = [0]

            def step(ins):
                own[0] += 1
                ins.then_inc(c_pool, 1)
                pool.wait_ge(c_pool, own[0])

            def tt(out, a, b, op):
                step(pool.tensor_tensor(out, a, b, op))

            pool.memset(ones[:, :], 1.0).then_inc(ones_set, 1)
            for r, w in enumerate((ssm_c_re, ssm_c_im)):
                for d in range(2):
                    pool.dma_start(Craw[r][:, :, 64 * d:64 * d + 64],
                                 w[0, d].rearrange("(b g) c p -> (g c) b p", b=NB)).then_inc(d_ssm, 16)
            for r, w in enumerate((ssm_b_re, ssm_b_im)):
                for d in range(2):
                    pool.dma_start(bb[r][64 * d:64 * d + 64, :, :],
                                 w[0, d].rearrange("g p c -> p g c")).then_inc(d_ssm, 16)
            step(pool.memset(mask, 1.0))
            step(pool.memset(mask[0:64, 0:1], 0.0))
            step(pool.memset(mask[64:128, M - 1:M], 0.0))
            for r in range(2):
                step(pool.memset(EXT[r], 0.0))
                step(pool.memset(Sst[r], 0.0))
            pool.sem_inc(zeros_set, 1)
            pool.wait_ge(trig_done, 3)
            one, two = (sm[:, 14, :], sm[:, 15, :]), (sm[:, 66, :], sm[:, 72, :])
            step(pool.tensor_copy(one[0], sm[:, 7, :]))
            step(pool.tensor_copy(one[1], sm[:, 8, :]))
            step(pool.tensor_scalar(one[1][64:128, :], sm[64:128, 8, :], -1.0, None, ALU.mult))

            def square(dst, src):
                t0, t1 = sm[:, 13, :], sm[:, 95, :]
                tt(t0, src[0], src[0], ALU.mult)
                tt(t1, src[1], src[1], ALU.mult)
                tt(dst[0], t0, t1, ALU.subtract)
                tt(t0, src[0], src[1], ALU.mult)
                tt(dst[1], t0, t0, ALU.add)

            square(two, one)
            square(one, two)
            square(two, one)
            levels = [(sm[:, 66 + n, :], sm[:, 72 + n, :]) for n in range(6)]
            for n in range(5):
                square(levels[n + 1], levels[n])
            await_full(pool, ("xT", KD - 1))
            step(pool.memset(Tre[:, :, 0:1], 1.0))
            step(pool.memset(Tim[:, :, 0:1], 0.0))

            def table_level(n):
                w = 1 << n
                tmp = [WS[:, 1024 * i:1024 * i + G * w].rearrange("p (g m) -> p g m", g=G) for i in range(2)]
                lr, li = (levels[n][r].unsqueeze(2).to_broadcast([P, G, w]) for r in range(2))
                tr, tim = Tre[:, :, 0:w], Tim[:, :, 0:w]
                tt(tmp[0], tr, lr, ALU.mult)
                tt(tmp[1], tim, li, ALU.mult)
                tt(Tre[:, :, w:2 * w], tmp[0], tmp[1], ALU.subtract)
                tt(tmp[0], tr, li, ALU.mult)
                tt(tmp[1], tim, lr, ALU.mult)
                tt(Tim[:, :, w:2 * w], tmp[0], tmp[1], ALU.add)

            def output_matrices(q):
                for half in range(2):
                    lo = GB * q + NB * half
                    gs, ws = slice(lo, lo + NB), slice(NB * half, NB * half + NB)
                    pr, pi = (sm[:, 50 + 8 * r:58 + 8 * r, gs].rearrange("p k g -> p g k").unsqueeze(3)
                              .to_broadcast([P, NB, CH, CG]) for r in range(2))
                    cr, ci = (c[:, gs, :].unsqueeze(2).to_broadcast([P, NB, CH, CG]) for c in (Cc[0], negC))
                    wre, wim = (w[:, ws] for w in Wst[q])
                    tt(wre, pr, cr, ALU.mult)
                    tt(Wtmp, pi, ci, ALU.mult)
                    tt(wre, wre, Wtmp, ALU.add)
                    tt(wim, pr, ci, ALU.mult)
                    tt(Wtmp, pi, cr, ALU.mult)
                    tt(wim, wim, Wtmp, ALU.subtract)
                pool.sem_inc(w_done, 1)

            for n in range(5):
                table_level(n)
            pool.wait_ge(pow_done, 1)
            output_matrices(0)
            table_level(5)
            pool.sem_inc(table_done, 1)
            for q in range(1, NB):
                output_matrices(q)

            for no in (unit_no[("mo", 0)], unit_no[("mo", 1)]):
                src, (hi, lo) = unit(units[no][0])
                await_slab(pool, unit_slab(units[no][0]))
                await_place(pool, no)
                await_full(pool, ("Qm", KD - 1))
                pool.wait_ge(w_lo, no)
                pool.wait_ge(w_hi, no + 1)
                pool.tensor_tensor(lo, src, hi, ALU.subtract).then_inc(w_lo, 1)

            def gather(dst, table, ix, s, signal):
                pool.sem_inc(apart_pool, 1)
                pool.indirect_dma_start(out=dst, out_offset=None, in_=table,
                                        in_offset=bass.IndirectOffsetOnAxis(ap=ix[:, s:s + 1], axis=0)).then_inc(signal, 16)

            def u_row(g, t, s, first=False):
                if not first or s >= URING:
                    pool.wait_ge(dots, g * TOPK + (s - (URING - 1)))
                gather(Ub[s % URING], peer_u, idx[t], s, ld_u[s % URING])

            def v_row(g, t, s, first=False):
                if not first:
                    pool.wait_ge(v_summed, g * TOPK + (s - (VRING - 1)))
                gather(Vb[s], peer_v, idx[t], s, ld_v[s])

            def head(h, first=False, last=False):
                for t in range(NT):
                    g = h * NT + t
                    more = not last or t < NT - 1
                    if more:
                        pool.wait_ge(idx_ready, g + 2)
                    for s in range(TOPK):
                        if more:
                            u_row(g + 1, (t + 1) % NT, s)
                        if not first or t:
                            v_row(g, t, s)

            await_drained(pool, ("pT", KD - 1))
            await_full(pool, ("mo", 3, 1))
            pool.wait_ge(idx_ready, 1)
            for s in range(URING):
                u_row(0, 0, s, first=True)
            for s in range(VRING):
                v_row(0, 0, s, first=True)
            for s in range(URING, TOPK):
                u_row(0, 0, s, first=True)
            head(0, first=True)
            with pool.Fori(1, PH - 1) as h:
                head(h)
            head(PH - 1, last=True)


NAMES = ["x", "mem", "positions", "g_mix", "w_in", "b_gate", "ssm_lam_re", "ssm_lam_im", "ssm_log_dt",
         "ssm_b_re", "ssm_b_im", "ssm_c_re", "ssm_c_im", "ssm_d", "w_ssm_glu", "g_q_lora", "w_uq",
         "g_kv_lora", "w_ukv", "w_mla_o", "w_out", "g_mem_q", "g_mem_kv", "w_mem_q", "w_mem_kv",
         "w_mem_o", "g_peer", "w_peer_q", "peer_sub_keys", "peer_u", "peer_v", "g_final"]
WEIGHTS = {"w_in", "w_ssm_glu", "w_uq", "w_ukv", "w_mla_o", "w_out", "w_mem_q", "w_mem_kv", "w_mem_o",
           "w_peer_q", "peer_u", "peer_v"}


def kernel(**inputs):
    import concourse.bacc as bacc
    from concourse.bass_utils import run_bass_kernel_spmd

    nc = bacc.Bacc("TRN2", target_bir_lowering=False, num_devices=1)
    arrays = {n: np.ascontiguousarray(inputs[n]) for n in NAMES}
    for n in WEIGHTS:
        arrays[n] = arrays[n].reshape(arrays[n].shape[1:])
    arrays["consts"] = host_constants()
    args = [nc.dram_tensor(f"in_{n}", a.shape, mybir.dt.from_np(a.dtype), kind="ExternalInput").ap()
            for n, a in arrays.items()]
    out = nc.dram_tensor("out_0", (1, T, D), F32, kind="ExternalOutput").ap()
    encoder_layer(nc, *args, out)
    r = run_bass_kernel_spmd(nc, [{f"in_{n}": a for n, a in arrays.items()}], core_ids=[0])
    return r.results[0]["out_0"]
```
